# Optimizing a Trainium2 kernel written in Bass

```python
import jax, jax.numpy as jnp
from jax import lax
import numpy as np

D_MODEL = 1024
BATCH = 1
SEQ = 256
DEPTH = 1
DEC_BATCH = 8
DEC_SEQ = 4
PAST_LEN = 2048
PAGE_SIZE = 128

N_META = 16
EPS = 1e-6
NEG_INF = -1e30
A_HEADS = 8
A_KV_HEADS = 2
A_HEAD_DIM = 64
A_GROUP = A_HEADS // A_KV_HEADS
WINDOW = 128
ATTN_BLOCK = 128
ROPE_THETA = 500000.0
ROPE_DIM = A_HEAD_DIM // 4
META_PAD = ATTN_BLOCK - N_META
B_HEADS = 4
B_KEY_DIM = 64
B_VAL_DIM = 128
GATE_RANK = 16
GATE_NORMALIZER = 16.0
GLA_CHUNK = 64
PEER_HEADS = 8
PEER_KEYS = 128
PEER_EXPERTS = PEER_KEYS * PEER_KEYS
PEER_QDIM = 128
PEER_HALF = PEER_QDIM // 2
PEER_TOPK = 16
PEER_BLOCK = 256
A_Q_WIDTH = A_HEADS * A_HEAD_DIM
A_KV_WIDTH = A_KV_HEADS * A_HEAD_DIM
B_QK_WIDTH = B_HEADS * B_KEY_DIM
B_V_WIDTH = B_HEADS * B_VAL_DIM
PROJ_SIZES = (A_Q_WIDTH, A_KV_WIDTH, A_KV_WIDTH, B_QK_WIDTH, B_QK_WIDTH, B_V_WIDTH, B_V_WIDTH, GATE_RANK, D_MODEL, D_MODEL)
PROJ_COLS = sum(PROJ_SIZES)

kernel_name = 'hybrid_swa_gla_peer_step'

def rms_norm(x, g):
    xf = x.astype(jnp.float32)
    y = xf * lax.rsqrt(jnp.mean(xf * xf, axis=-1, keepdims=True) + EPS)
    return (y * g.astype(jnp.float32)).astype(x.dtype)

def rope(x, pos):
    half = ROPE_DIM // 2
    inv = ROPE_THETA ** (-jnp.arange(0, ROPE_DIM, 2, dtype=jnp.float32) / ROPE_DIM)
    ang = pos.astype(jnp.float32)[:, None] * inv[None, :]
    cos = jnp.cos(ang)[:, None, :]
    sin = jnp.sin(ang)[:, None, :]
    xf = x.astype(jnp.float32)
    x1 = xf[..., :half]
    x2 = xf[..., half:ROPE_DIM]
    out = jnp.concatenate([x1 * cos - x2 * sin, x2 * cos + x1 * sin, xf[..., ROPE_DIM:]], axis=-1)
    return out.astype(x.dtype)

def split_columns(z):
    offsets = [int(o) for o in np.cumsum(PROJ_SIZES)[:-1]]
    return jnp.split(z, offsets, axis=-1)

def mixer_inputs(h, pos, w_in, w_gate_up, b_gate):
    lead = h.shape[:-1]
    qa, ka, va, qb, kb, vb, gb, lr, gate_a, gate_b = split_columns(h @ w_in)
    qa = rope(qa.reshape(lead + (A_HEADS, A_HEAD_DIM)), pos)
    ka = rope(ka.reshape(lead + (A_KV_HEADS, A_HEAD_DIM)), pos)
    va = va.reshape(lead + (A_KV_HEADS, A_HEAD_DIM))
    qb = qb.reshape(lead + (B_HEADS, B_KEY_DIM)) * (B_KEY_DIM ** -0.5)
    kb = kb.reshape(lead + (B_HEADS, B_KEY_DIM))
    vb = vb.reshape(lead + (B_HEADS, B_VAL_DIM))
    log_decay = jax.nn.log_sigmoid((lr @ w_gate_up + b_gate).astype(jnp.float32)) / GATE_NORMALIZER
    log_decay = log_decay.reshape(lead + (B_HEADS, B_KEY_DIM))
    return qa, ka, va, qb, kb, vb, gb, log_decay, gate_a, gate_b

def sink_softmax(s, mask, sink):
    sink = sink.astype(jnp.float32)
    s = jnp.where(mask, s, NEG_INF)
    m = jnp.maximum(jnp.max(s, axis=-1, keepdims=True), sink)
    e = jnp.exp(s - m)
    return e / (jnp.sum(e, axis=-1, keepdims=True) + jnp.exp(sink - m))

def swa_prompt(q, k, v, sinks):
    bsz, lp = q.shape[:2]
    nb = lp // ATTN_BLOCK
    qb = q.reshape(bsz, nb, ATTN_BLOCK, A_KV_HEADS, A_GROUP, A_HEAD_DIM)
    kb = k.reshape(bsz, nb, ATTN_BLOCK, A_KV_HEADS, A_HEAD_DIM)
    vb = v.reshape(bsz, nb, ATTN_BLOCK, A_KV_HEADS, A_HEAD_DIM)
    pad = ((0, 0), (1, 0), (0, 0), (0, 0), (0, 0))
    kk = jnp.concatenate([jnp.pad(kb, pad)[:, :-1], kb], axis=2)
    vv = jnp.concatenate([jnp.pad(vb, pad)[:, :-1], vb], axis=2)
    s = jnp.einsum('bnqkgd,bnskd->bnkgqs', qb, kk).astype(jnp.float32) * (A_HEAD_DIM ** -0.5)
    qi = jnp.arange(nb)[:, None] * ATTN_BLOCK + jnp.arange(ATTN_BLOCK)[None, :]
    ki = jnp.arange(nb)[:, None] * ATTN_BLOCK - ATTN_BLOCK + jnp.arange(2 * ATTN_BLOCK)[None, :]
    diff = qi[:, :, None] - ki[:, None, :]
    mask = (diff >= 0) & (diff <= WINDOW) & (ki[:, None, :] >= META_PAD)
    p = sink_softmax(s, mask[None, :, None, None], sinks.reshape(A_KV_HEADS, A_GROUP, 1, 1))
    o = jnp.einsum('bnkgqs,bnskd->bnqkgd', p.astype(vv.dtype), vv)
    return o.reshape(bsz, lp, A_Q_WIDTH)

def swa_sample(q, k_new, v_new, cache_k, cache_v, sinks):
    dbsz, t = q.shape[:2]
    w = cache_k.shape[1]
    kk = jnp.concatenate([cache_k.astype(k_new.dtype), k_new], axis=1)
    vv = jnp.concatenate([cache_v.astype(v_new.dtype), v_new], axis=1)
    qg = q.reshape(dbsz, t, A_KV_HEADS, A_GROUP, A_HEAD_DIM)
    s = jnp.einsum('bqkgd,bskd->bkgqs', qg, kk).astype(jnp.float32) * (A_HEAD_DIM ** -0.5)
    qpos = PAST_LEN + jnp.arange(t)
    kpos = PAST_LEN - w + jnp.arange(w + t)
    diff = qpos[:, None] - kpos[None, :]
    mask = (diff >= 0) & (diff <= WINDOW)
    p = sink_softmax(s, mask, sinks.reshape(A_KV_HEADS, A_GROUP, 1, 1))
    o = jnp.einsum('bkgqs,bskd->bqkgd', p.astype(vv.dtype), vv)
    return o.reshape(dbsz, t, A_Q_WIDTH), kk[:, -w:], vv[:, -w:]

def gla_chunked(q, k, v, g, s0):
    q, k, v, g = (a.astype(jnp.float32) for a in (q, k, v, g))
    b = jnp.cumsum(g, axis=2)
    b_last = b[:, :, -1:]
    q_t = q * jnp.exp(b)
    k_t = k * jnp.exp(-b)
    k_end = k * jnp.exp(b_last - b)
    c = q.shape[2]
    causal = jnp.tril(jnp.ones((c, c), dtype=bool))
    a = jnp.where(causal, jnp.einsum('bnihd,bnjhd->bnhij', q_t, k_t), 0.0)
    o_intra = jnp.einsum('bnhij,bnjhe->bnihe', a, v)
    decay = jnp.exp(b_last[:, :, 0])

    def step(state, inp):
        qn, kn, vn, dn = inp
        o = jnp.einsum('bihd,bhde->bihe', qn, state)
        state = state * dn[..., None] + jnp.einsum('bjhd,bjhe->bhde', kn, vn)
        return state, o

    xs = tuple(jnp.moveaxis(t, 1, 0) for t in (q_t, k_end, v, decay))
    s_fin, o_inter = lax.scan(step, s0.astype(jnp.float32), xs)
    return o_intra + jnp.moveaxis(o_inter, 0, 1), s_fin

def gla_output(o, g_out, g_norm, dtype):
    lead = o.shape[:-2]
    gate = jax.nn.silu(g_out.reshape(lead + (B_HEADS, B_VAL_DIM)).astype(jnp.float32))
    y = rms_norm(o, g_norm) * gate
    return y.reshape(lead + (B_V_WIDTH,)).astype(dtype)

def merge_branches(gate_a, gate_b, ya, yb, w_branch_a, w_branch_b, w_out):
    m = jax.nn.sigmoid(gate_a) * (ya @ w_branch_a) + jax.nn.sigmoid(gate_b) * (yb @ w_branch_b)
    return m @ w_out

def peer(h, w_q, sub_keys, u, v):
    t = h.shape[0]
    nblk = -(-t // PEER_BLOCK)
    hp = jnp.pad(h, ((0, nblk * PEER_BLOCK - t), (0, 0))).reshape(nblk, PEER_BLOCK, D_MODEL)
    kk = PEER_TOPK * PEER_TOPK

    def one_block(hb):
        q = (hb @ w_q).reshape(PEER_BLOCK, PEER_HEADS, 2, PEER_HALF)
        s = jnp.einsum('thcd,hcnd->thcn', q, sub_keys).astype(jnp.float32)
        sv, si = lax.top_k(s, PEER_TOPK)
        cand = (sv[:, :, 0, :, None] + sv[:, :, 1, None, :]).reshape(PEER_BLOCK, PEER_HEADS, kk)
        cidx = (si[:, :, 0, :, None] * PEER_KEYS + si[:, :, 1, None, :]).reshape(PEER_BLOCK, PEER_HEADS, kk)
        fv, fpos = lax.top_k(cand, PEER_TOPK)
        eidx = jnp.take_along_axis(cidx, fpos, axis=-1)
        wts = jax.nn.softmax(fv, axis=-1)
        act = jax.nn.gelu(jnp.einsum('thkd,td->thk', u[eidx], hb).astype(jnp.float32), approximate=False)
        return jnp.einsum('thk,thkd->td', (wts * act).astype(hb.dtype), v[eidx])

    return lax.map(one_block, hp).reshape(-1, D_MODEL)[:t]

def to_chunks(t, bsz, n_chunks):
    return t.reshape((bsz, n_chunks, GLA_CHUNK) + t.shape[2:])

def setup_inputs(seed: int = 0) -> dict:
    key = jax.random.key(seed)
    ks = jax.random.split(key, 21)

    def nrm(k, shape, scale):
        return jax.random.normal(k, shape, jnp.float32) * scale

    return {
        'x_prompt': nrm(ks[0], (BATCH, SEQ, D_MODEL), 1.0),
        'x_sample': nrm(ks[1], (DEC_BATCH, DEC_SEQ, D_MODEL), 1.0),
        'cache_k_window': nrm(ks[2], (DEPTH, DEC_BATCH, WINDOW, A_KV_HEADS, A_HEAD_DIM), 1.0),
        'cache_v_window': nrm(ks[3], (DEPTH, DEC_BATCH, WINDOW, A_KV_HEADS, A_HEAD_DIM), 1.0),
        'state_gla': nrm(ks[4], (DEPTH, DEC_BATCH, B_HEADS, B_KEY_DIM, B_VAL_DIM), 0.5),
        'meta_tokens': nrm(ks[5], (N_META, D_MODEL), 1.0),
        'g_norm_mix': 1.0 + nrm(ks[6], (DEPTH, D_MODEL), 0.05),
        'w_in': nrm(ks[7], (DEPTH, D_MODEL, PROJ_COLS), D_MODEL ** -0.5),
        'w_gate_up': nrm(ks[8], (DEPTH, GATE_RANK, B_QK_WIDTH), GATE_RANK ** -0.5),
        'b_gate': nrm(ks[9], (DEPTH, B_QK_WIDTH), 0.1),
        'attn_sinks': nrm(ks[10], (DEPTH, A_HEADS), 0.5),
        'g_gla_norm': 1.0 + nrm(ks[11], (DEPTH, B_VAL_DIM), 0.05),
        'w_branch_a': nrm(ks[12], (DEPTH, A_Q_WIDTH, D_MODEL), A_Q_WIDTH ** -0.5),
        'w_branch_b': nrm(ks[13], (DEPTH, B_V_WIDTH, D_MODEL), B_V_WIDTH ** -0.5),
        'w_out': nrm(ks[14], (DEPTH, D_MODEL, D_MODEL), D_MODEL ** -0.5),
        'g_norm_ffn': 1.0 + nrm(ks[15], (DEPTH, D_MODEL), 0.05),
        'w_peer_q': nrm(ks[16], (DEPTH, D_MODEL, PEER_HEADS * PEER_QDIM), D_MODEL ** -0.5),
        'peer_sub_keys': nrm(ks[17], (DEPTH, PEER_HEADS, 2, PEER_KEYS, PEER_HALF), PEER_HALF ** -0.5),
        'peer_u': nrm(ks[18], (DEPTH, PEER_EXPERTS, D_MODEL), D_MODEL ** -0.5),
        'peer_v': nrm(ks[19], (DEPTH, PEER_EXPERTS, D_MODEL), PEER_HEADS ** -0.5),
        'g_norm_final': 1.0 + nrm(ks[20], (D_MODEL,), 0.05),
    }

def reference(x_prompt, x_sample, cache_k_window, cache_v_window, state_gla, meta_tokens, g_norm_mix, w_in,
              w_gate_up, b_gate, attn_sinks, g_gla_norm, w_branch_a, w_branch_b, w_out, g_norm_ffn, w_peer_q,
              peer_sub_keys, peer_u, peer_v, g_norm_final):
    bsz = x_prompt.shape[0]
    tdec = x_sample.shape[1]
    meta = jnp.broadcast_to(meta_tokens[None].astype(x_prompt.dtype), (bsz, N_META, D_MODEL))
    xp = jnp.concatenate([meta, x_prompt], axis=1)
    lp_len = xp.shape[1] + META_PAD
    pos_p = jnp.arange(lp_len) - META_PAD
    pos_s = PAST_LEN + jnp.arange(tdec)
    valid_p = (jnp.arange(lp_len) >= META_PAD)[None, :, None, None]
    n_chunks = lp_len // GLA_CHUNK
    xs = x_sample
    kp_list, vp_list, sp_list, ks_list, vs_list, ss_list = [], [], [], [], [], []
    for l in range(DEPTH):
        h = jnp.pad(rms_norm(xp, g_norm_mix[l]), ((0, 0), (META_PAD, 0), (0, 0)))
        qa, ka, va, qb, kb, vb, gb, ld, ga, gbr = mixer_inputs(h, pos_p, w_in[l], w_gate_up[l], b_gate[l])
        ya = swa_prompt(qa, ka, va, attn_sinks[l])
        ld = jnp.where(valid_p, ld, 0.0)
        s0 = jnp.zeros((bsz, B_HEADS, B_KEY_DIM, B_VAL_DIM), jnp.float32)
        o, s_fin = gla_chunked(to_chunks(qb, bsz, n_chunks), to_chunks(kb, bsz, n_chunks),
                               to_chunks(vb, bsz, n_chunks), to_chunks(ld, bsz, n_chunks), s0)
        yb = gla_output(o.reshape(bsz, lp_len, B_HEADS, B_VAL_DIM), gb, g_gla_norm[l], xp.dtype)
        xp = xp + merge_branches(ga[:, META_PAD:], gbr[:, META_PAD:], ya[:, META_PAD:], yb[:, META_PAD:],
                                 w_branch_a[l], w_branch_b[l], w_out[l])
        xp = xp + peer(rms_norm(xp, g_norm_ffn[l]).reshape(-1, D_MODEL), w_peer_q[l], peer_sub_keys[l],
                       peer_u[l], peer_v[l]).reshape(xp.shape)
        kp_list.append(ka[:, -WINDOW:])
        vp_list.append(va[:, -WINDOW:])
        sp_list.append(s_fin.astype(xp.dtype))
        h = rms_norm(xs, g_norm_mix[l])
        qa, ka, va, qb, kb, vb, gb, ld, ga, gbr = mixer_inputs(h, pos_s, w_in[l], w_gate_up[l], b_gate[l])
        ya, nk, nv = swa_sample(qa, ka, va, cache_k_window[l], cache_v_window[l], attn_sinks[l])
        o, s_fin = gla_chunked(qb[:, None], kb[:, None], vb[:, None], ld[:, None], state_gla[l])
        yb = gla_output(o[:, 0], gb, g_gla_norm[l], xs.dtype)
        xs = xs + merge_branches(ga, gbr, ya, yb, w_branch_a[l], w_branch_b[l], w_out[l])
        xs = xs + peer(rms_norm(xs, g_norm_ffn[l]).reshape(-1, D_MODEL), w_peer_q[l], peer_sub_keys[l],
                       peer_u[l], peer_v[l]).reshape(xs.shape)
        ks_list.append(nk)
        vs_list.append(nv)
        ss_list.append(s_fin.astype(xs.dtype))
    y_prompt = rms_norm(xp, g_norm_final)[:, N_META:]
    y_sample = rms_norm(xs, g_norm_final)
    return (y_prompt, y_sample, jnp.stack(kp_list), jnp.stack(vp_list), jnp.stack(sp_list),
            jnp.stack(ks_list), jnp.stack(vs_list), jnp.stack(ss_list))


_drawn_inputs = setup_inputs


def setup_inputs(seed=0):
    import zlib

    import numpy as np

    out = dict(_drawn_inputs(seed))
    spreads = {}
    factors = {'attn_sinks': 8.0}
    for name, (base, spread) in spreads.items():
        noise = np.random.default_rng([zlib.crc32(name.encode()), seed]).standard_normal(out[name].shape)
        drawn = base * np.exp(spread * noise) if base else spread * noise
        out[name] = __import__('jax').numpy.asarray(drawn.astype(out[name].dtype))
    for name, factor in factors.items():
        out[name] = (out[name] * factor).astype(out[name].dtype)
    return out
```

```python
from contextlib import ExitStack

import numpy as np

import concourse.bass as bass
from concourse import mybir

F32 = mybir.dt.float32
F32R = mybir.dt.float32r
I32 = mybir.dt.int32
U32 = mybir.dt.uint32
ALU = mybir.AluOpType
ACT = mybir.ActivationFunctionType
AX_X = mybir.AxisListType.X

P = 128
D = 1024
KT = D // P
SEQ, META, DEC_B, DEC_T = 256, 16, 8, 4
SAMP = DEC_B * DEC_T
PAST, META_PAD, WINDOW = 2048, 112, 128
AH, AKV, AD = 8, 2, 64
AG = AH // AKV
ROPE = AD // 4
THETA = 500000.0
BH, BK, BV = 4, 64, 128
CHUNK = 64
RANK = 16
PH, PK, TOPK = 8, 128, 16
NEXP = PK * PK
EPS = 1e-6
NEG = -1e30
FLOOR = -3.0e38

A, B, C = 0, 1, 2
COL = (0, 128, 256)
ROWS = (128, 128, SAMP + META)
OUTS = (128, 128, SAMP)
NT = 304
NO = 288
TILES = (A, B, C)

Q0, K0, QB0, KB0, VB0, GB0, LR0, GA0, GR0 = 0, 512, 768, 1024, 1280, 1792, 2304, 2320, 3344

CST = dict(ident=128, cos=3 * ROPE, sin=3 * ROPE // 2, mask_a=176, mask_b=256, mask_s=320, gla=128, gla_s=SAMP,
           reset=NT, hsel=AH, batch=DEC_B * SAMP, batch_rows=DEC_B, iota=TOPK, spot=255)
CST_AT, _n = {}, 0
for _name, _w in CST.items():
    CST_AT[_name] = (_n, _w)
    _n += _w
CST_COLS = _n


def shape_constants():
    c = {k: np.zeros((P, w), np.float32) for k, w in CST.items()}
    c["ident"][:] = np.eye(P)
    inv = np.float32(THETA) ** (-np.arange(0, ROPE, 2, dtype=np.float32) / np.float32(ROPE))
    r = np.arange(P)
    pos = np.stack([META + r, META + 128 + r, np.where(r < SAMP, PAST + r % DEC_T, r - SAMP)], 1)
    ang = pos.astype(np.float32)[:, :, None] * inv.astype(np.float32)
    cos, sin = np.cos(ang).astype(np.float32), np.sin(ang).astype(np.float32)
    c["cos"][:] = np.concatenate([cos, cos], 2).reshape(P, -1)
    c["sin"][:] = sin.reshape(P, -1)
    q = r[:, None]
    key = np.arange(176)[None]
    own = key <= q
    meta = (key >= 160) & (q <= META_PAD + key - 160)
    c["mask_a"][:] = np.where(np.where(key < 128, own, meta), 0.0, NEG)
    key = np.arange(256)[None]
    c["mask_b"][:] = np.where(np.where(key < 128, key >= q, key - 128 <= q), 0.0, NEG)
    step = q % DEC_T
    for grp in range(2):
        key = np.arange(160)[None]
        new = (key - 128) // DEC_T == grp * 4 + q // 32
        new = new & ((key - 128) % DEC_T <= step)
        c["mask_s"][:, grp * 160:grp * 160 + 160] = np.where(np.where(key < 128, key >= step, new), 0.0, NEG)
    i = np.arange(P)[None]
    c["gla"][:] = (q <= i) & (q // CHUNK == i // CHUNK)
    i = np.arange(SAMP)[None]
    c["gla_s"][:] = (q <= i) & (q // DEC_T == i // DEC_T)
    c["reset"][:] = 1.0
    c["reset"][:, [0, 64, 128, 192, *range(256, 288, DEC_T), 288]] = 0.0
    b, i = np.arange(DEC_B)[:, None], np.arange(SAMP)[None]
    c["batch"][:] = (i // DEC_T == b).reshape(1, -1)
    c["batch_rows"][:] = q // DEC_T == np.arange(DEC_B)[None]
    c["iota"][:] = np.arange(TOPK)
    c["hsel"][:] = q // DEC_T % AH == np.arange(AH)[None]
    c["spot"][:, 127] = 1.0
    return np.concatenate([c[k] for k in CST], 1)


def psum_jobs():
    jobs = [("gvecT", "v")]
    jobs += [(f"hT{t}.{half}", "v") for t in TILES for half in range(2)]
    jobs += [(f"q{t}", "a") for t in TILES]
    jobs += [(f"kv{t}", "a") for t in TILES]
    jobs += [("lrT", "v"), ("ld0", "v"), ("ld1", "v")]
    jobs += [(f"vb{t}", "a") for t in TILES]
    jobs += [(f"kT{t}", "v") for t in TILES] + [(f"qT{t}", "a") for t in TILES]
    jobs += [(f"gb{t}", "v") for t in TILES]
    jobs += [("kb0", "v"), ("kb1", "v"), ("qb0", "v"), ("qb1", "v")]
    jobs += [(f"scA.{j}", "v") for j in range(AG)]
    jobs += [("kcT0", "a"), ("kcT1", "a"), ("ss0", "v"), ("ss1", "v")]
    jobs += [(f"pTA.{i}", "a") for i in range(4)] + [("pvA", "v"), ("yaT0", "a")]
    jobs += [(f"scB.{j}", "v") for j in range(AG)]
    jobs += [("spT0", "v"), ("spT1", "v"), ("spv0", "v"), ("spv1", "v"), ("soT0", "v"), ("soT1", "v")]
    jobs += [(f"pTB.{i}", "a") for i in range(4)] + [("pvB", "v"), ("yaT1", "a")]
    jobs += [(f"keT{t}", "a") for t in TILES] + [(f"AT{t}", "v") for t in TILES]
    jobs += [(f"up{n}", "v") for n in range(5)]
    jobs += [(f"o{t}", "v") for t in TILES] + [(f"ybT{t}", "a") for t in TILES]
    jobs += [(f"us{h}.{x}", "v") for h in range(BH) for x in range(2)]
    for m in range(KT):
        jobs += [(f"ga{m}", "a"), (f"za{m}", "v"), (f"gr{m}", "a"), (f"zb{m}", "v")]
    jobs += [(f"wo{n}.{t}", "v") for n in range(2) for t in TILES]
    jobs += [("kk0", "v"), ("kk1", "v")]
    jobs += [(f"h2T{t}.{half}", "v") for t in TILES for half in range(2)]
    jobs += [(f"pq{h}", "a") for h in range(PH)]
    jobs += [(f"ps{t}.{i}", "a") for t in (C, A, B) for i in range(4)]
    jobs += [(f"rT{t}", "v") for t in (C, A, B)]
    return jobs


JOBS = psum_jobs()
AT = {name: i for i, (name, _) in enumerate(JOBS)}
DRAINS = {"v": [n for n, e in JOBS if e == "v"], "a": [n for n, e in JOBS if e == "a"]}
ORDINAL = {n: i + 1 for e in "va" for i, n in enumerate(DRAINS[e])}
DRAINER = dict(JOBS)

RING = 3
UNITS = [("q", "q2"), ("kv", "lrT"), ("vb", "vb2"), ("gb", "gb2"), ("qkb", "qb1")]
for _i in range(4):
    UNITS += [(f"gates{_i}", f"gr{2 * _i + 1}"), (f"branch{_i}", f"zb{2 * _i + 1}")]
UNITS += [("wo0", "wo0.2"), ("wo1", "wo1.2"), ("wq0", "pq3"), ("wq1", "pq7")]
UNIT_AT = {n: i for i, (n, _) in enumerate(UNITS)}

NS = 4
ORDER = (C, A, B)
GROUP0 = {C: 0, A: OUTS[C] // NS, B: (OUTS[C] + OUTS[A]) // NS}


def hybrid_step(nc, x_prompt, x_sample, cache_k, cache_v, state_gla, meta_tokens, g_mix, w_in, w_gate_up, b_gate,
                sinks, g_gla, w_a, w_b, w_out, g_ffn, w_pq, sub_keys, peer_u, peer_v, g_final, cst_in,
                y_prompt, y_sample, nk_prompt, nv_prompt, ns_prompt, nk_sample, nv_sample, ns_sample):
    with ExitStack() as ctx:
        def sb(name, shape, dt=F32):
            return ctx.enter_context(nc.sbuf_tensor(name, shape, dt))

        def overlay(room, *variants):
            found, most = {}, 0
            for variant in variants:
                with ExitStack() as turn:
                    for name, shape, *dt in variant:
                        found[name] = turn.enter_context(nc.sbuf_tensor(name, shape, *(dt or [F32])))
                most = max(most, sum(int(np.prod(v[1][1:])) for v in variant))
            sb(room, [P, most])
            return found

        def sem(name):
            return ctx.enter_context(nc.semaphore(name))

        ps = ctx.enter_context(nc.psum_tensor("ps", [P, 8, 512], F32))

        cst = sb("cst", [P, CST_COLS])
        x = sb("x", [P, 3, D])
        hT = sb("hT", [P, KT, NT])
        gvec = sb("gvec", [18, P])
        gT = sb("gT", [P, 18])
        gffn = sb("gffn", [P, D])
        stat = sb("stat", [P, 4, 4])
        mT = sb("mT", [P, KT, NT])
        yaT = sb("yaT", [P, AG, NT])
        ybT = sb("ybT", [P, BH, NT])
        o1 = overlay("room_ring", [("ring", [P, RING, 4096])],
                     [("ub", [P, NS, D]), ("vbuf", [P, NS, D])]
                     + [(f"onehot{s}", [P, P], F32R) for s in range(NS)] + [(f"wz{s}", [P, P]) for s in range(NS)]
                     + [(f"islot{s}", [P, 1], I32) for s in range(NS)] + [("dots", [P, NS]), ("acts", [P, NS])])
        ring, ub, vbuf, dots, acts = (o1[k] for k in ("ring", "ub", "vbuf", "dots", "acts"))
        onehot, wz, islot = ([o1[f"{k}{s}"] for s in range(NS)] for k in ("onehot", "wz", "islot"))
        mixer = [("qkv", [P, 3, 768]), ("qT", [P, AG, NT]), ("kz", [P, AKV, NT]), ("kTs", [P, SAMP]),
                 ("kcT", [P, DEC_B, P]), ("vc", [P, DEC_B, P]), ("sinkb", [P, AH]), ("sinkr", [P, 1]),
                 ("sinkt", [P, AH]), ("soft", [P, 6, AH]), ("softs", [P, 6, 2]), ("qs", [P, 2, P]),
                 ("qzs", [P, DEC_B, P]), ("pss", [P, 2, 160]), ("pz", [P, 2, 4 * P]), ("pnT", [SAMP, 2, P]),
                 ("ya", [P, 512]), ("vb", [P, 3, 512]), ("gate", [P, 3, 512]), ("gnb", [P, BV]),
                 ("wgu", [RANK, 256]), ("lrT", [RANK, NT]), ("eb", [P, 2, NT]), ("bcum", [P, 2, NT]),
                 ("kt", [P, 2, NT]), ("ket", [P, 2, NT]), ("qh", [P, BH, NT]), ("atm", [P, 2, BH, P]),
                 ("ats", [SAMP, BH, SAMP]), ("ke", [P, 3, 2, P]), ("s0", [P, 2, DEC_B, BV]), ("oss", [P, 3, 4, BH])]
        m = {}
        with ExitStack() as mixers:
            for name, shape in mixer:
                m[name] = mixers.enter_context(nc.sbuf_tensor(name, shape, F32))
            with ExitStack() as turn:
                m["kc"] = turn.enter_context(nc.sbuf_tensor("kc", [P, DEC_B, P], F32))
            m["st"] = mixers.enter_context(nc.sbuf_tensor("st", [P, 5, 2, BV], F32))
            for variant in ([("hrow", [P, 3, D])],
                            [("ropet", [P, 10, 2 * ROPE]), ("so", [P, 2, P]), ("sm", [P, AH, 256]),
                             ("pT", [P, AH, 2, P])],
                            [("qsz", [P, BH, DEC_B, SAMP]), ("vblk", [SAMP, DEC_B, BV]), ("yb", [P, 3, 512]),
                             ("sga", [P, 2, NT])]):
                with ExitStack() as turn:
                    for name, shape in variant:
                        m[name] = turn.enter_context(nc.sbuf_tensor(name, shape, F32))
        (qkv, qT, kz, kTs, kcT, vc, sinkb, sinkr, sinkt, soft, softs, qs, qzs, pss, pz, pnT, ya, vb, gate, gnb, wgu,
         lrT, eb, bcum, kt, ket, qh, atm, ats, ke, s0, oss) = (m[k] for k, _ in mixer)
        kc, st, hrow, ropet, so, sm, pT, qsz, vblk, yb, sga = (m[k] for k in (
            "kc", "st", "hrow", "ropet", "so", "sm", "pT", "qsz", "vblk", "yb", "sga"))
        h2hi = sb("h2hi", [P, 3, D], F32R)
        h2lo = sb("h2lo", [P, 3, D], F32R)
        h2 = sb("h2", [P, 2, D])
        h2c = sb("h2c", [P, D])
        keys = sb("keys", [P, PH, P])
        kbd = sb("kbd", [P, PH, 2 * PK])
        qp = sb("qp", [P, PH, NO])
        sc = sb("sc", [P, 3, PH, 2 * PK])
        gfin = sb("gfin", [P, D])
        less = sb("less", [P, PK])
        sv = sb("sv", [P, PH, 2, TOPK])
        si = sb("si", [P, PH, 2, TOPK], U32)
        sif = sb("sif", [P, PH, 2, TOPK])
        cand = sb("cand", [P, TOPK * TOPK])
        cand2 = sb("cand2", [P, TOPK * TOPK])
        fv = sb("fv", [P, PH, TOPK])
        fpos = sb("fpos", [P, PH, TOPK], U32)
        fij = sb("fij", [P, 2, PH * TOPK], U32)
        fijf = sb("fijf", [P, 2, PH, TOPK])
        pick = sb("pick", [P, PH, TOPK, TOPK])
        eij = sb("eij", [P, 2, PH * TOPK])
        route = sb("route", [P, 2, PH, TOPK])
        wsum = sb("wsum", [P, 2, PH])
        idxT = sb("idxT", [P, NO], I32)
        wT = sb("wT", [P, NO])

        h2hold = [h2[:, 0, :], h2[:, 1, :], h2c[:, :]]

        def C_(name):
            at, w = CST_AT[name]
            return cst[:, at:at + w]

        ident = C_("ident")

        x_in = [sem(f"x_in{t}") for t in TILES]
        cst_landed = sem("cst_landed")
        small_landed = sem("small_landed")
        cache_landed = sem("cache_landed")
        unit_landed = [sem(f"unit_landed{s}") for s in range(RING)]
        router_landed = sem("router_landed")
        mixer_out = sem("mixer_out")
        cache_copied = sem("cache_copied")
        y_out = [sem(f"y_out{i}") for i in range(3)]
        u_landed = [sem(f"u_landed{s}") for s in range(NS)]
        v_landed = [sem(f"v_landed{s}") for s in range(NS)]
        filled = sem("bank_filled")
        drained = {"v": sem("bank_drained_v"), "a": sem("bank_drained_a")}
        v_step = sem("v_step")
        a_step = sem("a_step")
        zeroed = sem("zeroed")
        ssq_done, mean_done, root_done, rows_normed = (sem(k) for k in ("ssq_done", "mean_done", "root_done",
                                                                        "rows_normed"))
        roped = sem("roped")
        ld_abs, ld_log, b_ready, b_exp, last_ready, ket_exp = (sem(k) for k in ("ld_abs", "ld_log", "b_ready",
                                                                                "b_exp", "last_ready", "ket_exp"))
        gate_sig = sem("gate_sig")
        max_ready, probs_ready = sem("max_ready"), sem("probs_ready")
        qs_ready, smax_ready, sprobs_ready = sem("qs_ready"), sem("smax_ready"), sem("sprobs_ready")
        states_ready = sem("states_ready")
        o_squared, o_mean, o_root, yb_ready = sem("o_squared"), sem("o_mean"), sem("o_root"), sem("yb_ready")
        qsz_ready, vblk_ready, sstate_ready = sem("qsz_ready"), sem("vblk_ready"), sem("sstate_ready")
        merged = sem("merged")
        x2_ready = sem("x2_ready")
        h2_split = sem("h2_split")
        kbd_ready = sem("kbd_ready")
        fv_ready, w_exp, routed = sem("fv_ready"), sem("w_exp"), sem("routed")
        idx_copied, onehot_ready = sem("idx_copied"), sem("onehot_ready")
        spread, dotted, gelued, wz_ready, combined = (sem(k) for k in ("spread", "dotted", "gelued", "wz_ready",
                                                                       "combined"))
        acc_read = sem("acc_read")
        pool_turn, v_turn = sem("pool_turn"), sem("v_turn")
        fin_ssq, fin_mean, fin_root, y_ready = (sem(k) for k in ("fin_ssq", "fin_mean", "fin_root", "y_ready"))

        N_SMALL_IN, N_CACHE_IN, N_MIX_OUT = 7, 4, 8

        def take(eng, job):
            eng.wait_ge(filled, AT[job] + 1)
            return ps[:, AT[job] % 8, :]

        def release(ins, job):
            ins.then_inc(drained[DRAINER[job]], 1)

        def need(eng, *names):
            for name in names:
                eng.wait_ge(drained[DRAINER[name]], ORDINAL[name])

        w_in_v = w_in[0].rearrange("(k p) n -> p k n", p=P)

        def slot(unit, k):
            s = UNIT_AT[unit] % RING
            return ring[:, s, :].rearrange("p (k n) -> p k n", k=k)

        def unit_dmas(unit):
            full = slot(unit, KT)
            if unit == "kv":
                return [(full[:, :, 0:256], w_in_v[:, :, K0:K0 + 256]),
                        (full[:, :, 256:256 + RANK], w_in_v[:, :, LR0:LR0 + RANK])]
            if unit in ("q", "vb", "gb", "qkb"):
                at = dict(q=Q0, vb=VB0, gb=GB0, qkb=QB0)[unit]
                return [(full, w_in_v[:, :, at:at + 512])]
            n = int(unit[-1])
            if unit.startswith("gates"):
                return [(full[:, :, 0:256], w_in_v[:, :, GA0 + 256 * n:GA0 + 256 * n + 256]),
                        (full[:, :, 256:512], w_in_v[:, :, GR0 + 256 * n:GR0 + 256 * n + 256])]
            if unit.startswith("branch"):
                wav = w_a[0].rearrange("(g j d) n -> g d j n", g=AKV, j=AG)
                cols = slice(256 * n, 256 * n + 256)
                return [(full[0:AD, 0:4, 0:256], wav[0, :, :, cols]), (full[AD:P, 0:4, 0:256], wav[1, :, :, cols]),
                        (full[:, 4:8, 0:256], w_b[0].rearrange("(h e) n -> e h n", h=BH)[:, :, cols])]
            w = w_out if unit.startswith("wo") else w_pq
            return [(full, w[0].rearrange("(k p) n -> p k n", p=P)[:, :, 512 * n:512 * n + 512])]

        landed_at, total = {}, [0] * RING
        for name, _ in UNITS:
            total[UNIT_AT[name] % RING] += 16 * len(unit_dmas(name))
            landed_at[name] = total[UNIT_AT[name] % RING]

        def unit_ready(eng, unit):
            eng.wait_ge(unit_landed[UNIT_AT[unit] % RING], landed_at[unit])

        def held(eng, value):
            return value if isinstance(value, int) else eng.snap(value)

        block = ctx.enter_context(nc.Block())

        @block.sync
        def _(sp):
            sp.dma_start(x[:, A, :], x_prompt[0, 0:128, :]).then_inc(x_in[A], 16)
            sp.dma_start(x[:, B, :], x_prompt[0, 128:256, :]).then_inc(x_in[B], 16)
            sp.dma_start(x[0:SAMP, C, :], x_sample.rearrange("b t d -> (b t) d")).then_inc(x_in[C], 16)
            sp.dma_start(x[SAMP:SAMP + META, C, :], meta_tokens).then_inc(x_in[C], 16)
            for n, (unit, _) in enumerate(UNITS):
                if n >= RING:
                    sp.wait_ge(filled, AT[UNITS[n - RING][1]] + 1)
                for dst, src in unit_dmas(unit):
                    sp.dma_start(dst, src).then_inc(unit_landed[n % RING], 16)
                if unit == "gates0":
                    sp.wait_ge(roped, 3)
                    need(sp, "kv0", "kv1", "kv2")
                    for c0, prompt, sample in ((512, nk_prompt, nk_sample), (640, nv_prompt, nv_sample)):
                        sp.dma_start(prompt[0, 0].rearrange("s g d -> s (g d)"),
                                     qkv[:, B, c0:c0 + P]).then_inc(mixer_out, 16)
                        sp.dma_start(sample[0, :, WINDOW - DEC_T:WINDOW].rearrange("b t g d -> b t (g d)"),
                                     qkv[0:SAMP, C, c0:c0 + P]).then_inc(mixer_out, 16)
                if unit == "wo1":
                    sp.wait_ge(states_ready, 4 * 5)
                    for p in range(2):
                        sp.dma_start(ns_prompt[0, 0, 2 * p:2 * p + 2].rearrange("h d e -> (h d) e"),
                                     st[:, 4, p, :]).then_inc(mixer_out, 16)
                    need(sp, "us3.1")
                    for p in range(2):
                        sp.dma_start(ns_sample[0, :, 2 * p:2 * p + 2].rearrange("b h d e -> (h d) b e"),
                                     s0[:, p]).then_inc(mixer_out, 16)
            sp.wait_ge(mixer_out, 16 * N_MIX_OUT)
            sp.wait_ge(merged, KT)
            sp.dma_start(keys[:, :, :].rearrange("n h (c d) -> n h c d", c=2),
                         sub_keys[0].rearrange("h c n d -> n h c d")).then_inc(router_landed, 16)
            sp.dma_start(gfin[:, :], g_final.rearrange("(o d) -> o d", o=1).broadcast_to([P, D])
                         ).then_inc(router_landed, 16)
            for i, t in enumerate(ORDER):
                sp.wait_ge(y_ready, i + 1)
                dst = y_sample.rearrange("b t d -> (b t) d") if t == C else y_prompt[0, 128 * t:128 * t + 128, :]
                sp.dma_start(dst, h2[0:OUTS[t], i % 2, :]).then_inc(y_out[i], 16)
            for i in range(3):
                sp.wait_ge(y_out[i], 16)
            sp.wait_ge(cache_copied, 16 * 2)

        @block.gpsimd
        def _(pool):
            pool.dma_start(cst[:, :], cst_in).then_inc(cst_landed, 16)
            for dst, src in ((gvec[0:8, :], g_mix[0].rearrange("(k p) -> k p", p=P)),
                             (gvec[8:16, :], g_ffn[0].rearrange("(k p) -> k p", p=P)),
                             (gvec[16:18, :], b_gate[0].rearrange("(k p) -> k p", p=P)),
                             (wgu[:, :], w_gate_up[0]),
                             (sinkb[:, :], sinks[0:1, :].broadcast_to([P, AH])),
                             (gnb[:, :], g_gla[0:1, :].broadcast_to([P, BV])),
                             (gffn[:, :], g_ffn[0:1, :].broadcast_to([P, D]))):
                pool.dma_start(dst, src).then_inc(small_landed, 16)
            for dst, src in ((kc[:, :, :], cache_k[0].rearrange("b s g d -> s b (g d)")),
                             (vc[:, :, :], cache_v[0].rearrange("b s g d -> s b (g d)")),
                             (s0[:, 0], state_gla[0, :, 0:2].rearrange("b h d e -> (h d) b e")),
                             (s0[:, 1], state_gla[0, :, 2:4].rearrange("b h d e -> (h d) b e"))):
                pool.dma_start(dst, src).then_inc(cache_landed, 16)
            for cache, out in ((cache_k, nk_sample), (cache_v, nv_sample)):
                pool.dma_start(out[0, :, 0:WINDOW - DEC_T].rearrange("b s g d -> b (s g d)"),
                               cache[0, :, DEC_T:WINDOW].rearrange("b s g d -> b (s g d)")
                               ).then_inc(cache_copied, 16)
            for buf in (kz, qh, qs, qzs, pz, atm, ats):
                pool.memset(buf[:], 0.0).then_inc(zeroed, 1)
            pool.wait_ge(mixer_out, 16 * N_MIX_OUT)
            pool.wait_ge(merged, KT)
            pool.memset(kbd[:, :, :], 0.0).then_inc(zeroed, 1)

            def token(first_use, tk, col, row, s):
                now, back = held(pool, tk + 1), held(pool, tk - (NS - 1))
                if not first_use:
                    pool.wait_ge(v_landed[s], 16 * ((tk - s) // NS))
                    pool.wait_ge(spread, back)
                pool.tensor_copy(islot[s][:, :], idxT[:, bass.ds(col, 1)]).then_inc(idx_copied, 1)
                pool.tensor_copy(onehot[s][:, :], ident[:, bass.ds(row, 1)].broadcast_to([P, P])
                                 ).then_inc(onehot_ready, 1)
                pool.wait_ge(idx_copied, now)
                if not first_use:
                    pool.wait_ge(dotted, back)
                pool.sem_inc(pool_turn, 1)
                pool.indirect_dma_start(ub[:, s, :], None, peer_u[0],
                                        bass.IndirectOffsetOnAxis(ap=islot[s][:, 0:1], axis=0)
                                        ).then_inc(u_landed[s], 16)
                if not first_use:
                    pool.wait_ge(combined, back)
                pool.sem_inc(pool_turn, 1)
                pool.indirect_dma_start(vbuf[:, s, :], None, peer_v[0],
                                        bass.IndirectOffsetOnAxis(ap=islot[s][:, 0:1], axis=0)
                                        ).then_inc(v_landed[s], 16)

            for t in ORDER:
                need(pool, f"rT{t}")
                g0 = 0
                if t == ORDER[0]:
                    need(pool, f"rT{ORDER[-1]}")
                    for s in range(NS):
                        token(True, s, COL[t] + s, s, s)
                    g0 = 1
                with pool.Fori(g0, OUTS[t] // NS) as g:
                    for s in range(NS):
                        token(False, (GROUP0[t] + g) * NS + s, g * NS + (COL[t] + s), g * NS + s, s)

        @block.tensor
        def _(pe):
            def open_(job):
                assert AT[job] == pe_at[0], (job, JOBS[pe_at[0]])
                pe_at[0] += 1
                if AT[job] >= 8:
                    need(pe, JOBS[AT[job] - 8][0])
                return ps[:, AT[job] % 8, :]

            pe_at = [0]

            def close(ins):
                ins.then_inc(filled, 1)

            pe.wait_ge(cst_landed, 16)
            pe.wait_ge(small_landed, 16 * N_SMALL_IN)
            bank = open_("gvecT")
            close(pe.transpose(bank[:, 0:18], gvec[:, :], ident[0:18, 0:18]))
            for t in TILES:
                pe.wait_ge(rows_normed, t + 1)
                r = ROWS[t]
                for half in range(2):
                    bank = open_(f"hT{t}.{half}").rearrange("p (k r) -> p k r", k=4)
                    for k in range(4):
                        c0 = (4 * half + k) * P
                        ins = pe.transpose(bank[:, k, 0:r], hrow[0:r, t, c0:c0 + P], ident[0:r, 0:r])
                    close(ins)

            def rows_of(unit, job, t, c0, n):
                bank, r, w = open_(job), ROWS[t], slot(unit, KT)
                for k in range(KT):
                    ins = pe.matmul(bank[0:r, 0:n], hT[:, k, COL[t]:COL[t] + r], w[:, k, c0:c0 + n],
                                    start=(k == 0), stop=(k == KT - 1))
                close(ins)

            def cols_of(unit, job, c0, n, width):
                bank, w = open_(job), slot(unit, KT)
                for k in range(KT):
                    ins = pe.matmul(bank[0:n, 0:width], w[:, k, c0:c0 + n], hT[:, k, 0:width],
                                    start=(k == 0), stop=(k == KT - 1))
                close(ins)

            unit_ready(pe, "q")
            for t in TILES:
                need(pe, f"hT{t}.1")
                rows_of("q", f"q{t}", t, 0, 512)
            unit_ready(pe, "kv")
            for t in TILES:
                rows_of("kv", f"kv{t}", t, 0, 256)
            cols_of("kv", "lrT", 256, RANK, NT)
            for p in range(2):
                bank = open_(f"ld{p}")
                need(pe, "lrT")
                close(pe.matmul(bank[:, 0:NT], wgu[:, p * P:p * P + P], lrT[:, :], start=True, stop=True))
            unit_ready(pe, "vb")
            for t in TILES:
                rows_of("vb", f"vb{t}", t, 0, 512)
            for t in TILES:
                bank, r = open_(f"kT{t}"), ROWS[t]
                pe.wait_ge(roped, t + 1)
                close(pe.transpose(bank[:, 0:r], qkv[0:r, t, 512:640], ident[0:r, 0:r]))
            for t in TILES:
                bank, r = open_(f"qT{t}").rearrange("p (j r) -> p j r", j=AG), ROWS[t]
                for j in range(AG):
                    ins = pe.transpose(bank[:, j, 0:r], qkv[0:r, t, j * P:j * P + P], ident[0:r, 0:r])
                close(ins)
            unit_ready(pe, "gb")
            for t in TILES:
                rows_of("gb", f"gb{t}", t, 0, 512)
            unit_ready(pe, "qkb")
            for p in range(2):
                cols_of("qkb", f"kb{p}", 256 + p * P, P, NT)
            for p in range(2):
                cols_of("qkb", f"qb{p}", p * P, P, NT)

            def scores(t):
                width = 176 if t == A else 256
                need(pe, f"qT{t}", "kT2")
                for j in range(AG):
                    bank = open_(f"sc{'AB'[t]}.{j}").rearrange("p (g k) -> p g k", g=2)
                    for g in range(AKV):
                        lhs = qT[:, j, COL[t]:COL[t] + P]
                        if t == A:
                            pe.matmul(bank[:, g, 0:128], lhs, kz[:, g, 0:128], start=True, stop=True)
                            ins = pe.matmul(bank[:, g, 128:width], lhs, kz[:, g, 256:304], start=True, stop=True)
                        else:
                            ins = pe.matmul(bank[:, g, :], lhs, kz[:, g, 0:256], start=True, stop=True)
                    close(ins)

            def attend(t):
                pe.wait_ge(probs_ready, t + 1)
                for i in range(4):
                    bank = open_(f"pT{'AB'[t]}.{i}").rearrange("p (h c q) -> p h c q", h=2, c=2)
                    for hh in range(2):
                        row = sm[:, 2 * i + hh, :]
                        pe.transpose(bank[:, hh, 0, :], row[:, 0:128], ident)
                        n = 48 if t == A else 128
                        ins = pe.transpose(bank[0:n, hh, 1, :], row[:, 128:128 + n], ident)
                    close(ins)
                bank = open_(f"pv{'AB'[t]}")
                need(pe, f"pT{'AB'[t]}.3", "kv2")
                for h in range(AH):
                    c0 = 640 + (h // AG) * AD
                    first, second = (A, C) if t == A else (A, B)
                    n = ROWS[second]
                    pe.matmul(bank[:, h * AD:h * AD + AD], pT[:, h, 0, :], qkv[:, first, c0:c0 + AD],
                              start=True, stop=False)
                    ins = pe.matmul(bank[:, h * AD:h * AD + AD], pT[0:n, h, 1, :], qkv[0:n, second, c0:c0 + AD],
                                    start=False, stop=True)
                close(ins)
                bank = open_(f"yaT{t}").rearrange("p (j r) -> p j r", j=AG)
                need(pe, f"pv{'AB'[t]}")
                for j in range(AG):
                    ins = pe.transpose(bank[:, j, :], ya[:, j * P:j * P + P], ident)
                close(ins)

            scores(A)
            pe.wait_ge(cache_landed, 16 * N_CACHE_IN)
            for i in range(2):
                bank = open_(f"kcT{i}").rearrange("p (b s) -> p b s", b=4)
                for b in range(4):
                    ins = pe.transpose(bank[:, b, :], kc[:, 4 * i + b, :], ident)
                close(ins)
            need(pe, "kcT1")
            pe.wait_ge(qs_ready, 1)
            for grp in range(2):
                bank = open_(f"ss{grp}")
                for b in range(4):
                    pe.matmul(bank[:, 0:WINDOW], qzs[:, 4 * grp + b, :], kcT[:, 4 * grp + b, :],
                              start=(b == 0), stop=(b == 3))
                close(pe.matmul(bank[:, WINDOW:160], qs[:, grp, :], kTs[:, :], start=True, stop=True))
            attend(A)
            scores(B)
            pe.wait_ge(sprobs_ready, 1)
            for grp in range(2):
                bank = open_(f"spT{grp}")
                pe.transpose(bank[:, 0:P], pss[:, grp, 0:WINDOW], ident)
                close(pe.transpose(bank[0:SAMP, P:2 * P], pss[:, grp, WINDOW:160], ident))
            for grp in range(2):
                bank = open_(f"spv{grp}")
                need(pe, f"spT{grp}")
                for b in range(4):
                    pe.matmul(bank[:, 0:P], pz[:, grp, b * P:b * P + P], vc[:, 4 * grp + b, :],
                              start=(b == 0), stop=False)
                close(pe.matmul(bank[:, 0:P], pnT[:, grp, :], qkv[0:SAMP, C, 640:768], start=False, stop=True))
            for grp in range(2):
                bank = open_(f"soT{grp}")
                need(pe, f"spv{grp}")
                close(pe.transpose(bank[:, 0:P], so[:, grp, :], ident))
            attend(B)

            for t in TILES:
                bank, r = open_(f"keT{t}").rearrange("p (c d) -> p c d", c=4), ROWS[t]
                need(pe, "kb1")
                for p in range(2):
                    ins = pe.transpose(bank[0:r, p, :], ket[:, p, COL[t]:COL[t] + r], ident)
                close(ins)
            for t in TILES:
                r = OUTS[t]
                bank = open_(f"AT{t}")
                need(pe, "qb1")
                for h in range(BH):
                    ins = pe.matmul(bank[0:r, h * r:h * r + r], kt[:, h // 2, COL[t]:COL[t] + r],
                                    qh[:, h, COL[t]:COL[t] + r], start=True, stop=True)
                close(ins)
            chunks = [(C, SAMP, META), (A, 0, CHUNK), (A, CHUNK, CHUNK), (B, 0, CHUNK), (B, CHUNK, CHUNK)]
            need(pe, "keT2", "vb2")
            for n, (t, r0, r) in enumerate(chunks):
                bank = open_(f"up{n}")
                for p in range(2):
                    ins = pe.matmul(bank[:, p * 256:p * 256 + 256], ke[r0:r0 + r, t, p, :],
                                    vb[r0:r0 + r, t, p * 256:p * 256 + 256], start=True, stop=True)
                close(ins)
            for t in (A, B):
                bank = open_(f"o{t}")
                need(pe, f"AT{t}")
                pe.wait_ge(states_ready, 4 * (2 * t + 2))
                for h in range(BH):
                    cols = slice(h * BV, h * BV + BV)
                    pe.matmul(bank[:, cols], atm[:, t, h, :], vb[:, t, cols], start=True, stop=False)
                    for c in range(2):
                        r0 = c * CHUNK
                        ins = pe.matmul(bank[r0:r0 + CHUNK, cols], qh[:, h, COL[t] + r0:COL[t] + r0 + CHUNK],
                                        st[:, 2 * t + c, h // 2, :], start=False, stop=True)
                close(ins)
            bank = open_("o2")
            need(pe, "AT2")
            pe.wait_ge(qsz_ready, 1)
            for h in range(BH):
                cols = slice(h * BV, h * BV + BV)
                pe.matmul(bank[0:SAMP, cols], ats[:, h, :], vb[0:SAMP, C, cols], start=True, stop=False)
                for b in range(DEC_B):
                    ins = pe.matmul(bank[0:SAMP, cols], qsz[:, h, b, :], s0[:, h // 2, b, :],
                                    start=False, stop=(b == DEC_B - 1))
            close(ins)
            for t in TILES:
                bank, r = open_(f"ybT{t}").rearrange("p (j r) -> p j r", j=BH), OUTS[t]
                pe.wait_ge(yb_ready, t + 1)
                for h in range(BH):
                    ins = pe.transpose(bank[:, h, 0:r], yb[0:r, t, h * BV:h * BV + BV], ident[0:r, 0:r])
                close(ins)
            for h in range(BH):
                pe.wait_ge(vblk_ready, h + 1)
                for i in range(2):
                    bank = open_(f"us{h}.{i}")
                    close(pe.matmul(bank, ke[0:SAMP, C, h // 2, :], vblk[:, 4 * i:4 * i + 4, :],
                                    start=True, stop=True))

            need(pe, "yaT1", "soT1", "ybT2")
            for mt in range(KT):
                n, c0 = mt // 2, (mt % 2) * P
                unit_ready(pe, f"gates{n}")
                cols_of(f"gates{n}", f"ga{mt}", c0, P, NO)
                unit_ready(pe, f"branch{n}")
                w = slot(f"branch{n}", KT)
                bank = open_(f"za{mt}")
                for j in range(AG):
                    ins = pe.matmul(bank[:, 0:NO], w[:, j, c0:c0 + P], yaT[:, j, 0:NO], start=(j == 0), stop=(j == 3))
                close(ins)
                cols_of(f"gates{n}", f"gr{mt}", 256 + c0, P, NO)
                bank = open_(f"zb{mt}")
                for j in range(BH):
                    ins = pe.matmul(bank[:, 0:NO], w[:, 4 + j, c0:c0 + P], ybT[:, j, 0:NO],
                                    start=(j == 0), stop=(j == 3))
                close(ins)
            pe.wait_ge(merged, KT)
            for n in range(2):
                unit_ready(pe, f"wo{n}")
                w = slot(f"wo{n}", KT)
                for t in TILES:
                    bank, r = open_(f"wo{n}.{t}"), OUTS[t]
                    for k in range(KT):
                        ins = pe.matmul(bank[0:r, :], mT[:, k, COL[t]:COL[t] + r], w[:, k, :],
                                        start=(k == 0), stop=(k == KT - 1))
                    close(ins)

            pe.wait_ge(router_landed, 16 * 2)
            for i in range(2):
                bank = open_(f"kk{i}").rearrange("p (h n) -> p h n", h=4)
                for h in range(4):
                    ins = pe.transpose(bank[:, h, :], keys[:, 4 * i + h, :], ident)
                close(ins)
            for t in TILES:
                pe.wait_ge(rows_normed, 3 + t + 1)
                r = OUTS[t]
                for half in range(2):
                    bank = open_(f"h2T{t}.{half}").rearrange("p (k r) -> p k r", k=4)
                    for k in range(4):
                        c0 = (4 * half + k) * P
                        ins = pe.transpose(bank[:, k, 0:r], h2hold[t][0:r, c0:c0 + P], ident[0:r, 0:r])
                    close(ins)
            need(pe, "h2T2.1")
            for h in range(PH):
                unit_ready(pe, f"wq{h // 4}")
                cols_of(f"wq{h // 4}", f"pq{h}", (h % 4) * P, P, NO)
            need(pe, "pq7")
            pe.wait_ge(kbd_ready, 1)
            for t in ORDER:
                r = OUTS[t]
                for i in range(4):
                    bank = open_(f"ps{t}.{i}")
                    for hh in range(2):
                        h = 2 * i + hh
                        ins = pe.matmul(bank[0:r, hh * 256:hh * 256 + 256], qp[:, h, COL[t]:COL[t] + r], kbd[:, h, :],
                                        start=True, stop=True)
                    close(ins)
            for i, t in enumerate(ORDER):
                bank, r = open_(f"rT{t}").rearrange("p (a r) -> p a r", a=4), OUTS[t]
                pe.wait_ge(routed, i + 1)
                for a in range(2):
                    ins = pe.transpose(bank[:, a, 0:r], route[0:r, a].rearrange("r h k -> r (h k)"), ident[0:r, 0:r])
                close(ins)

            need(pe, DRAINS["v"][-1], DRAINS["a"][-1])
            pe.wait_ge(h2_split, 3)

            def spread_row(t, tk, s, free):
                r = OUTS[t]
                pe.wait_ge(onehot_ready, tk + 1)
                if free:
                    pe.wait_ge(dotted, tk - 1)
                for n in range(2):
                    cols = slice(512 * n, 512 * n + 512)
                    out = ps[:, 2 * (s % 2) + n, :]
                    pe.matmul(out, onehot[s][0:r, :], h2hi[0:r, t, cols], start=True, stop=False)
                    ins = pe.matmul(out, onehot[s][0:r, :], h2lo[0:r, t, cols], start=False, stop=True)
                ins.then_inc(spread, 1)

            def combine(tk, g, s, first, last):
                pe.wait_ge(wz_ready, tk + 1)
                pe.wait_ge(v_landed[s], 16 * (g + 1))
                for n in range(2):
                    ins = pe.matmul(ps[:, 4 + n, :], wz[s][:, :], vbuf[:, s, 512 * n:512 * n + 512],
                                    start=first, stop=last, skip_group_check=True)
                ins.then_inc(combined, 1)

            for i, t in enumerate(ORDER):
                groups = OUTS[t] // NS

                def group(g, first=False, last=False):
                    tk = (GROUP0[t] + g) * NS
                    for s in range(NS):
                        if not (last and s == NS - 1):
                            spread_row(t, tk + s + 1, (s + 1) % NS, i > 0 or not first or s >= 1)
                        combine(tk + s, GROUP0[t] + g, s, first and s == 0, last and s == NS - 1)

                spread_row(t, GROUP0[t] * NS, 0, i > 0)
                if i:
                    pe.wait_ge(acc_read, i)
                group(0, first=True)
                with pe.Fori(1, groups - 1) as g:
                    group(g)
                group(groups - 1, last=True)

        @block.scalar
        def _(act):
            def drains(job):
                assert DRAINS["a"][a_at[0]] == job, (job, DRAINS["a"][a_at[0]])
                a_at[0] += 1
                return take(act, job)

            a_at, junk = [0], mT[:, 0:4, 0:256]

            def copy(out, in_, job):
                release(act.activation(out, in_, ACT.Copy), job)

            for t in TILES:
                act.wait_ge(x_in[t], 32 if t == C else 16)
                r = ROWS[t]
                if t:
                    act.wait_ge(ssq_done, t)
                act.activation(junk[0:r], x[0:r, t, :].rearrange("p (a b) -> p a b", a=4), ACT.Square,
                               accum_out=stat[0:r, t, 0:1]).then_inc(ssq_done, 1)
            for t in TILES:
                act.wait_ge(mean_done, t + 1)
                act.activation(stat[0:ROWS[t], t, 2:3], stat[0:ROWS[t], t, 1:2], ACT.Sqrt).then_inc(root_done, 1)
            for t in TILES:
                r = ROWS[t]
                bank = drains(f"q{t}")[0:r, :].rearrange("r (g j d) -> r g j d", g=AKV, j=AG)
                copy(qkv[0:r, t, 0:512].rearrange("r (j g d) -> r g j d", g=AKV, j=AG), bank, f"q{t}")
            for t in TILES:
                r = ROWS[t]
                copy(qkv[0:r, t, 512:768], drains(f"kv{t}")[0:r, 0:256], f"kv{t}")
            act.wait_ge(ld_abs, 1)
            act.activation(bcum[:, :, :], kt[:, :, :], ACT.Exp, scale=-1.0).then_inc(a_step, 1)
            act.wait_ge(a_step, 1)
            act.activation(bcum[:, :, :], bcum[:, :, :], ACT.Ln, bias=1.0).then_inc(ld_log, 1)
            for t in TILES:
                r = ROWS[t]
                copy(vb[0:r, t, :], drains(f"vb{t}")[0:r, :], f"vb{t}")
            act.wait_ge(b_ready, 1)
            act.activation(eb[:, :, :], bcum[:, :, :], ACT.Exp).then_inc(b_exp, 1)
            act.activation(kt[:, :, :], bcum[:, :, :], ACT.Exp, scale=-1.0).then_inc(b_exp, 1)
            act.wait_ge(last_ready, 3)
            act.activation(ket[:, :, :], ket[:, :, :], ACT.Exp).then_inc(ket_exp, 1)
            for t in TILES:
                r = ROWS[t]
                bank = drains(f"qT{t}").rearrange("p (j r) -> p j r", j=AG)
                copy(qT[:, :, COL[t]:COL[t] + r], bank[:, :, 0:r], f"qT{t}")
            for t in TILES:
                r = OUTS[t]
                bank = take(act, f"gb{t}")
                act.activation(gate[0:r, t, :], bank[0:r, :], ACT.Sigmoid).then_inc(gate_sig, 1)

            def probs(i, width):
                act.wait_ge(max_ready, i + 1)
                for h in range(AH):
                    act.activation(sm[:, h, 0:width], sm[:, h, 0:width], ACT.Exp, bias=soft[:, 1, h:h + 1],
                                   accum_out=soft[:, 3, h:h + 1])
                act.activation(soft[:, 4, :], soft[:, 2, :], ACT.Exp).then_inc(probs_ready, 1)

            def turn(t):
                for i in range(4):
                    job = f"pT{'AB'[t]}.{i}"
                    bank = drains(job).rearrange("p (h c q) -> p h c q", h=2, c=2)
                    if t == A:
                        act.activation(pT[:, 2 * i:2 * i + 2, 0, :], bank[:, :, 0, :], ACT.Copy)
                        copy(pT[0:48, 2 * i:2 * i + 2, 1, :], bank[0:48, :, 1, :], job)
                    else:
                        copy(pT[:, 2 * i:2 * i + 2], bank, job)
                job = f"yaT{t}"
                bank = drains(job).rearrange("p (j r) -> p j r", j=AG)
                copy(yaT[:, :, COL[t]:COL[t] + P], bank, job)

            for i in range(2):
                job = f"kcT{i}"
                bank = drains(job).rearrange("p (b s) -> p b s", b=4)
                copy(kcT[:, 4 * i:4 * i + 4, :], bank, job)
            probs(0, 176)
            act.wait_ge(smax_ready, 1)
            for grp in range(2):
                act.activation(pss[:, grp, :], pss[:, grp, :], ACT.Exp, bias=softs[:, 1, grp:grp + 1],
                               accum_out=softs[:, 3, grp:grp + 1])
            act.activation(softs[:, 4, :], softs[:, 2, :], ACT.Exp).then_inc(sprobs_ready, 1)
            turn(A)
            probs(1, 256)
            turn(B)
            for t in TILES:
                job, r = f"keT{t}", ROWS[t]
                bank = drains(job).rearrange("p (c d) -> p c d", c=4)
                copy(ke[0:r, t], bank[0:r, 0:2, :], job)
            for t in TILES:
                r, bank = OUTS[t], take(act, f"o{t}")
                if t:
                    act.wait_ge(o_squared, t)
                for h in range(BH):
                    ins = act.activation(junk[0:r, h, 0:BV], bank[0:r, h * BV:h * BV + BV], ACT.Square,
                                         accum_out=oss[0:r, t, 0, h:h + 1])
                ins.then_inc(o_squared, 1)
                act.wait_ge(o_mean, t + 1)
                act.activation(oss[0:r, t, 2, :], oss[0:r, t, 1, :], ACT.Sqrt).then_inc(o_root, 1)
            for t in TILES:
                job, r = f"ybT{t}", OUTS[t]
                bank = drains(job).rearrange("p (j r) -> p j r", j=BH)
                copy(ybT[:, :, COL[t]:COL[t] + r], bank[:, :, 0:r], job)
            for mt in range(KT):
                for i, job in enumerate((f"ga{mt}", f"gr{mt}")):
                    bank = drains(job)
                    if mt:
                        act.wait_ge(merged, mt)
                    elif i == 0:
                        need(act, "ybT2")
                    release(act.activation(sga[:, i, 0:NO], bank[:, 0:NO], ACT.Sigmoid), job)
            for t in TILES:
                act.wait_ge(x2_ready, t + 1)
                if t:
                    act.wait_ge(ssq_done, 3 + t)
                r = OUTS[t]
                act.activation(hT[0:r, 0:4, 0:256], x[0:r, t, :].rearrange("p (a b) -> p a b", a=4), ACT.Square,
                               accum_out=stat[0:r, t, 0:1]).then_inc(ssq_done, 1)
            for t in TILES:
                r = OUTS[t]
                act.wait_ge(mean_done, 3 + t + 1)
                act.activation(stat[0:r, t, 2:3], stat[0:r, t, 1:2], ACT.Sqrt).then_inc(root_done, 1)
            for h in range(PH):
                copy(qp[:, h, :], drains(f"pq{h}")[:, 0:NO], f"pq{h}")
            for t in ORDER:
                for i in range(4):
                    job, r = f"ps{t}.{i}", OUTS[t]
                    bank = drains(job)
                    copy(sc[0:r, t, 2 * i:2 * i + 2].rearrange("r h n -> r (h n)"), bank[0:r, :], job)
            for i, t in enumerate(ORDER):
                r = OUTS[t]
                act.wait_ge(fv_ready, i + 1)
                act.activation(route[0:r, 1], route[0:r, 1], ACT.Exp).then_inc(w_exp, 1)

            for i, t in enumerate(ORDER):
                with act.Fori(0, OUTS[t] // NS) as g:
                    for s in range(NS):
                        act.wait_ge(dotted, (GROUP0[t] + g) * NS + (s + 1))
                        act.activation(acts[:, s:s + 1], dots[:, s:s + 1], ACT.Gelu).then_inc(gelued, 1)
                r = OUTS[t]
                act.wait_ge(acc_read, i + 1)
                act.activation(hT[0:r, 0:4, 0:256], x[0:r, t, :].rearrange("p (a b) -> p a b", a=4), ACT.Square,
                               accum_out=stat[0:r, t, 0:1]).then_inc(fin_ssq, 1)
                act.wait_ge(fin_mean, i + 1)
                act.activation(stat[0:r, t, 2:3], stat[0:r, t, 1:2], ACT.Sqrt).then_inc(fin_root, 1)

        @block.vector
        def _(dve):
            links, v_at = [0], [0]

            def link(ins):
                links[0] += 1
                ins.then_inc(v_step, 1)
                dve.wait_ge(v_step, links[0])

            def drains(job):
                assert DRAINS["v"][v_at[0]] == job, (job, DRAINS["v"][v_at[0]])
                v_at[0] += 1
                return take(dve, job)

            def mean(t, r, ssq, done):
                ins = dve.tensor_scalar(stat[0:r, t, 1:2], stat[0:r, t, 0:1], 1.0 / D, EPS, ALU.mult, ALU.add)
                ins.then_inc(done, 1)

            dve.wait_ge(cst_landed, 16)
            dve.wait_ge(small_landed, 16 * N_SMALL_IN)
            for t in TILES:
                dve.wait_ge(ssq_done, t + 1)
                mean(t, ROWS[t], ssq_done, mean_done)
            for t in TILES:
                r = ROWS[t]
                dve.wait_ge(root_done, t + 1)
                link(dve.reciprocal(stat[0:r, t, 3:4], stat[0:r, t, 2:3]))
                dve.tensor_scalar(hrow[0:r, t, :], x[0:r, t, :], stat[0:r, t, 3:4], None, ALU.mult
                                  ).then_inc(rows_normed, 1)
            bank = drains("gvecT")
            release(dve.tensor_copy(gT[:, :], bank[:, 0:18]), "gvecT")
            need(dve, "gvecT")
            for t in TILES:
                for half in range(2):
                    job, r = f"hT{t}.{half}", ROWS[t]
                    bank = drains(job).rearrange("p (k r) -> p k r", k=4)
                    gain = gT[:, 4 * half:4 * half + 4].unsqueeze(2).broadcast_to([P, 4, r])
                    release(dve.tensor_tensor(hT[:, 4 * half:4 * half + 4, COL[t]:COL[t] + r], bank[:, :, 0:r], gain,
                                              ALU.mult), job)

            def rope(t):
                r = ROWS[t]
                need(dve, f"q{t}", f"kv{t}")
                if t:
                    dve.wait_ge(roped, t)
                heads = qkv[0:r, t, 0:640].rearrange("r (h d) -> r h d", d=AD)
                half = ROPE // 2
                cos = C_("cos")[0:r, t * ROPE:t * ROPE + ROPE].unsqueeze(1).broadcast_to([r, 10, ROPE])
                sin = C_("sin")[0:r, t * half:t * half + half].unsqueeze(1).broadcast_to([r, 10, half])
                dve.tensor_tensor(ropet[0:r, :, 0:ROPE], heads[:, :, 0:ROPE], cos, ALU.mult)
                dve.tensor_tensor(ropet[0:r, :, ROPE:ROPE + half], heads[:, :, half:ROPE], sin, ALU.mult)
                link(dve.tensor_tensor(ropet[0:r, :, ROPE + half:2 * ROPE], heads[:, :, 0:half], sin, ALU.mult))
                dve.tensor_tensor(heads[:, :, 0:half], ropet[0:r, :, 0:half], ropet[0:r, :, ROPE:ROPE + half],
                                  ALU.subtract)
                dve.tensor_tensor(heads[:, :, half:ROPE], ropet[0:r, :, half:ROPE],
                                  ropet[0:r, :, ROPE + half:2 * ROPE], ALU.add).then_inc(roped, 1)

            for t in TILES:
                rope(t)
            bank = drains("lrT")
            release(dve.tensor_copy(lrT[:, :], bank[0:RANK, 0:NT]), "lrT")
            for p in range(2):
                bank = drains(f"ld{p}")
                release(dve.tensor_scalar(eb[:, p, :], bank[:, 0:NT], gT[:, 16 + p:17 + p], None, ALU.add), f"ld{p}")
            need(dve, "ld1")
            dve.scalar_tensor_tensor(out=kt[:, :, :], in0=eb[:, :, :], scalar=-1.0, in1=eb[:, :, :], op0=ALU.mult,
                                     op1=ALU.max).then_inc(ld_abs, 1)
            link(dve.tensor_scalar(ket[:, :, :], eb[:, :, :], 0.0, 1.0 / 16, ALU.min, ALU.mult))
            dve.wait_ge(ld_log, 1)
            link(dve.scalar_tensor_tensor(out=ket[:, :, :], in0=bcum[:, :, :], scalar=-1.0 / 16, in1=ket[:, :, :],
                                          op0=ALU.mult, op1=ALU.add))
            for p in range(2):
                ins = dve.tensor_tensor_scan(bcum[:, p, :], C_("reset"), ket[:, p, :], 0.0, ALU.mult, ALU.add)
            ins.then_inc(b_ready, 1)
            dve.wait_ge(b_ready, 1)
            for c0, n, w in ((0, 4, CHUNK), (256, DEC_B, DEC_T), (288, 1, META)):
                b = bcum[:, :, c0:c0 + n * w].rearrange("p a (n w) -> p a n w", w=w)
                out = ket[:, :, c0:c0 + n * w].rearrange("p a (n w) -> p a n w", w=w)
                dve.tensor_tensor(out, b[:, :, :, w - 1:w].broadcast_to([P, 2, n, w]), b, ALU.subtract
                                  ).then_inc(last_ready, 1)

            dve.wait_ge(zeroed, 7)
            for t in TILES:
                job, r = f"kT{t}", ROWS[t]
                bank = drains(job)
                if t == C:
                    dve.tensor_copy(kTs[:, :], bank[:, 0:SAMP])
                dve.tensor_copy(kz[0:AD, 0, COL[t]:COL[t] + r], bank[0:AD, 0:r])
                release(dve.tensor_copy(kz[AD:P, 1, COL[t]:COL[t] + r], bank[AD:P, 0:r]), job)
            for t in TILES:
                job, r = f"gb{t}", ROWS[t]
                bank = drains(job)
                r = OUTS[t]
                dve.wait_ge(gate_sig, t + 1)
                release(dve.tensor_tensor(gate[0:r, t, :], bank[0:r, :], gate[0:r, t, :], ALU.mult), job)
                need(dve, job)
                rows = gate[0:r, t, :].rearrange("r (h e) -> r h e", h=BH)
                dve.tensor_tensor(rows, rows, gnb[0:r, :].unsqueeze(1).broadcast_to([r, BH, BV]), ALU.mult)
            dve.wait_ge(b_exp, 2)
            dve.wait_ge(ket_exp, 1)
            for p in range(2):
                job = f"kb{p}"
                bank = drains(job)
                dve.tensor_tensor(kt[:, p, :], bank[:, 0:NT], kt[:, p, :], ALU.mult)
                release(dve.tensor_tensor(ket[:, p, :], bank[:, 0:NT], ket[:, p, :], ALU.mult), job)
            for p in range(2):
                job = f"qb{p}"
                bank = drains(job)
                for hh in range(2):
                    lanes = slice(hh * BK, hh * BK + BK)
                    ins = dve.scalar_tensor_tensor(out=qh[lanes, 2 * p + hh, :], in0=bank[lanes, 0:NT],
                                                   scalar=BK ** -0.5, in1=eb[lanes, p, :], op0=ALU.mult, op1=ALU.mult)
                release(ins, job)

            def row_max(t):
                width, mask = (176, C_("mask_a")) if t == A else (256, C_("mask_b"))
                for j in range(AG):
                    job = f"sc{'AB'[t]}.{j}"
                    bank = drains(job).rearrange("p (g k) -> p g k", g=2)
                    out = sm[:, :, :].rearrange("p (g j) k -> p j g k", g=2)[:, j, :, 0:width]
                    release(dve.scalar_tensor_tensor(out=out, in0=bank[:, :, 0:width], scalar=AD ** -0.5,
                                                     in1=mask.unsqueeze(1).broadcast_to([P, 2, width]),
                                                     op0=ALU.mult, op1=ALU.add), job)
                need(dve, job)
                link(dve.tensor_reduce(soft[:, 0, :], sm[:, :, 0:width], AX_X, ALU.max))
                link(dve.tensor_tensor(soft[:, 0, :], soft[:, 0, :], sinkb[:, :], ALU.max))
                dve.tensor_scalar(soft[:, 1, :], soft[:, 0, :], -1.0, None, ALU.mult)
                dve.tensor_tensor(soft[:, 2, :], sinkb[:, :], soft[:, 0, :], ALU.subtract).then_inc(max_ready, 1)

            def weigh(t):
                dve.wait_ge(probs_ready, t + 1)
                link(dve.tensor_tensor(soft[:, 5, :], soft[:, 3, :], soft[:, 4, :], ALU.add))
                link(dve.reciprocal(soft[:, 5, :], soft[:, 5, :]))
                job = f"pv{'AB'[t]}"
                bank = drains(job).rearrange("p (g j d) -> p g j d", g=AKV, j=AG)
                share = soft[:, 5, :].rearrange("p (g j) -> p g j", g=AKV).unsqueeze(3).broadcast_to([P, AKV, AG, AD])
                release(dve.tensor_tensor(ya[:, :].rearrange("p (j g d) -> p g j d", g=AKV, j=AG), bank, share,
                                          ALU.mult), job)

            row_max(A)
            need(dve, "qT2")
            for g in range(AKV):
                lanes = slice(g * AD, g * AD + AD)
                for grp in range(2):
                    out = qs[lanes, grp, :].rearrange("p (b h t) -> p h b t", b=4, h=AH)[:, 4 * g:4 * g + 4]
                    src = qT[lanes, :, 256 + 16 * grp:272 + 16 * grp].rearrange("p j (b t) -> p j b t", t=DEC_T)
                    ins = dve.tensor_copy(out, src)
            link(ins)
            for b in range(DEC_B):
                c0 = (b % 4) * 32
                ins = dve.tensor_copy(qzs[:, b, c0:c0 + 32], qs[:, b // 4, c0:c0 + 32])
            ins.then_inc(qs_ready, 1)
            dve.tensor_tensor(sinkt[:, :], sinkb[:, :], C_("hsel"), ALU.mult).then_inc(v_step, 1)
            links[0] += 1
            dve.wait_ge(v_step, links[0])
            link(dve.tensor_reduce(sinkr[:, :], sinkt[:, :], AX_X, ALU.add))
            for grp in range(2):
                job = f"ss{grp}"
                bank = drains(job)
                release(dve.scalar_tensor_tensor(out=pss[:, grp, :], in0=bank[:, 0:160], scalar=AD ** -0.5,
                                                 in1=C_("mask_s")[:, grp * 160:grp * 160 + 160], op0=ALU.mult,
                                                 op1=ALU.add), job)
            need(dve, "ss1")
            link(dve.tensor_reduce(softs[:, 0, :], pss[:, :, :], AX_X, ALU.max))
            link(dve.tensor_scalar(softs[:, 0, :], softs[:, 0, :], sinkr[:, 0:1], None, ALU.max))
            dve.tensor_scalar(softs[:, 1, :], softs[:, 0, :], -1.0, None, ALU.mult)
            dve.tensor_scalar(softs[:, 2, :], softs[:, 0, :], -1.0, sinkr[:, 0:1], ALU.mult, ALU.add
                              ).then_inc(smax_ready, 1)
            weigh(A)
            row_max(B)
            dve.wait_ge(sprobs_ready, 1)
            link(dve.tensor_tensor(softs[:, 5, :], softs[:, 3, :], softs[:, 4, :], ALU.add))
            link(dve.reciprocal(softs[:, 5, :], softs[:, 5, :]))
            for grp in range(2):
                job = f"spT{grp}"
                bank = drains(job)
                for b in range(4):
                    c0 = b * 32
                    dve.tensor_copy(pz[:, grp, b * P + c0:b * P + c0 + 32], bank[:, c0:c0 + 32])
                release(dve.tensor_copy(pnT[:, grp, :], bank[0:SAMP, P:2 * P]), job)
            for grp in range(2):
                job = f"spv{grp}"
                bank = drains(job)
                release(dve.tensor_scalar(so[:, grp, :], bank[:, 0:P], softs[:, 5, grp:grp + 1], None, ALU.mult), job)
            for grp in range(2):
                job = f"soT{grp}"
                bank = drains(job)
                for g in range(AKV):
                    lanes = slice(g * AD, g * AD + AD)
                    c0 = 256 + grp * 16
                    out = yaT[lanes, :, c0:c0 + 16].rearrange("p j (b t) -> p j b t", t=DEC_T)
                    src = bank[lanes, 0:P].rearrange("p (b h t) -> p h b t", b=4, h=AH)[:, 4 * g:4 * g + 4]
                    ins = dve.tensor_copy(out, src)
                release(ins, job)
            weigh(B)

            for t in TILES:
                job, r = f"AT{t}", OUTS[t]
                bank = drains(job)[0:r, 0:BH * r].rearrange("p (h i) -> p h i", h=BH)
                out = ats[:, :, :] if t == C else atm[:, t]
                mask = (C_("gla_s") if t == C else C_("gla"))[0:r].bitcast(U32)
                release(dve.copy_predicated(out, mask.unsqueeze(1).broadcast_to([r, BH, r]), bank), job)
            last = [288 + META - 1, CHUNK - 1, 2 * CHUNK - 1, 3 * CHUNK - 1, 4 * CHUNK - 1]
            for n in range(5):
                job = f"up{n}"
                bank = drains(job)
                if n:
                    dve.wait_ge(states_ready, 4 * n)
                for p in range(2):
                    for hh in range(2):
                        lanes = slice(hh * BK, hh * BK + BK)
                        src = bank[lanes, p * 256 + hh * BV:p * 256 + hh * BV + BV]
                        if n == 0:
                            ins = dve.tensor_copy(st[lanes, 0, p, :], src)
                        else:
                            ins = dve.scalar_tensor_tensor(out=st[lanes, n, p, :], in0=st[lanes, n - 1, p, :],
                                                           scalar=eb[lanes, p, last[n]:last[n] + 1], in1=src,
                                                           op0=ALU.mult, op1=ALU.add)
                        if not (p and hh):
                            ins.then_inc(states_ready, 1)
                dve.wait_ge(states_ready, 4 * n + 3)
                release(ins, job)
                need(dve, job)
                dve.engine_nop().then_inc(states_ready, 1)
            for h in range(BH):
                src = qh[:, h, 256:288].unsqueeze(1).broadcast_to([P, DEC_B, SAMP])
                ins = dve.tensor_tensor(qsz[:, h], src, C_("batch").rearrange("p (b i) -> p b i", b=DEC_B), ALU.mult)
            ins.then_inc(qsz_ready, 1)
            for t in TILES:
                job, r = f"o{t}", OUTS[t]
                bank = drains(job)
                dve.wait_ge(o_squared, t + 1)
                dve.tensor_scalar(oss[0:r, t, 1, :], oss[0:r, t, 0, :], 1.0 / BV, EPS, ALU.mult, ALU.add
                                  ).then_inc(o_mean, 1)
                dve.wait_ge(o_root, t + 1)
                link(dve.reciprocal(oss[0:r, t, 3, :], oss[0:r, t, 2, :]))
                rows = yb[0:r, t, :].rearrange("r (h e) -> r h e", h=BH)
                release(dve.tensor_tensor(rows, bank[0:r, :].rearrange("r (h e) -> r h e", h=BH),
                                          oss[0:r, t, 3, :].unsqueeze(2).broadcast_to([r, BH, BV]), ALU.mult), job)
                need(dve, job)
                dve.tensor_tensor(yb[0:r, t, :], yb[0:r, t, :], gate[0:r, t, :], ALU.mult).then_inc(yb_ready, 1)
            for p in range(2):
                decay = eb[:, p, 256:288].rearrange("p (b t) -> p b t", t=DEC_T)[:, :, DEC_T - 1:DEC_T]
                ins = dve.tensor_tensor(s0[:, p], s0[:, p], decay.broadcast_to([P, DEC_B, BV]), ALU.mult)
            link(ins)
            for h in range(BH):
                src = vb[0:SAMP, C, h * BV:h * BV + BV].unsqueeze(1).broadcast_to([SAMP, DEC_B, BV])
                dve.tensor_tensor(vblk[:, :, :], src,
                                  C_("batch_rows")[0:SAMP].unsqueeze(2).broadcast_to([SAMP, DEC_B, BV]), ALU.mult
                                  ).then_inc(vblk_ready, 1)
                lanes = slice((h % 2) * BK, (h % 2) * BK + BK)
                for i in range(2):
                    job = f"us{h}.{i}"
                    bank = drains(job).rearrange("p (b e) -> p b e", b=4)
                    part = s0[lanes, h // 2, 4 * i:4 * i + 4, :]
                    release(dve.tensor_tensor(part, part, bank[lanes], ALU.add), job)
            for mt in range(KT):
                need(dve, f"ga{mt}")
                job = f"za{mt}"
                bank = drains(job)
                release(dve.tensor_tensor(mT[:, mt, 0:NO], bank[:, 0:NO], sga[:, 0, 0:NO], ALU.mult), job)
                need(dve, job, f"gr{mt}")
                job = f"zb{mt}"
                bank = drains(job)
                release(dve.tensor_tensor(sga[:, 1, 0:NO], bank[:, 0:NO], sga[:, 1, 0:NO], ALU.mult), job)
                need(dve, job)
                dve.tensor_tensor(mT[:, mt, 0:NO], mT[:, mt, 0:NO], sga[:, 1, 0:NO], ALU.add).then_inc(merged, 1)
            for n in range(2):
                for t in TILES:
                    job, r = f"wo{n}.{t}", OUTS[t]
                    bank = drains(job)
                    part = x[0:r, t, 512 * n:512 * n + 512]
                    release(dve.tensor_tensor(part, part, bank[0:r, :], ALU.add), job)
                    if n:
                        need(dve, job)
                        dve.engine_nop().then_inc(x2_ready, 1)
            dve.wait_ge(mixer_out, 16 * N_MIX_OUT)
            dve.wait_ge(zeroed, 8)
            for i in range(2):
                job = f"kk{i}"
                bank = drains(job).rearrange("p (h n) -> p h n", h=4)
                dve.tensor_copy(kbd[0:64, 4 * i:4 * i + 4, 0:PK], bank[0:64])
                ins = dve.tensor_copy(kbd[64:P, 4 * i:4 * i + 4, PK:2 * PK], bank[64:P])
                release(ins, job)
            need(dve, "kk1")
            dve.engine_nop().then_inc(kbd_ready, 1)
            for t in TILES:
                dve.wait_ge(ssq_done, 3 + t + 1)
                mean(t, OUTS[t], ssq_done, mean_done)
            for t in TILES:
                r = OUTS[t]
                dve.wait_ge(root_done, 3 + t + 1)
                link(dve.reciprocal(stat[0:r, t, 3:4], stat[0:r, t, 2:3]))
                row = h2hold[t][0:r, :]
                dve.scalar_tensor_tensor(out=row, in0=x[0:r, t, :], scalar=stat[0:r, t, 3:4], in1=gffn[0:r, :],
                                         op0=ALU.mult, op1=ALU.mult).then_inc(rows_normed, 1)
                dve.wait_ge(rows_normed, 3 + t + 1)
                link(dve.tensor_copy(h2hi[0:r, t, :], row))
                dve.tensor_tensor(h2lo[0:r, t, :], row, h2hi[0:r, t, :].bitcast(F32), ALU.subtract
                                  ).then_inc(h2_split, 1)
            for t in TILES:
                for half in range(2):
                    job, r = f"h2T{t}.{half}", OUTS[t]
                    bank = drains(job).rearrange("p (k r) -> p k r", k=4)
                    release(dve.tensor_copy(hT[:, 4 * half:4 * half + 4, COL[t]:COL[t] + r], bank[:, :, 0:r]), job)

            def top16(values, spare, out, index):
                link(dve.max(out[:, 0:8], values))
                link(dve.max_index(index[:, 0:8], out[:, 0:8], values))
                link(dve.match_replace(spare, out[:, 0:8], values, FLOOR))
                link(dve.max(out[:, 8:16], spare))
                link(dve.max_index(index[:, 8:16], out[:, 8:16], spare))

            for i, t in enumerate(ORDER):
                r = OUTS[t]
                need(dve, f"ps{t}.3")
                if i:
                    need(dve, f"rT{ORDER[i - 1]}")
                for h in range(PH):
                    for c in range(2):
                        top16(sc[0:r, t, h, c * PK:c * PK + PK], less[0:r, :], sv[0:r, h, c, :], si[0:r, h, c, :])
                    a = sv[0:r, h, 0, :].unsqueeze(2).broadcast_to([r, TOPK, TOPK])
                    b = sv[0:r, h, 1, :].unsqueeze(1).broadcast_to([r, TOPK, TOPK])
                    link(dve.tensor_tensor(cand[0:r, :].rearrange("r (i j) -> r i j", i=TOPK), a, b, ALU.add))
                    top16(cand[0:r, :], cand2[0:r, :], fv[0:r, h, :], fpos[0:r, h, :])
                link(dve.tensor_tensor(route[0:r, 1], fv[0:r], fv[0:r, :, 0:1].broadcast_to([r, PH, TOPK]),
                                       ALU.subtract))
                dve.engine_nop().then_inc(fv_ready, 1)
                pos = fpos[0:r].rearrange("r h k -> r (h k)")
                dve.tensor_single_scalar(fij[0:r, 0, :], pos, 4, ALU.logical_shift_right)
                dve.tensor_single_scalar(fij[0:r, 1, :], pos, TOPK - 1, ALU.bitwise_and)
                link(dve.tensor_copy(sif[0:r], si[0:r]))
                link(dve.tensor_copy(fijf[0:r].rearrange("r c h k -> r (c h k)"),
                                     fij[0:r].rearrange("r c k -> r (c k)")))
                for c in range(2):
                    want = fijf[0:r, c].rearrange("r h k -> r (h k)").unsqueeze(2).broadcast_to([r, P, TOPK])
                    have = C_("iota")[0:r].unsqueeze(1).broadcast_to([r, P, TOPK])
                    grid = pick[0:r].rearrange("r h k i -> r (h k) i")
                    link(dve.tensor_tensor(grid, want, have, ALU.is_equal))
                    number = sif[0:r, :, c, :].unsqueeze(2).broadcast_to([r, PH, TOPK, TOPK])
                    link(dve.tensor_tensor(pick[0:r], pick[0:r], number, ALU.mult))
                    link(dve.tensor_reduce(eij[0:r, c, :], grid, AX_X, ALU.add))
                dve.scalar_tensor_tensor(out=route[0:r, 0].rearrange("r h k -> r (h k)"), in0=eij[0:r, 0, :],
                                         scalar=float(PK), in1=eij[0:r, 1, :], op0=ALU.mult, op1=ALU.add)
                dve.wait_ge(w_exp, i + 1)
                link(dve.tensor_reduce(wsum[0:r, 0, :], route[0:r, 1], AX_X, ALU.add))
                link(dve.reciprocal(wsum[0:r, 1, :], wsum[0:r, 0, :]))
                dve.tensor_tensor(route[0:r, 1], route[0:r, 1],
                                  wsum[0:r, 1, :].unsqueeze(2).broadcast_to([r, PH, TOPK]), ALU.mult
                                  ).then_inc(routed, 1)
                job = f"rT{t}"
                bank = drains(job).rearrange("p (a r) -> p a r", a=4)
                dve.tensor_copy(wT[:, COL[t]:COL[t] + r], bank[:, 1, 0:r])
                release(dve.tensor_copy(idxT[:, COL[t]:COL[t] + r], bank[:, 0, 0:r]), job)

            spot = C_("spot")

            def token(tk, g, col, row, s, reuse):
                now, back, place = held(dve, tk + 1), held(dve, tk - (NS - 1)), held(dve, 127 - row)
                dve.wait_ge(spread, now)
                dve.wait_ge(u_landed[s], 16 * (g + 1))
                row_on_all = ps[:, 2 * (s % 2):2 * (s % 2) + 2, :]
                u = ub[:, s, :].rearrange("p (a b) -> p a b", a=2)
                dve.tensor_tensor_reduce(u, row_on_all, u, 1.0, 0.0, ALU.mult, ALU.add, dots[:, s:s + 1]
                                         ).then_inc(dotted, 1)
                if reuse:
                    dve.wait_ge(combined, back)
                dve.wait_ge(gelued, now)
                dve.sem_inc(v_turn, 1)
                dve.tensor_scalar(wz[s][:, :], spot[:, bass.ds(place, P)], wT[:, bass.ds(col, 1)],
                                  acts[:, s:s + 1], ALU.mult, ALU.mult).then_inc(wz_ready, 1)

            for i, t in enumerate(ORDER):
                r, g0 = OUTS[t], 0
                if i == 0:
                    for s in range(NS):
                        token(s, 0, COL[t] + s, s, s, False)
                    g0 = 1
                with dve.Fori(g0, r // NS) as g:
                    for s in range(NS):
                        token((GROUP0[t] + g) * NS + s, GROUP0[t] + g, g * NS + (COL[t] + s), g * NS + s, s, True)
                dve.wait_ge(combined, (GROUP0[t] + r // NS) * NS)
                rows = x[0:r, t, :].rearrange("p (a b) -> p a b", a=2)
                dve.tensor_tensor(rows, rows, ps[0:r, 4:6, :], ALU.add).then_inc(acc_read, 1)
                dve.wait_ge(fin_ssq, i + 1)
                mean(t, r, fin_ssq, fin_mean)
                dve.wait_ge(fin_root, i + 1)
                link(dve.reciprocal(stat[0:r, t, 3:4], stat[0:r, t, 2:3]))
                dve.wait_ge(router_landed, 16 * 2)
                if i == 2:
                    dve.wait_ge(y_out[0], 16)
                dve.scalar_tensor_tensor(out=h2[0:r, i % 2, :], in0=x[0:r, t, :], scalar=stat[0:r, t, 3:4],
                                         in1=gfin[0:r, :], op0=ALU.mult, op1=ALU.mult).then_inc(y_ready, 1)


_INS = ["x_prompt", "x_sample", "cache_k_window", "cache_v_window", "state_gla", "meta_tokens", "g_norm_mix", "w_in",
        "w_gate_up", "b_gate", "attn_sinks", "g_gla_norm", "w_branch_a", "w_branch_b", "w_out", "g_norm_ffn",
        "w_peer_q", "peer_sub_keys", "peer_u", "peer_v", "g_norm_final"]
_OUTS = [(1, SEQ, D), (DEC_B, DEC_T, D), (1, 1, WINDOW, AKV, AD), (1, 1, WINDOW, AKV, AD), (1, 1, BH, BK, BV),
         (1, DEC_B, WINDOW, AKV, AD), (1, DEC_B, WINDOW, AKV, AD), (1, DEC_B, BH, BK, BV)]


def kernel(**inputs):
    import concourse.bacc as bacc
    from concourse.bass_utils import run_bass_kernel_spmd

    nc = bacc.Bacc("TRN2", target_bir_lowering=False, num_devices=1)
    arrays, args = {}, []
    for name in _INS:
        a = np.ascontiguousarray(inputs[name])
        arrays[f"in_{name}"] = a
        args.append(nc.dram_tensor(f"in_{name}", a.shape, mybir.dt.from_np(a.dtype), kind="ExternalInput").ap())
    arrays["shape_constants"] = shape_constants()
    args.append(nc.dram_tensor("shape_constants", (P, CST_COLS), F32, kind="ExternalInput").ap())
    for i, shape in enumerate(_OUTS):
        args.append(nc.dram_tensor(f"out_{i}", shape, F32, kind="ExternalOutput").ap())
    hybrid_step(nc, *args)
    r = run_bass_kernel_spmd(nc, [arrays], core_ids=[0])
    return tuple(r.results[0][f"out_{i}"] for i in range(len(_OUTS)))
```

```python
from contextlib import ExitStack

import numpy as np

import concourse.bass as bass
from concourse import mybir

F32 = mybir.dt.float32
F32R = mybir.dt.float32r
I32 = mybir.dt.int32
U32 = mybir.dt.uint32
ALU = mybir.AluOpType
ACT = mybir.ActivationFunctionType
AX_X = mybir.AxisListType.X

P = 128
D = 1024
KT = D // P
SEQ, META, DEC_B, DEC_T = 256, 16, 8, 4
SAMP = DEC_B * DEC_T
PAST, META_PAD, WINDOW = 2048, 112, 128
AH, AKV, AD = 8, 2, 64
AG = AH // AKV
ROPE = AD // 4
THETA = 500000.0
BH, BK, BV = 4, 64, 128
CHUNK = 64
RANK = 16
PH, PK, TOPK = 8, 128, 16
NEXP = PK * PK
EPS = 1e-6
NEG = -1e30
FLOOR = -3.0e38

A, B, C = 0, 1, 2
COL = (0, 128, 256)
ROWS = (128, 128, SAMP + META)
OUTS = (128, 128, SAMP)
NT = 304
NO = 288
TILES = (A, B, C)
ORDER = (C, A, B)

Q0, K0, QB0, KB0, VB0, GB0, LR0, GA0, GR0 = 0, 512, 768, 1024, 1280, 1792, 2304, 2320, 3344

CST = dict(ident=128, cos=3 * ROPE, sin=3 * ROPE // 2, mask_a=176, mask_b=256, mask_s=320, gla=128, gla_s=SAMP,
           reset=NT, hsel=AH, batch=DEC_B * SAMP, batch_rows=DEC_B, iota=TOPK, spot=255)
CST_AT, _n = {}, 0
for _name, _w in CST.items():
    CST_AT[_name] = (_n, _w)
    _n += _w
CST_COLS = _n


def shape_constants():
    c = {k: np.zeros((P, w), np.float32) for k, w in CST.items()}
    c["ident"][:] = np.eye(P)
    inv = np.float32(THETA) ** (-np.arange(0, ROPE, 2, dtype=np.float32) / np.float32(ROPE))
    r = np.arange(P)
    pos = np.stack([META + r, META + 128 + r, np.where(r < SAMP, PAST + r % DEC_T, r - SAMP)], 1)
    ang = pos.astype(np.float32)[:, :, None] * inv.astype(np.float32)
    cos, sin = np.cos(ang).astype(np.float32), np.sin(ang).astype(np.float32)
    c["cos"][:] = np.concatenate([cos, cos], 2).reshape(P, -1)
    c["sin"][:] = sin.reshape(P, -1)
    q = r[:, None]
    key = np.arange(176)[None]
    own = key <= q
    meta = (key >= 160) & (q <= META_PAD + key - 160)
    c["mask_a"][:] = np.where(np.where(key < 128, own, meta), 0.0, NEG)
    key = np.arange(256)[None]
    c["mask_b"][:] = np.where(np.where(key < 128, key >= q, key - 128 <= q), 0.0, NEG)
    step = q % DEC_T
    for grp in range(2):
        key = np.arange(160)[None]
        new = (key - 128) // DEC_T == grp * 4 + q // 32
        new = new & ((key - 128) % DEC_T <= step)
        c["mask_s"][:, grp * 160:grp * 160 + 160] = np.where(np.where(key < 128, key >= step, new), 0.0, NEG)
    i = np.arange(P)[None]
    c["gla"][:] = (q <= i) & (q // CHUNK == i // CHUNK)
    i = np.arange(SAMP)[None]
    c["gla_s"][:] = (q <= i) & (q // DEC_T == i // DEC_T)
    c["reset"][:] = 1.0
    c["reset"][:, [0, 64, 128, 192, *range(256, 288, DEC_T), 288]] = 0.0
    b, i = np.arange(DEC_B)[:, None], np.arange(SAMP)[None]
    c["batch"][:] = (i // DEC_T == b).reshape(1, -1)
    c["batch_rows"][:] = q // DEC_T == np.arange(DEC_B)[None]
    c["iota"][:] = np.arange(TOPK)
    c["hsel"][:] = q // DEC_T % AH == np.arange(AH)[None]
    c["spot"][:, 127] = 1.0
    return np.concatenate([c[k] for k in CST], 1)


def psum_jobs():
    jobs = [("gvecT", "v")]
    jobs += [(f"hT{t}.{half}", "v") for t in TILES for half in range(2)]
    jobs += [(f"q{t}", "a") for t in TILES]
    jobs += [(f"kv{t}", "a") for t in TILES]
    jobs += [("lrT", "v"), ("ld0", "v"), ("ld1", "v")]
    jobs += [(f"vb{t}", "a") for t in TILES]
    jobs += [(f"kT{t}", "v") for t in TILES] + [(f"qT{t}", "a") for t in TILES]
    jobs += [(f"gb{t}", "v") for t in TILES]
    jobs += [("kb0", "v"), ("kb1", "v"), ("qb0", "v"), ("qb1", "v")]
    jobs += [(f"scA.{j}", "v") for j in range(AG)]
    jobs += [("kcT0", "a"), ("kcT1", "a"), ("ss0", "v"), ("ss1", "v")]
    jobs += [(f"pTA.{i}", "a") for i in range(4)] + [("pvA", "v"), ("yaT0", "a")]
    jobs += [(f"scB.{j}", "v") for j in range(AG)]
    jobs += [("spT0", "v"), ("spT1", "v"), ("spv0", "v"), ("spv1", "v"), ("soT0", "v"), ("soT1", "v")]
    jobs += [(f"pTB.{i}", "a") for i in range(4)] + [("pvB", "v"), ("yaT1", "a")]
    jobs += [(f"keT{t}", "a") for t in TILES] + [(f"AT{t}", "v") for t in TILES]
    jobs += [(f"up{n}", "v") for n in range(5)]
    jobs += [(f"o{t}", "v") for t in TILES] + [(f"ybT{t}", "a") for t in TILES]
    jobs += [(f"us{h}.{x}", "v") for h in range(BH) for x in range(2)]
    for m in range(KT):
        jobs += [(f"ga{m}", "a"), (f"za{m}", "v"), (f"gr{m}", "a"), (f"zb{m}", "v")]
    jobs += [(f"wo{n}.{t}", "v") for n in range(2) for t in ORDER]
    jobs += [("kk0", "v"), ("kk1", "v")]
    jobs += [(f"h2T{C}.{half}", "v") for half in range(2)] + [("pqs", "a"), ("pss", "a")]
    jobs += [(f"h2T{t}.{half}", "a") for t in (A, B) for half in range(2)]
    jobs += [(f"pq{h}", "a") for h in range(PH)]
    jobs += [(f"ps{t}.{i}", "a") for t in (A, B) for i in range(4)]
    return jobs


JOBS = psum_jobs()
AT = {name: i for i, (name, _) in enumerate(JOBS)}
DRAINS = {"v": [n for n, e in JOBS if e == "v"], "a": [n for n, e in JOBS if e == "a"]}
ORDINAL = {n: i + 1 for e in "va" for i, n in enumerate(DRAINS[e])}
DRAINER = dict(JOBS)

RING = 3
UNITS = [("q", "q2"), ("kv", "lrT"), ("vb", "vb2"), ("gb", "gb2"), ("qkb", "qb1")]
for _i in range(4):
    UNITS += [(f"gates{_i}", f"gr{2 * _i + 1}"), (f"branch{_i}", f"zb{2 * _i + 1}")]
UNITS += [("wo0", "wo0.1"), ("wo1", "wo1.1"), ("wq0", "pq3"), ("wq1", "pq7")]
UNIT_AT = {n: i for i, (n, _) in enumerate(UNITS)}

NS = 4
LIST_AHEAD = (2, 4, 0)
SUM_BANK = (4, 6, 4)
LIST_BANK = (None, 6, 4)
GROUP0 = {C: 0, A: OUTS[C] // NS, B: (OUTS[C] + OUTS[A]) // NS}


def hybrid_step(nc, x_prompt, x_sample, cache_k, cache_v, state_gla, meta_tokens, g_mix, w_in, w_gate_up, b_gate,
                sinks, g_gla, w_a, w_b, w_out, g_ffn, w_pq, sub_keys, peer_uv, g_final, cst_in,
                y_prompt, y_sample, nk_prompt, nv_prompt, ns_prompt, nk_sample, nv_sample, ns_sample):
    with ExitStack() as ctx:
        def sb(name, shape, dt=F32):
            return ctx.enter_context(nc.sbuf_tensor(name, shape, dt))

        def overlay(room, *variants):
            found, most = {}, 0
            for variant in variants:
                with ExitStack() as turn:
                    for name, shape, *dt in variant:
                        found[name] = turn.enter_context(nc.sbuf_tensor(name, shape, *(dt or [F32])))
                most = max(most, sum(int(np.prod(v[1][1:])) for v in variant))
            sb(room, [P, most])
            return found

        def sem(name):
            return ctx.enter_context(nc.semaphore(name))

        ps = ctx.enter_context(nc.psum_tensor("ps", [P, 8, 512], F32))

        cst = sb("cst", [P, CST_COLS])
        x = sb("x", [P, 3, D])
        hT = sb("hT", [P, KT, NT])
        gvec = sb("gvec", [18, P])
        gT = sb("gT", [P, 18])
        gffn = sb("gffn", [P, D])
        stat = sb("stat", [P, 4, 4])
        mT = sb("mT", [P, KT, NT])
        yaT = sb("yaT", [P, AG, NT])
        ybT = sb("ybT", [P, BH, NT])
        o1 = overlay("room_ring", [("ring", [P, RING, 4096])],
                     [("uv", [P, NS, 2 * D])]
                     + [(f"onehot{s}", [P, P], F32R) for s in range(NS)] + [(f"wz{s}", [P, P]) for s in range(NS)]
                     + [(f"islot{s}", [P, 1], I32) for s in range(NS)] + [("dots", [P, NS]), ("acts", [P, NS])])
        ring, uv, dots, acts = (o1[k] for k in ("ring", "uv", "dots", "acts"))
        onehot, wz, islot = ([o1[f"{k}{s}"] for s in range(NS)] for k in ("onehot", "wz", "islot"))
        mixer = [("qkv", [P, 3, 768]), ("qT", [P, AG, NT]), ("kz", [P, AKV, NT]), ("kTs", [P, SAMP]),
                 ("kcT", [P, DEC_B, P]), ("vc", [P, DEC_B, P]), ("sinkb", [P, AH]), ("sinkr", [P, 1]),
                 ("sinkt", [P, AH]), ("soft", [P, 6, AH]), ("softs", [P, 6, 2]), ("qs", [P, 2, P]),
                 ("qzs", [P, DEC_B, P]), ("pss", [P, 2, 160]), ("pz", [P, 2, 4 * P]), ("pnT", [SAMP, 2, P]),
                 ("ya", [P, 512]), ("vb", [P, 3, 512]), ("gate", [P, 3, 512]), ("gnb", [P, BV]),
                 ("wgu", [RANK, 256]), ("lrT", [RANK, NT]), ("eb", [P, 2, NT]), ("bcum", [P, 2, NT]),
                 ("kt", [P, 2, NT]), ("ket", [P, 2, NT]), ("qh", [P, BH, NT]), ("atm", [P, 2, BH, P]),
                 ("ats", [SAMP, BH, SAMP]), ("ke", [P, 3, 2, P]), ("s0", [P, 2, DEC_B, BV]), ("oss", [P, 3, 4, BH])]
        m = {}
        with ExitStack() as mixers:
            for name, shape in mixer:
                m[name] = mixers.enter_context(nc.sbuf_tensor(name, shape, F32))
            with ExitStack() as turn:
                m["kc"] = turn.enter_context(nc.sbuf_tensor("kc", [P, DEC_B, P], F32))
            m["st"] = mixers.enter_context(nc.sbuf_tensor("st", [P, 5, 2, BV], F32))
            for variant in ([("hrow", [P, 3, D])],
                            [("ropet", [P, 10, 2 * ROPE]), ("so", [P, 2, P]), ("sm", [P, AH, 256]),
                             ("pT", [P, AH, 2, P])],
                            [("qsz", [P, BH, DEC_B, SAMP]), ("vblk", [SAMP, DEC_B, BV]), ("yb", [P, 3, 512]),
                             ("sga", [P, 2, NT])]):
                with ExitStack() as turn:
                    for name, shape in variant:
                        m[name] = turn.enter_context(nc.sbuf_tensor(name, shape, F32))
        (qkv, qT, kz, kTs, kcT, vc, sinkb, sinkr, sinkt, soft, softs, qs, qzs, pss, pz, pnT, ya, vb, gate, gnb, wgu,
         lrT, eb, bcum, kt, ket, qh, atm, ats, ke, s0, oss) = (m[k] for k, _ in mixer)
        kc, st, hrow, ropet, so, sm, pT, qsz, vblk, yb, sga = (m[k] for k in (
            "kc", "st", "hrow", "ropet", "so", "sm", "pT", "qsz", "vblk", "yb", "sga"))
        h2hi = sb("h2hi", [P, 3, D], F32R)
        h2lo = sb("h2lo", [P, 3, D], F32R)
        h2 = sb("h2", [P, 2, D])
        h2c = sb("h2c", [P, D])
        keys = sb("keys", [P, PH, P])
        kbd = sb("kbd", [P, PH, 2 * PK])
        qp = sb("qp", [P, PH, NO])
        sc = sb("sc", [P, 3, PH, 2 * PK])
        gfin = sb("gfin", [P, D])
        less = sb("less", [P, 2, PK])
        sv = sb("sv", [P, 2, TOPK])
        si = sb("si", [P, 2, 2, TOPK], U32)
        sif = sb("sif", [P, 2, TOPK])
        cand = sb("cand", [P, TOPK * TOPK])
        cand2 = sb("cand2", [P, TOPK * TOPK])
        fv = sb("fv", [P, PH, TOPK])
        fpos = sb("fpos", [P, 2, TOPK], U32)
        fij = sb("fij", [P, 2, TOPK], U32)
        fijf = sb("fijf", [P, 2, TOPK])
        pick = sb("pick", [P, 2, TOPK, TOPK])
        eij = sb("eij", [P, 2, TOPK])
        turned_s = sb("turned_s", [P, SAMP])
        route = sb("route", [P, 2, PH, TOPK])
        wsum = sb("wsum", [P, 2, PH])
        idxT = sb("idxT", [P, NO], I32)
        wT = sb("wT", [P, NO])

        h2hold = [h2[:, 0, :], h2[:, 1, :], h2c[:, :]]

        def C_(name):
            at, w = CST_AT[name]
            return cst[:, at:at + w]

        ident = C_("ident")

        x_in = [sem(f"x_in{t}") for t in TILES]
        ident_landed, cst_landed = sem("ident_landed"), sem("cst_landed")
        gains_landed = sem("gains_landed")
        small_landed = sem("small_landed")
        cache_landed = sem("cache_landed")
        unit_landed = [sem(f"unit_landed{s}") for s in range(RING)]
        router_landed = sem("router_landed")
        mixer_out = sem("mixer_out")
        cache_copied = sem("cache_copied")
        y_out = [sem(f"y_out{i}") for i in range(3)]
        uv_landed = [sem(f"uv_landed{s}") for s in range(NS)]
        filled = sem("bank_filled")
        drained = {"v": sem("bank_drained_v"), "a": sem("bank_drained_a")}
        v_step = sem("v_step")
        a_step = sem("a_step")
        zeroed = sem("zeroed")
        ssq_done, mean_done, root_done, rows_normed = (sem(k) for k in ("ssq_done", "mean_done", "root_done",
                                                                        "rows_normed"))
        roped = sem("roped")
        ld_abs, ld_log, b_ready, b_exp, last_ready, ket_exp = (sem(k) for k in ("ld_abs", "ld_log", "b_ready",
                                                                                "b_exp", "last_ready", "ket_exp"))
        gate_sig = sem("gate_sig")
        max_ready, probs_ready = sem("max_ready"), sem("probs_ready")
        qs_ready, smax_ready, sprobs_ready = sem("qs_ready"), sem("smax_ready"), sem("sprobs_ready")
        states_ready = sem("states_ready")
        o_squared, o_mean, o_root, yb_ready = sem("o_squared"), sem("o_mean"), sem("o_root"), sem("yb_ready")
        qsz_ready, vblk_ready, sstate_ready = sem("qsz_ready"), sem("vblk_ready"), sem("sstate_ready")
        merged = sem("merged")
        x2_ready = sem("x2_ready")
        h2_high, h2_split = sem("h2_high"), sem("h2_split")
        kbd_ready = sem("kbd_ready")
        fv_ready, w_exp, routed = sem("fv_ready"), sem("w_exp"), sem("routed")
        lists_turned, listed, weights_listed = sem("lists_turned"), sem("listed"), sem("weights_listed")
        idx_copied, onehot_ready = sem("idx_copied"), sem("onehot_ready")
        spread, dotted, factored, wz_ready, combined = (sem(k) for k in ("spread", "dotted", "factored", "wz_ready",
                                                                       "combined"))
        acc_read = sem("acc_read")
        pool_turn = sem("pool_turn")
        fin_ssq, fin_mean, fin_root, y_ready = (sem(k) for k in ("fin_ssq", "fin_mean", "fin_root", "y_ready"))

        N_SMALL_IN, N_CACHE_IN, N_MIX_OUT = 4, 4, 8

        def take(eng, job):
            eng.wait_ge(filled, AT[job] + 1)
            return ps[:, AT[job] % 8, :]

        def release(ins, job):
            ins.then_inc(drained[DRAINER[job]], 1)

        def need(eng, *names):
            for name in names:
                eng.wait_ge(drained[DRAINER[name]], ORDINAL[name])

        w_in_v = w_in[0].rearrange("(k p) n -> p k n", p=P)

        def slot(unit, k):
            s = UNIT_AT[unit] % RING
            return ring[:, s, :].rearrange("p (k n) -> p k n", k=k)

        def unit_dmas(unit):
            full = slot(unit, KT)
            if unit == "kv":
                return [(full[:, :, 0:256], w_in_v[:, :, K0:K0 + 256]),
                        (full[:, :, 256:256 + RANK], w_in_v[:, :, LR0:LR0 + RANK])]
            if unit in ("q", "vb", "gb", "qkb"):
                at = dict(q=Q0, vb=VB0, gb=GB0, qkb=QB0)[unit]
                return [(full, w_in_v[:, :, at:at + 512])]
            n = int(unit[-1])
            if unit.startswith("gates"):
                return [(full[:, :, 0:256], w_in_v[:, :, GA0 + 256 * n:GA0 + 256 * n + 256]),
                        (full[:, :, 256:512], w_in_v[:, :, GR0 + 256 * n:GR0 + 256 * n + 256])]
            if unit.startswith("branch"):
                wav = w_a[0].rearrange("(g j d) n -> g d j n", g=AKV, j=AG)
                cols = slice(256 * n, 256 * n + 256)
                return [(full[0:AD, 0:4, 0:256], wav[0, :, :, cols]), (full[AD:P, 0:4, 0:256], wav[1, :, :, cols]),
                        (full[:, 4:8, 0:256], w_b[0].rearrange("(h e) n -> e h n", h=BH)[:, :, cols])]
            w = w_out if unit.startswith("wo") else w_pq
            return [(full, w[0].rearrange("(k p) n -> p k n", p=P)[:, :, 512 * n:512 * n + 512])]

        landed_at, total = {}, [0] * RING
        for name, _ in UNITS:
            total[UNIT_AT[name] % RING] += 16 * len(unit_dmas(name))
            landed_at[name] = total[UNIT_AT[name] % RING]

        def unit_ready(eng, unit):
            eng.wait_ge(unit_landed[UNIT_AT[unit] % RING], landed_at[unit])

        def held(eng, value):
            return value if isinstance(value, int) else eng.snap(value)

        block = ctx.enter_context(nc.Block())

        @block.sync
        def _(sp):
            for dst, src in ((gvec[0:8, :], g_mix[0].rearrange("(k p) -> k p", p=P)),
                             (gvec[8:16, :], g_ffn[0].rearrange("(k p) -> k p", p=P)),
                             (gvec[16:18, :], b_gate[0].rearrange("(k p) -> k p", p=P))):
                sp.dma_start(dst, src).then_inc(gains_landed, 16)
            sp.dma_start(x[:, A, :], x_prompt[0, 0:128, :]).then_inc(x_in[A], 16)
            sp.dma_start(x[:, B, :], x_prompt[0, 128:256, :]).then_inc(x_in[B], 16)
            sp.dma_start(x[0:SAMP, C, :], x_sample.rearrange("b t d -> (b t) d")).then_inc(x_in[C], 16)
            sp.dma_start(x[SAMP:SAMP + META, C, :], meta_tokens).then_inc(x_in[C], 16)
            for n, (unit, _) in enumerate(UNITS):
                if n >= RING:
                    sp.wait_ge(filled, AT[UNITS[n - RING][1]] + 1)
                for dst, src in unit_dmas(unit):
                    sp.dma_start(dst, src).then_inc(unit_landed[n % RING], 16)
                if unit == "gates0":
                    sp.wait_ge(roped, 3)
                    need(sp, "kv0", "kv1", "kv2")
                    for c0, prompt, sample in ((512, nk_prompt, nk_sample), (640, nv_prompt, nv_sample)):
                        sp.dma_start(prompt[0, 0].rearrange("s g d -> s (g d)"),
                                     qkv[:, B, c0:c0 + P]).then_inc(mixer_out, 16)
                        sp.dma_start(sample[0, :, WINDOW - DEC_T:WINDOW].rearrange("b t g d -> b t (g d)"),
                                     qkv[0:SAMP, C, c0:c0 + P]).then_inc(mixer_out, 16)
                if unit == "wo1":
                    sp.wait_ge(states_ready, 4 * 5)
                    for p in range(2):
                        sp.dma_start(ns_prompt[0, 0, 2 * p:2 * p + 2].rearrange("h d e -> (h d) e"),
                                     st[:, 4, p, :]).then_inc(mixer_out, 16)
                    need(sp, "us3.1")
                    for p in range(2):
                        sp.dma_start(ns_sample[0, :, 2 * p:2 * p + 2].rearrange("b h d e -> (h d) b e"),
                                     s0[:, p]).then_inc(mixer_out, 16)
            sp.wait_ge(mixer_out, 16 * N_MIX_OUT)
            sp.wait_ge(merged, KT)
            sp.dma_start(keys[:, :, :].rearrange("n h (c d) -> n h c d", c=2),
                         sub_keys[0].rearrange("h c n d -> n h c d")).then_inc(router_landed, 16)
            sp.dma_start(gfin[:, :], g_final.rearrange("(o d) -> o d", o=1).broadcast_to([P, D])
                         ).then_inc(router_landed, 16)
            for i, t in enumerate(ORDER):
                sp.wait_ge(y_ready, i + 1)
                dst = y_sample.rearrange("b t d -> (b t) d") if t == C else y_prompt[0, 128 * t:128 * t + 128, :]
                sp.dma_start(dst, h2[0:OUTS[t], i % 2, :]).then_inc(y_out[i], 16)
            for i in range(3):
                sp.wait_ge(y_out[i], 16)
            sp.wait_ge(cache_copied, 16 * 2)

        @block.gpsimd
        def _(pool):
            pool.dma_start(cst[:, 0:P], cst_in[:, 0:P]).then_inc(ident_landed, 16)
            pool.dma_start(cst[:, P:CST_COLS], cst_in[:, P:CST_COLS]).then_inc(cst_landed, 16)
            for dst, src in ((wgu[:, :], w_gate_up[0]),
                             (sinkb[:, :], sinks[0:1, :].broadcast_to([P, AH])),
                             (gnb[:, :], g_gla[0:1, :].broadcast_to([P, BV])),
                             (gffn[:, :], g_ffn[0:1, :].broadcast_to([P, D]))):
                pool.dma_start(dst, src).then_inc(small_landed, 16)
            for dst, src in ((kc[:, :, :], cache_k[0].rearrange("b s g d -> s b (g d)")),
                             (vc[:, :, :], cache_v[0].rearrange("b s g d -> s b (g d)")),
                             (s0[:, 0], state_gla[0, :, 0:2].rearrange("b h d e -> (h d) b e")),
                             (s0[:, 1], state_gla[0, :, 2:4].rearrange("b h d e -> (h d) b e"))):
                pool.dma_start(dst, src).then_inc(cache_landed, 16)
            for cache, out in ((cache_k, nk_sample), (cache_v, nv_sample)):
                pool.dma_start(out[0, :, 0:WINDOW - DEC_T].rearrange("b s g d -> b (s g d)"),
                               cache[0, :, DEC_T:WINDOW].rearrange("b s g d -> b (s g d)")
                               ).then_inc(cache_copied, 16)
            for buf in (kz, qh, qs, qzs, pz, atm, ats):
                pool.memset(buf[:], 0.0).then_inc(zeroed, 1)
            pool.wait_ge(mixer_out, 16 * N_MIX_OUT)
            pool.wait_ge(merged, KT)
            pool.memset(kbd[:, :, :], 0.0).then_inc(zeroed, 1)

            def token(first_use, tk, col, row, s):
                now, back = held(pool, tk + 1), held(pool, tk - (NS - 1))
                if not first_use:
                    pool.wait_ge(uv_landed[s], 16 * ((tk - s) // NS))
                    pool.wait_ge(spread, back)
                pool.tensor_copy(islot[s][:, :], idxT[:, bass.ds(col, 1)]).then_inc(idx_copied, 1)
                pool.tensor_copy(onehot[s][:, :], ident[:, bass.ds(row, 1)].broadcast_to([P, P])
                                 ).then_inc(onehot_ready, 1)
                pool.wait_ge(idx_copied, now)
                if not first_use:
                    pool.wait_ge(combined, back)
                pool.sem_inc(pool_turn, 1)
                pool.indirect_dma_start(uv[:, s, :], None, peer_uv,
                                        bass.IndirectOffsetOnAxis(ap=islot[s][:, 0:1], axis=0)
                                        ).then_inc(uv_landed[s], 16)

            for i, t in enumerate(ORDER):
                r = OUTS[t]
                pool.wait_ge(rows_normed, 3 + i + 1)
                pool.tensor_copy(h2hi[0:r, t, :], h2hold[t][0:r, :]).then_inc(h2_high, 1)
                pool.wait_ge(h2_high, i + 1)
                pool.tensor_tensor(h2lo[0:r, t, :], h2hold[t][0:r, :], h2hi[0:r, t, :].bitcast(F32), ALU.subtract
                                   ).then_inc(h2_split, 1)
            need(pool, f"pq{PH - 1}")
            for i, t in enumerate(ORDER):
                pool.wait_ge(listed, i + 1)
                g0 = 0
                if i == 0:
                    for s in range(NS):
                        token(True, s, COL[t] + s, s, s)
                    g0 = 1
                with pool.Fori(g0, OUTS[t] // NS) as g:
                    for s in range(NS):
                        token(False, (GROUP0[t] + g) * NS + s, g * NS + (COL[t] + s), g * NS + s, s)

        @block.tensor
        def _(pe):
            def open_(job):
                assert AT[job] == pe_at[0], (job, JOBS[pe_at[0]])
                pe_at[0] += 1
                if AT[job] >= 8:
                    need(pe, JOBS[AT[job] - 8][0])
                return ps[:, AT[job] % 8, :]

            pe_at = [0]

            def close(ins):
                ins.then_inc(filled, 1)

            pe.wait_ge(ident_landed, 16)
            pe.wait_ge(gains_landed, 16 * 3)
            bank = open_("gvecT")
            close(pe.transpose(bank[:, 0:18], gvec[:, :], ident[0:18, 0:18]))
            for t in TILES:
                pe.wait_ge(rows_normed, t + 1)
                r = ROWS[t]
                for half in range(2):
                    bank = open_(f"hT{t}.{half}").rearrange("p (k r) -> p k r", k=4)
                    for k in range(4):
                        c0 = (4 * half + k) * P
                        ins = pe.transpose(bank[:, k, 0:r], hrow[0:r, t, c0:c0 + P], ident[0:r, 0:r])
                    close(ins)

            def rows_of(unit, job, t, c0, n):
                bank, r, w = open_(job), ROWS[t], slot(unit, KT)
                for k in range(KT):
                    ins = pe.matmul(bank[0:r, 0:n], hT[:, k, COL[t]:COL[t] + r], w[:, k, c0:c0 + n],
                                    start=(k == 0), stop=(k == KT - 1))
                close(ins)

            def cols_of(unit, job, c0, n, width):
                bank, w = open_(job), slot(unit, KT)
                for k in range(KT):
                    ins = pe.matmul(bank[0:n, 0:width], w[:, k, c0:c0 + n], hT[:, k, 0:width],
                                    start=(k == 0), stop=(k == KT - 1))
                close(ins)

            unit_ready(pe, "q")
            for t in TILES:
                need(pe, f"hT{t}.1")
                rows_of("q", f"q{t}", t, 0, 512)
            unit_ready(pe, "kv")
            for t in TILES:
                rows_of("kv", f"kv{t}", t, 0, 256)
            cols_of("kv", "lrT", 256, RANK, NT)
            pe.wait_ge(small_landed, 16 * N_SMALL_IN)
            for p in range(2):
                bank = open_(f"ld{p}")
                need(pe, "lrT")
                close(pe.matmul(bank[:, 0:NT], wgu[:, p * P:p * P + P], lrT[:, :], start=True, stop=True))
            unit_ready(pe, "vb")
            for t in TILES:
                rows_of("vb", f"vb{t}", t, 0, 512)
            for t in TILES:
                bank, r = open_(f"kT{t}"), ROWS[t]
                pe.wait_ge(roped, t + 1)
                close(pe.transpose(bank[:, 0:r], qkv[0:r, t, 512:640], ident[0:r, 0:r]))
            for t in TILES:
                bank, r = open_(f"qT{t}").rearrange("p (j r) -> p j r", j=AG), ROWS[t]
                for j in range(AG):
                    ins = pe.transpose(bank[:, j, 0:r], qkv[0:r, t, j * P:j * P + P], ident[0:r, 0:r])
                close(ins)
            unit_ready(pe, "gb")
            for t in TILES:
                rows_of("gb", f"gb{t}", t, 0, 512)
            unit_ready(pe, "qkb")
            for p in range(2):
                cols_of("qkb", f"kb{p}", 256 + p * P, P, NT)
            for p in range(2):
                cols_of("qkb", f"qb{p}", p * P, P, NT)

            def scores(t):
                width = 176 if t == A else 256
                need(pe, f"qT{t}", "kT2")
                for j in range(AG):
                    bank = open_(f"sc{'AB'[t]}.{j}").rearrange("p (g k) -> p g k", g=2)
                    for g in range(AKV):
                        lhs = qT[:, j, COL[t]:COL[t] + P]
                        if t == A:
                            pe.matmul(bank[:, g, 0:128], lhs, kz[:, g, 0:128], start=True, stop=True)
                            ins = pe.matmul(bank[:, g, 128:width], lhs, kz[:, g, 256:304], start=True, stop=True)
                        else:
                            ins = pe.matmul(bank[:, g, :], lhs, kz[:, g, 0:256], start=True, stop=True)
                    close(ins)

            def attend(t):
                pe.wait_ge(probs_ready, t + 1)
                for i in range(4):
                    bank = open_(f"pT{'AB'[t]}.{i}").rearrange("p (h c q) -> p h c q", h=2, c=2)
                    for hh in range(2):
                        row = sm[:, 2 * i + hh, :]
                        pe.transpose(bank[:, hh, 0, :], row[:, 0:128], ident)
                        n = 48 if t == A else 128
                        ins = pe.transpose(bank[0:n, hh, 1, :], row[:, 128:128 + n], ident)
                    close(ins)
                bank = open_(f"pv{'AB'[t]}")
                need(pe, f"pT{'AB'[t]}.3", "kv2")
                for h in range(AH):
                    c0 = 640 + (h // AG) * AD
                    first, second = (A, C) if t == A else (A, B)
                    n = ROWS[second]
                    pe.matmul(bank[:, h * AD:h * AD + AD], pT[:, h, 0, :], qkv[:, first, c0:c0 + AD],
                              start=True, stop=False)
                    ins = pe.matmul(bank[:, h * AD:h * AD + AD], pT[0:n, h, 1, :], qkv[0:n, second, c0:c0 + AD],
                                    start=False, stop=True)
                close(ins)
                bank = open_(f"yaT{t}").rearrange("p (j r) -> p j r", j=AG)
                need(pe, f"pv{'AB'[t]}")
                for j in range(AG):
                    ins = pe.transpose(bank[:, j, :], ya[:, j * P:j * P + P], ident)
                close(ins)

            scores(A)
            pe.wait_ge(cache_landed, 16 * N_CACHE_IN)
            for i in range(2):
                bank = open_(f"kcT{i}").rearrange("p (b s) -> p b s", b=4)
                for b in range(4):
                    ins = pe.transpose(bank[:, b, :], kc[:, 4 * i + b, :], ident)
                close(ins)
            need(pe, "kcT1")
            pe.wait_ge(qs_ready, 1)
            for grp in range(2):
                bank = open_(f"ss{grp}")
                for b in range(4):
                    pe.matmul(bank[:, 0:WINDOW], qzs[:, 4 * grp + b, :], kcT[:, 4 * grp + b, :],
                              start=(b == 0), stop=(b == 3))
                close(pe.matmul(bank[:, WINDOW:160], qs[:, grp, :], kTs[:, :], start=True, stop=True))
            attend(A)
            scores(B)
            pe.wait_ge(sprobs_ready, 1)
            for grp in range(2):
                bank = open_(f"spT{grp}")
                pe.transpose(bank[:, 0:P], pss[:, grp, 0:WINDOW], ident)
                close(pe.transpose(bank[0:SAMP, P:2 * P], pss[:, grp, WINDOW:160], ident))
            for grp in range(2):
                bank = open_(f"spv{grp}")
                need(pe, f"spT{grp}")
                for b in range(4):
                    pe.matmul(bank[:, 0:P], pz[:, grp, b * P:b * P + P], vc[:, 4 * grp + b, :],
                              start=(b == 0), stop=False)
                close(pe.matmul(bank[:, 0:P], pnT[:, grp, :], qkv[0:SAMP, C, 640:768], start=False, stop=True))
            for grp in range(2):
                bank = open_(f"soT{grp}")
                need(pe, f"spv{grp}")
                close(pe.transpose(bank[:, 0:P], so[:, grp, :], ident))
            attend(B)

            for t in TILES:
                bank, r = open_(f"keT{t}").rearrange("p (c d) -> p c d", c=4), ROWS[t]
                need(pe, "kb1")
                for p in range(2):
                    ins = pe.transpose(bank[0:r, p, :], ket[:, p, COL[t]:COL[t] + r], ident)
                close(ins)
            for t in TILES:
                r = OUTS[t]
                bank = open_(f"AT{t}")
                need(pe, "qb1")
                for h in range(BH):
                    ins = pe.matmul(bank[0:r, h * r:h * r + r], kt[:, h // 2, COL[t]:COL[t] + r],
                                    qh[:, h, COL[t]:COL[t] + r], start=True, stop=True)
                close(ins)
            chunks = [(C, SAMP, META), (A, 0, CHUNK), (A, CHUNK, CHUNK), (B, 0, CHUNK), (B, CHUNK, CHUNK)]
            need(pe, "keT2", "vb2")
            for n, (t, r0, r) in enumerate(chunks):
                bank = open_(f"up{n}")
                for p in range(2):
                    ins = pe.matmul(bank[:, p * 256:p * 256 + 256], ke[r0:r0 + r, t, p, :],
                                    vb[r0:r0 + r, t, p * 256:p * 256 + 256], start=True, stop=True)
                close(ins)
            for t in (A, B):
                bank = open_(f"o{t}")
                need(pe, f"AT{t}")
                pe.wait_ge(states_ready, 4 * (2 * t + 2))
                for h in range(BH):
                    cols = slice(h * BV, h * BV + BV)
                    pe.matmul(bank[:, cols], atm[:, t, h, :], vb[:, t, cols], start=True, stop=False)
                    for c in range(2):
                        r0 = c * CHUNK
                        ins = pe.matmul(bank[r0:r0 + CHUNK, cols], qh[:, h, COL[t] + r0:COL[t] + r0 + CHUNK],
                                        st[:, 2 * t + c, h // 2, :], start=False, stop=True)
                close(ins)
            bank = open_("o2")
            need(pe, "AT2")
            pe.wait_ge(qsz_ready, 1)
            for h in range(BH):
                cols = slice(h * BV, h * BV + BV)
                pe.matmul(bank[0:SAMP, cols], ats[:, h, :], vb[0:SAMP, C, cols], start=True, stop=False)
                for b in range(DEC_B):
                    ins = pe.matmul(bank[0:SAMP, cols], qsz[:, h, b, :], s0[:, h // 2, b, :],
                                    start=False, stop=(b == DEC_B - 1))
            close(ins)
            for t in TILES:
                bank, r = open_(f"ybT{t}").rearrange("p (j r) -> p j r", j=BH), OUTS[t]
                pe.wait_ge(yb_ready, t + 1)
                for h in range(BH):
                    ins = pe.transpose(bank[:, h, 0:r], yb[0:r, t, h * BV:h * BV + BV], ident[0:r, 0:r])
                close(ins)
            for h in range(BH):
                pe.wait_ge(vblk_ready, h + 1)
                for i in range(2):
                    bank = open_(f"us{h}.{i}")
                    close(pe.matmul(bank, ke[0:SAMP, C, h // 2, :], vblk[:, 4 * i:4 * i + 4, :],
                                    start=True, stop=True))

            need(pe, "yaT1", "soT1", "ybT2")
            for mt in range(KT):
                n, c0 = mt // 2, (mt % 2) * P
                unit_ready(pe, f"gates{n}")
                cols_of(f"gates{n}", f"ga{mt}", c0, P, NO)
                unit_ready(pe, f"branch{n}")
                w = slot(f"branch{n}", KT)
                bank = open_(f"za{mt}")
                for j in range(AG):
                    ins = pe.matmul(bank[:, 0:NO], w[:, j, c0:c0 + P], yaT[:, j, 0:NO], start=(j == 0), stop=(j == 3))
                close(ins)
                cols_of(f"gates{n}", f"gr{mt}", 256 + c0, P, NO)
                bank = open_(f"zb{mt}")
                for j in range(BH):
                    ins = pe.matmul(bank[:, 0:NO], w[:, 4 + j, c0:c0 + P], ybT[:, j, 0:NO],
                                    start=(j == 0), stop=(j == 3))
                close(ins)
            pe.wait_ge(merged, KT)
            for n in range(2):
                unit_ready(pe, f"wo{n}")
                w = slot(f"wo{n}", KT)
                for t in ORDER:
                    bank, r = open_(f"wo{n}.{t}"), OUTS[t]
                    for k in range(KT):
                        ins = pe.matmul(bank[0:r, :], mT[:, k, COL[t]:COL[t] + r], w[:, k, :],
                                        start=(k == 0), stop=(k == KT - 1))
                    close(ins)

            pe.wait_ge(router_landed, 16 * 2)
            for i in range(2):
                bank = open_(f"kk{i}").rearrange("p (h n) -> p h n", h=4)
                for h in range(4):
                    ins = pe.transpose(bank[:, h, :], keys[:, 4 * i + h, :], ident)
                close(ins)

            def turn_rows(i, t):
                pe.wait_ge(rows_normed, 3 + i + 1)
                r = OUTS[t]
                for half in range(2):
                    bank = open_(f"h2T{t}.{half}").rearrange("p (k r) -> p k r", k=4)
                    for k in range(4):
                        c0 = (4 * half + k) * P
                        ins = pe.transpose(bank[:, k, 0:r], h2hold[t][0:r, c0:c0 + P], ident[0:r, 0:r])
                    close(ins)

            turn_rows(0, C)
            need(pe, f"h2T{C}.1")
            bank = open_("pqs").rearrange("p (h r) -> p h r", r=SAMP)[:, 0:PH]
            for h in range(PH):
                unit_ready(pe, f"wq{h // 4}")
                w = slot(f"wq{h // 4}", KT)
                for k in range(KT):
                    ins = pe.matmul(bank[:, h, :], w[:, k, (h % 4) * P:(h % 4) * P + P], hT[:, k, 256:NO],
                                    start=(k == 0), stop=(k == KT - 1))
            close(ins)
            need(pe, "pqs")
            pe.wait_ge(kbd_ready, 1)
            bank = open_("pss").rearrange("p (h n) -> p h n", h=2)
            for h in range(PH):
                ins = pe.matmul(bank[32 * (h // 2):32 * (h // 2) + 32, h % 2, :], qp[:, h, 256:NO], kbd[:, h, :],
                                start=True, stop=True)
            close(ins)
            for i, t in ((1, A), (2, B)):
                turn_rows(i, t)
            need(pe, f"h2T{B}.1")
            for h in range(PH):
                cols_of(f"wq{h // 4}", f"pq{h}", (h % 4) * P, P, 256)
            need(pe, "pq7")
            for t in (A, B):
                for i in range(4):
                    bank = open_(f"ps{t}.{i}")
                    for hh in range(2):
                        h = 2 * i + hh
                        ins = pe.matmul(bank[:, hh * 256:hh * 256 + 256], qp[:, h, COL[t]:COL[t] + P], kbd[:, h, :],
                                        start=True, stop=True)
                    close(ins)

            def turn_lists(i):
                pe.wait_ge(routed, i + 1)
                if i == 2:
                    pe.wait_ge(acc_read, 1)
                bank = ps[:, LIST_BANK[i], :].rearrange("p (a r) -> p a r", a=4)
                for a in range(2):
                    ins = pe.transpose(bank[:, a, :], route[:, a].rearrange("r h k -> r (h k)"), ident)
                ins.then_inc(lists_turned, 1)

            need(pe, DRAINS["v"][-1], DRAINS["a"][-1])
            pe.wait_ge(h2_split, 3)

            def spread_row(t, tk, s, free):
                r = OUTS[t]
                pe.wait_ge(onehot_ready, tk + 1)
                if free:
                    pe.wait_ge(dotted, tk - 1)
                for n in range(2):
                    cols = slice(512 * n, 512 * n + 512)
                    out = ps[:, 2 * (s % 2) + n, :]
                    pe.matmul(out, onehot[s][0:r, :], h2hi[0:r, t, cols], start=True, stop=False)
                    ins = pe.matmul(out, onehot[s][0:r, :], h2lo[0:r, t, cols], start=False, stop=True)
                ins.then_inc(spread, 1)

            def combine(i, tk, g, s, first, last):
                pe.wait_ge(wz_ready, tk + 1)
                pe.wait_ge(uv_landed[s], 16 * (g + 1))
                for n in range(2):
                    ins = pe.matmul(ps[:, SUM_BANK[i] + n, :], wz[s][:, :], uv[:, s, D + 512 * n:D + 512 * n + 512],
                                    start=first, stop=last, skip_group_check=True)
                ins.then_inc(combined, 1)

            for i, t in enumerate(ORDER):
                groups = OUTS[t] // NS

                def group(g, first=False, last=False, turn=False):
                    tk = (GROUP0[t] + g) * NS
                    for s in range(NS):
                        if not (last and s >= NS - 2):
                            spread_row(t, tk + s + 2, (s + 2) % NS, True)
                        elif i < 2:
                            spread_row(ORDER[i + 1], tk + s + 2, (s + 2) % NS, True)
                        combine(i, tk + s, GROUP0[t] + g, s, first and s == 0, last and s == NS - 1)
                        if turn and s == 0:
                            turn_lists(i + 1)

                if i == 0:
                    for s in range(2):
                        spread_row(t, s, s, False)
                else:
                    pe.wait_ge(weights_listed, i + 1)
                group(0, first=True)
                if LIST_AHEAD[i]:
                    with pe.Fori(1, groups - LIST_AHEAD[i]) as g:
                        group(g)
                    group(groups - LIST_AHEAD[i], turn=True)
                rest = groups - LIST_AHEAD[i] + 1 if LIST_AHEAD[i] else 1
                if rest < groups - 1:
                    with pe.Fori(rest, groups - 1) as g:
                        group(g)
                group(groups - 1, last=True)

        @block.scalar
        def _(act):
            def drains(job):
                assert DRAINS["a"][a_at[0]] == job, (job, DRAINS["a"][a_at[0]])
                a_at[0] += 1
                return take(act, job)

            a_at, junk = [0], mT[:, 0:4, 0:256]

            def copy(out, in_, job):
                release(act.activation(out, in_, ACT.Copy), job)

            for t in TILES:
                act.wait_ge(x_in[t], 32 if t == C else 16)
                r = ROWS[t]
                if t:
                    act.wait_ge(ssq_done, t)
                act.activation(junk[0:r], x[0:r, t, :].rearrange("p (a b) -> p a b", a=4), ACT.Square,
                               accum_out=stat[0:r, t, 0:1]).then_inc(ssq_done, 1)
            for t in TILES:
                act.wait_ge(mean_done, t + 1)
                act.activation(stat[0:ROWS[t], t, 2:3], stat[0:ROWS[t], t, 1:2], ACT.Sqrt).then_inc(root_done, 1)
            for t in TILES:
                r = ROWS[t]
                bank = drains(f"q{t}")[0:r, :].rearrange("r (g j d) -> r g j d", g=AKV, j=AG)
                copy(qkv[0:r, t, 0:512].rearrange("r (j g d) -> r g j d", g=AKV, j=AG), bank, f"q{t}")
            for t in TILES:
                r = ROWS[t]
                copy(qkv[0:r, t, 512:768], drains(f"kv{t}")[0:r, 0:256], f"kv{t}")
            act.wait_ge(ld_abs, 1)
            act.activation(bcum[:, :, :], kt[:, :, :], ACT.Exp, scale=-1.0).then_inc(a_step, 1)
            act.wait_ge(a_step, 1)
            act.activation(bcum[:, :, :], bcum[:, :, :], ACT.Ln, bias=1.0).then_inc(ld_log, 1)
            for t in TILES:
                r = ROWS[t]
                copy(vb[0:r, t, :], drains(f"vb{t}")[0:r, :], f"vb{t}")
            act.wait_ge(b_ready, 1)
            act.activation(eb[:, :, :], bcum[:, :, :], ACT.Exp).then_inc(b_exp, 1)
            act.activation(kt[:, :, :], bcum[:, :, :], ACT.Exp, scale=-1.0).then_inc(b_exp, 1)
            act.wait_ge(last_ready, 3)
            act.activation(ket[:, :, :], ket[:, :, :], ACT.Exp).then_inc(ket_exp, 1)
            for t in TILES:
                r = ROWS[t]
                bank = drains(f"qT{t}").rearrange("p (j r) -> p j r", j=AG)
                copy(qT[:, :, COL[t]:COL[t] + r], bank[:, :, 0:r], f"qT{t}")
            for t in TILES:
                r = OUTS[t]
                bank = take(act, f"gb{t}")
                act.activation(gate[0:r, t, :], bank[0:r, :], ACT.Sigmoid).then_inc(gate_sig, 1)

            def probs(i, width):
                act.wait_ge(max_ready, i + 1)
                for h in range(AH):
                    act.activation(sm[:, h, 0:width], sm[:, h, 0:width], ACT.Exp, bias=soft[:, 1, h:h + 1],
                                   accum_out=soft[:, 3, h:h + 1])
                act.activation(soft[:, 4, :], soft[:, 2, :], ACT.Exp).then_inc(probs_ready, 1)

            def turn(t):
                for i in range(4):
                    job = f"pT{'AB'[t]}.{i}"
                    bank = drains(job).rearrange("p (h c q) -> p h c q", h=2, c=2)
                    if t == A:
                        act.activation(pT[:, 2 * i:2 * i + 2, 0, :], bank[:, :, 0, :], ACT.Copy)
                        copy(pT[0:48, 2 * i:2 * i + 2, 1, :], bank[0:48, :, 1, :], job)
                    else:
                        copy(pT[:, 2 * i:2 * i + 2], bank, job)
                job = f"yaT{t}"
                bank = drains(job).rearrange("p (j r) -> p j r", j=AG)
                copy(yaT[:, :, COL[t]:COL[t] + P], bank, job)

            for i in range(2):
                job = f"kcT{i}"
                bank = drains(job).rearrange("p (b s) -> p b s", b=4)
                copy(kcT[:, 4 * i:4 * i + 4, :], bank, job)
            probs(0, 176)
            act.wait_ge(smax_ready, 1)
            for grp in range(2):
                act.activation(pss[:, grp, :], pss[:, grp, :], ACT.Exp, bias=softs[:, 1, grp:grp + 1],
                               accum_out=softs[:, 3, grp:grp + 1])
            act.activation(softs[:, 4, :], softs[:, 2, :], ACT.Exp).then_inc(sprobs_ready, 1)
            turn(A)
            probs(1, 256)
            turn(B)
            for t in TILES:
                job, r = f"keT{t}", ROWS[t]
                bank = drains(job).rearrange("p (c d) -> p c d", c=4)
                copy(ke[0:r, t], bank[0:r, 0:2, :], job)
            for t in TILES:
                r, bank = OUTS[t], take(act, f"o{t}")
                if t:
                    act.wait_ge(o_squared, t)
                for h in range(BH):
                    ins = act.activation(junk[0:r, h, 0:BV], bank[0:r, h * BV:h * BV + BV], ACT.Square,
                                         accum_out=oss[0:r, t, 0, h:h + 1])
                ins.then_inc(o_squared, 1)
                act.wait_ge(o_mean, t + 1)
                act.activation(oss[0:r, t, 2, :], oss[0:r, t, 1, :], ACT.Sqrt).then_inc(o_root, 1)
            for t in TILES:
                job, r = f"ybT{t}", OUTS[t]
                bank = drains(job).rearrange("p (j r) -> p j r", j=BH)
                copy(ybT[:, :, COL[t]:COL[t] + r], bank[:, :, 0:r], job)
            for mt in range(KT):
                for i, job in enumerate((f"ga{mt}", f"gr{mt}")):
                    bank = drains(job)
                    if mt:
                        act.wait_ge(merged, mt)
                    elif i == 0:
                        need(act, "ybT2")
                    release(act.activation(sga[:, i, 0:NO], bank[:, 0:NO], ACT.Sigmoid), job)
            for i, t in enumerate(ORDER):
                act.wait_ge(x2_ready, i + 1)
                if i:
                    act.wait_ge(ssq_done, 3 + i)
                r = OUTS[t]
                act.activation(hT[0:r, 0:4, 0:256], x[0:r, t, :].rearrange("p (a b) -> p a b", a=4), ACT.Square,
                               accum_out=stat[0:r, t, 0:1]).then_inc(ssq_done, 1)
            for i, t in enumerate(ORDER):
                r = OUTS[t]
                act.wait_ge(mean_done, 3 + i + 1)
                act.activation(stat[0:r, t, 2:3], stat[0:r, t, 1:2], ACT.Sqrt).then_inc(root_done, 1)
            copy(qp[:, :, 256:NO], drains("pqs").rearrange("p (h r) -> p h r", r=SAMP)[:, 0:PH], "pqs")
            copy(sc[:, C, 0:2].rearrange("r h n -> r (h n)"), drains("pss"), "pss")
            for t in (A, B):
                for half in range(2):
                    job = f"h2T{t}.{half}"
                    bank = drains(job).rearrange("p (k r) -> p k r", k=4)
                    copy(hT[:, 4 * half:4 * half + 4, COL[t]:COL[t] + P], bank, job)
            def list_exp(i, heads):
                act.wait_ge(fv_ready, i + 1)
                act.activation(route[:, 1, 0:heads], route[:, 1, 0:heads], ACT.Exp).then_inc(w_exp, 1)

            for h in range(PH):
                copy(qp[:, h, 0:256], drains(f"pq{h}")[:, 0:256], f"pq{h}")
                if h == PH - 3:
                    list_exp(0, 2)
            for t in (A, B):
                for i in range(4):
                    job = f"ps{t}.{i}"
                    copy(sc[:, t, 2 * i:2 * i + 2].rearrange("r h n -> r (h n)"), drains(job), job)

            spot = C_("spot")

            def weigh_experts(t, g, s, reuse=True):
                tk, row = (GROUP0[t] + g) * NS + s, g * NS + s
                now, back, both = held(act, tk + 1), held(act, tk - (NS - 1)), held(act, 2 * tk + 2)
                place = held(act, 127 - row)
                if reuse:
                    act.wait_ge(combined, back)
                act.activation(wz[s][:, :], spot[:, bass.ds(place, P)], ACT.Copy,
                               scale=wT[:, bass.ds(row + COL[t], 1)]).then_inc(factored, 1)
                act.wait_ge(dotted, now)
                act.activation(acts[:, s:s + 1], dots[:, s:s + 1], ACT.Gelu).then_inc(factored, 1)
                act.wait_ge(factored, both)
                act.activation(wz[s][:, :], wz[s][:, :], ACT.Copy, scale=acts[:, s:s + 1]).then_inc(wz_ready, 1)

            def final_squares(i):
                r, t = OUTS[ORDER[i]], ORDER[i]
                act.wait_ge(acc_read, i + 1)
                act.activation(hT[0:r, 0:4, 0:256], x[0:r, t, :].rearrange("p (a b) -> p a b", a=4), ACT.Square,
                               accum_out=stat[0:r, t, 0:1]).then_inc(fin_ssq, 1)

            def final_root(i):
                r, t = OUTS[ORDER[i]], ORDER[i]
                act.wait_ge(fin_mean, i + 1)
                act.activation(stat[0:r, t, 2:3], stat[0:r, t, 1:2], ACT.Sqrt).then_inc(fin_root, 1)

            for i, t in enumerate(ORDER):
                groups = OUTS[t] // NS
                act.wait_ge(weights_listed, i + 1)
                for s in range(NS):
                    weigh_experts(t, 0, s, reuse=i > 0)
                    if i and s == 1:
                        final_squares(i - 1)
                    if i and s == 2:
                        final_root(i - 1)
                with act.Fori(1, groups - LIST_AHEAD[i]) as g:
                    for s in range(NS):
                        weigh_experts(t, g, s)
                if LIST_AHEAD[i]:
                    list_exp(i + 1, PH)
                    with act.Fori(groups - LIST_AHEAD[i], groups) as g:
                        for s in range(NS):
                            weigh_experts(t, g, s)
            final_squares(2)
            final_root(2)

        @block.vector
        def _(dve):
            links, v_at = [0], [0]

            def link(ins):
                links[0] += 1
                ins.then_inc(v_step, 1)
                dve.wait_ge(v_step, links[0])

            def drains(job):
                assert DRAINS["v"][v_at[0]] == job, (job, DRAINS["v"][v_at[0]])
                v_at[0] += 1
                return take(dve, job)

            def mean(t, r, ssq, done):
                ins = dve.tensor_scalar(stat[0:r, t, 1:2], stat[0:r, t, 0:1], 1.0 / D, EPS, ALU.mult, ALU.add)
                ins.then_inc(done, 1)

            for t in TILES:
                dve.wait_ge(ssq_done, t + 1)
                mean(t, ROWS[t], ssq_done, mean_done)
            for t in TILES:
                r = ROWS[t]
                dve.wait_ge(root_done, t + 1)
                link(dve.reciprocal(stat[0:r, t, 3:4], stat[0:r, t, 2:3]))
                dve.tensor_scalar(hrow[0:r, t, :], x[0:r, t, :], stat[0:r, t, 3:4], None, ALU.mult
                                  ).then_inc(rows_normed, 1)
            bank = drains("gvecT")
            release(dve.tensor_copy(gT[:, :], bank[:, 0:18]), "gvecT")
            need(dve, "gvecT")
            for t in TILES:
                for half in range(2):
                    job, r = f"hT{t}.{half}", ROWS[t]
                    bank = drains(job).rearrange("p (k r) -> p k r", k=4)
                    gain = gT[:, 4 * half:4 * half + 4].unsqueeze(2).broadcast_to([P, 4, r])
                    release(dve.tensor_tensor(hT[:, 4 * half:4 * half + 4, COL[t]:COL[t] + r], bank[:, :, 0:r], gain,
                                              ALU.mult), job)
            dve.wait_ge(cst_landed, 16)
            dve.wait_ge(small_landed, 16 * N_SMALL_IN)

            def rope(t):
                r = ROWS[t]
                need(dve, f"q{t}", f"kv{t}")
                if t:
                    dve.wait_ge(roped, t)
                heads = qkv[0:r, t, 0:640].rearrange("r (h d) -> r h d", d=AD)
                half = ROPE // 2
                cos = C_("cos")[0:r, t * ROPE:t * ROPE + ROPE].unsqueeze(1).broadcast_to([r, 10, ROPE])
                sin = C_("sin")[0:r, t * half:t * half + half].unsqueeze(1).broadcast_to([r, 10, half])
                dve.tensor_tensor(ropet[0:r, :, 0:ROPE], heads[:, :, 0:ROPE], cos, ALU.mult)
                dve.tensor_tensor(ropet[0:r, :, ROPE:ROPE + half], heads[:, :, half:ROPE], sin, ALU.mult)
                link(dve.tensor_tensor(ropet[0:r, :, ROPE + half:2 * ROPE], heads[:, :, 0:half], sin, ALU.mult))
                dve.tensor_tensor(heads[:, :, 0:half], ropet[0:r, :, 0:half], ropet[0:r, :, ROPE:ROPE + half],
                                  ALU.subtract)
                dve.tensor_tensor(heads[:, :, half:ROPE], ropet[0:r, :, half:ROPE],
                                  ropet[0:r, :, ROPE + half:2 * ROPE], ALU.add).then_inc(roped, 1)

            for t in TILES:
                rope(t)
            bank = drains("lrT")
            release(dve.tensor_copy(lrT[:, :], bank[0:RANK, 0:NT]), "lrT")
            for p in range(2):
                bank = drains(f"ld{p}")
                release(dve.tensor_scalar(eb[:, p, :], bank[:, 0:NT], gT[:, 16 + p:17 + p], None, ALU.add), f"ld{p}")
            need(dve, "ld1")
            dve.scalar_tensor_tensor(out=kt[:, :, :], in0=eb[:, :, :], scalar=-1.0, in1=eb[:, :, :], op0=ALU.mult,
                                     op1=ALU.max).then_inc(ld_abs, 1)
            link(dve.tensor_scalar(ket[:, :, :], eb[:, :, :], 0.0, 1.0 / 16, ALU.min, ALU.mult))
            dve.wait_ge(ld_log, 1)
            link(dve.scalar_tensor_tensor(out=ket[:, :, :], in0=bcum[:, :, :], scalar=-1.0 / 16, in1=ket[:, :, :],
                                          op0=ALU.mult, op1=ALU.add))
            for p in range(2):
                ins = dve.tensor_tensor_scan(bcum[:, p, :], C_("reset"), ket[:, p, :], 0.0, ALU.mult, ALU.add)
            ins.then_inc(b_ready, 1)
            dve.wait_ge(b_ready, 1)
            for c0, n, w in ((0, 4, CHUNK), (256, DEC_B, DEC_T), (288, 1, META)):
                b = bcum[:, :, c0:c0 + n * w].rearrange("p a (n w) -> p a n w", w=w)
                out = ket[:, :, c0:c0 + n * w].rearrange("p a (n w) -> p a n w", w=w)
                dve.tensor_tensor(out, b[:, :, :, w - 1:w].broadcast_to([P, 2, n, w]), b, ALU.subtract
                                  ).then_inc(last_ready, 1)

            dve.wait_ge(zeroed, 7)
            for t in TILES:
                job, r = f"kT{t}", ROWS[t]
                bank = drains(job)
                if t == C:
                    dve.tensor_copy(kTs[:, :], bank[:, 0:SAMP])
                dve.tensor_copy(kz[0:AD, 0, COL[t]:COL[t] + r], bank[0:AD, 0:r])
                release(dve.tensor_copy(kz[AD:P, 1, COL[t]:COL[t] + r], bank[AD:P, 0:r]), job)
            for t in TILES:
                job, r = f"gb{t}", ROWS[t]
                bank = drains(job)
                r = OUTS[t]
                dve.wait_ge(gate_sig, t + 1)
                release(dve.tensor_tensor(gate[0:r, t, :], bank[0:r, :], gate[0:r, t, :], ALU.mult), job)
                need(dve, job)
                rows = gate[0:r, t, :].rearrange("r (h e) -> r h e", h=BH)
                dve.tensor_tensor(rows, rows, gnb[0:r, :].unsqueeze(1).broadcast_to([r, BH, BV]), ALU.mult)
            dve.wait_ge(b_exp, 2)
            dve.wait_ge(ket_exp, 1)
            for p in range(2):
                job = f"kb{p}"
                bank = drains(job)
                dve.tensor_tensor(kt[:, p, :], bank[:, 0:NT], kt[:, p, :], ALU.mult)
                release(dve.tensor_tensor(ket[:, p, :], bank[:, 0:NT], ket[:, p, :], ALU.mult), job)
            for p in range(2):
                job = f"qb{p}"
                bank = drains(job)
                for hh in range(2):
                    lanes = slice(hh * BK, hh * BK + BK)
                    ins = dve.scalar_tensor_tensor(out=qh[lanes, 2 * p + hh, :], in0=bank[lanes, 0:NT],
                                                   scalar=BK ** -0.5, in1=eb[lanes, p, :], op0=ALU.mult, op1=ALU.mult)
                release(ins, job)

            def row_max(t):
                width, mask = (176, C_("mask_a")) if t == A else (256, C_("mask_b"))
                for j in range(AG):
                    job = f"sc{'AB'[t]}.{j}"
                    bank = drains(job).rearrange("p (g k) -> p g k", g=2)
                    out = sm[:, :, :].rearrange("p (g j) k -> p j g k", g=2)[:, j, :, 0:width]
                    release(dve.scalar_tensor_tensor(out=out, in0=bank[:, :, 0:width], scalar=AD ** -0.5,
                                                     in1=mask.unsqueeze(1).broadcast_to([P, 2, width]),
                                                     op0=ALU.mult, op1=ALU.add), job)
                need(dve, job)
                link(dve.tensor_reduce(soft[:, 0, :], sm[:, :, 0:width], AX_X, ALU.max))
                link(dve.tensor_tensor(soft[:, 0, :], soft[:, 0, :], sinkb[:, :], ALU.max))
                dve.tensor_scalar(soft[:, 1, :], soft[:, 0, :], -1.0, None, ALU.mult)
                dve.tensor_tensor(soft[:, 2, :], sinkb[:, :], soft[:, 0, :], ALU.subtract).then_inc(max_ready, 1)

            def weigh(t):
                dve.wait_ge(probs_ready, t + 1)
                link(dve.tensor_tensor(soft[:, 5, :], soft[:, 3, :], soft[:, 4, :], ALU.add))
                link(dve.reciprocal(soft[:, 5, :], soft[:, 5, :]))
                job = f"pv{'AB'[t]}"
                bank = drains(job).rearrange("p (g j d) -> p g j d", g=AKV, j=AG)
                share = soft[:, 5, :].rearrange("p (g j) -> p g j", g=AKV).unsqueeze(3).broadcast_to([P, AKV, AG, AD])
                release(dve.tensor_tensor(ya[:, :].rearrange("p (j g d) -> p g j d", g=AKV, j=AG), bank, share,
                                          ALU.mult), job)

            row_max(A)
            need(dve, "qT2")
            for g in range(AKV):
                lanes = slice(g * AD, g * AD + AD)
                for grp in range(2):
                    out = qs[lanes, grp, :].rearrange("p (b h t) -> p h b t", b=4, h=AH)[:, 4 * g:4 * g + 4]
                    src = qT[lanes, :, 256 + 16 * grp:272 + 16 * grp].rearrange("p j (b t) -> p j b t", t=DEC_T)
                    ins = dve.tensor_copy(out, src)
            link(ins)
            for b in range(DEC_B):
                c0 = (b % 4) * 32
                ins = dve.tensor_copy(qzs[:, b, c0:c0 + 32], qs[:, b // 4, c0:c0 + 32])
            ins.then_inc(qs_ready, 1)
            dve.tensor_tensor(sinkt[:, :], sinkb[:, :], C_("hsel"), ALU.mult).then_inc(v_step, 1)
            links[0] += 1
            dve.wait_ge(v_step, links[0])
            link(dve.tensor_reduce(sinkr[:, :], sinkt[:, :], AX_X, ALU.add))
            for grp in range(2):
                job = f"ss{grp}"
                bank = drains(job)
                release(dve.scalar_tensor_tensor(out=pss[:, grp, :], in0=bank[:, 0:160], scalar=AD ** -0.5,
                                                 in1=C_("mask_s")[:, grp * 160:grp * 160 + 160], op0=ALU.mult,
                                                 op1=ALU.add), job)
            need(dve, "ss1")
            link(dve.tensor_reduce(softs[:, 0, :], pss[:, :, :], AX_X, ALU.max))
            link(dve.tensor_scalar(softs[:, 0, :], softs[:, 0, :], sinkr[:, 0:1], None, ALU.max))
            dve.tensor_scalar(softs[:, 1, :], softs[:, 0, :], -1.0, None, ALU.mult)
            dve.tensor_scalar(softs[:, 2, :], softs[:, 0, :], -1.0, sinkr[:, 0:1], ALU.mult, ALU.add
                              ).then_inc(smax_ready, 1)
            weigh(A)
            row_max(B)
            dve.wait_ge(sprobs_ready, 1)
            link(dve.tensor_tensor(softs[:, 5, :], softs[:, 3, :], softs[:, 4, :], ALU.add))
            link(dve.reciprocal(softs[:, 5, :], softs[:, 5, :]))
            for grp in range(2):
                job = f"spT{grp}"
                bank = drains(job)
                for b in range(4):
                    c0 = b * 32
                    dve.tensor_copy(pz[:, grp, b * P + c0:b * P + c0 + 32], bank[:, c0:c0 + 32])
                release(dve.tensor_copy(pnT[:, grp, :], bank[0:SAMP, P:2 * P]), job)
            for grp in range(2):
                job = f"spv{grp}"
                bank = drains(job)
                release(dve.tensor_scalar(so[:, grp, :], bank[:, 0:P], softs[:, 5, grp:grp + 1], None, ALU.mult), job)
            for grp in range(2):
                job = f"soT{grp}"
                bank = drains(job)
                for g in range(AKV):
                    lanes = slice(g * AD, g * AD + AD)
                    c0 = 256 + grp * 16
                    out = yaT[lanes, :, c0:c0 + 16].rearrange("p j (b t) -> p j b t", t=DEC_T)
                    src = bank[lanes, 0:P].rearrange("p (b h t) -> p h b t", b=4, h=AH)[:, 4 * g:4 * g + 4]
                    ins = dve.tensor_copy(out, src)
                release(ins, job)
            weigh(B)

            for t in TILES:
                job, r = f"AT{t}", OUTS[t]
                bank = drains(job)[0:r, 0:BH * r].rearrange("p (h i) -> p h i", h=BH)
                out = ats[:, :, :] if t == C else atm[:, t]
                mask = (C_("gla_s") if t == C else C_("gla"))[0:r].bitcast(U32)
                release(dve.copy_predicated(out, mask.unsqueeze(1).broadcast_to([r, BH, r]), bank), job)
            last = [288 + META - 1, CHUNK - 1, 2 * CHUNK - 1, 3 * CHUNK - 1, 4 * CHUNK - 1]
            for n in range(5):
                job = f"up{n}"
                bank = drains(job)
                if n:
                    dve.wait_ge(states_ready, 4 * n)
                for p in range(2):
                    for hh in range(2):
                        lanes = slice(hh * BK, hh * BK + BK)
                        src = bank[lanes, p * 256 + hh * BV:p * 256 + hh * BV + BV]
                        if n == 0:
                            ins = dve.tensor_copy(st[lanes, 0, p, :], src)
                        else:
                            ins = dve.scalar_tensor_tensor(out=st[lanes, n, p, :], in0=st[lanes, n - 1, p, :],
                                                           scalar=eb[lanes, p, last[n]:last[n] + 1], in1=src,
                                                           op0=ALU.mult, op1=ALU.add)
                        if not (p and hh):
                            ins.then_inc(states_ready, 1)
                dve.wait_ge(states_ready, 4 * n + 3)
                release(ins, job)
                need(dve, job)
                dve.engine_nop().then_inc(states_ready, 1)
            for h in range(BH):
                src = qh[:, h, 256:288].unsqueeze(1).broadcast_to([P, DEC_B, SAMP])
                ins = dve.tensor_tensor(qsz[:, h], src, C_("batch").rearrange("p (b i) -> p b i", b=DEC_B), ALU.mult)
            ins.then_inc(qsz_ready, 1)
            for t in TILES:
                job, r = f"o{t}", OUTS[t]
                bank = drains(job)
                dve.wait_ge(o_squared, t + 1)
                dve.tensor_scalar(oss[0:r, t, 1, :], oss[0:r, t, 0, :], 1.0 / BV, EPS, ALU.mult, ALU.add
                                  ).then_inc(o_mean, 1)
                dve.wait_ge(o_root, t + 1)
                link(dve.reciprocal(oss[0:r, t, 3, :], oss[0:r, t, 2, :]))
                rows = yb[0:r, t, :].rearrange("r (h e) -> r h e", h=BH)
                release(dve.tensor_tensor(rows, bank[0:r, :].rearrange("r (h e) -> r h e", h=BH),
                                          oss[0:r, t, 3, :].unsqueeze(2).broadcast_to([r, BH, BV]), ALU.mult), job)
                need(dve, job)
                dve.tensor_tensor(yb[0:r, t, :], yb[0:r, t, :], gate[0:r, t, :], ALU.mult).then_inc(yb_ready, 1)
            for p in range(2):
                decay = eb[:, p, 256:288].rearrange("p (b t) -> p b t", t=DEC_T)[:, :, DEC_T - 1:DEC_T]
                ins = dve.tensor_tensor(s0[:, p], s0[:, p], decay.broadcast_to([P, DEC_B, BV]), ALU.mult)
            link(ins)
            for h in range(BH):
                src = vb[0:SAMP, C, h * BV:h * BV + BV].unsqueeze(1).broadcast_to([SAMP, DEC_B, BV])
                dve.tensor_tensor(vblk[:, :, :], src,
                                  C_("batch_rows")[0:SAMP].unsqueeze(2).broadcast_to([SAMP, DEC_B, BV]), ALU.mult
                                  ).then_inc(vblk_ready, 1)
                lanes = slice((h % 2) * BK, (h % 2) * BK + BK)
                for i in range(2):
                    job = f"us{h}.{i}"
                    bank = drains(job).rearrange("p (b e) -> p b e", b=4)
                    part = s0[lanes, h // 2, 4 * i:4 * i + 4, :]
                    release(dve.tensor_tensor(part, part, bank[lanes], ALU.add), job)
            for mt in range(KT):
                need(dve, f"ga{mt}")
                job = f"za{mt}"
                bank = drains(job)
                release(dve.tensor_tensor(mT[:, mt, 0:NO], bank[:, 0:NO], sga[:, 0, 0:NO], ALU.mult), job)
                need(dve, job, f"gr{mt}")
                job = f"zb{mt}"
                bank = drains(job)
                release(dve.tensor_tensor(sga[:, 1, 0:NO], bank[:, 0:NO], sga[:, 1, 0:NO], ALU.mult), job)
                need(dve, job)
                dve.tensor_tensor(mT[:, mt, 0:NO], mT[:, mt, 0:NO], sga[:, 1, 0:NO], ALU.add).then_inc(merged, 1)
            for n in range(2):
                for t in ORDER:
                    job, r = f"wo{n}.{t}", OUTS[t]
                    bank = drains(job)
                    part = x[0:r, t, 512 * n:512 * n + 512]
                    release(dve.tensor_tensor(part, part, bank[0:r, :], ALU.add), job)
                    if n:
                        need(dve, job)
                        dve.engine_nop().then_inc(x2_ready, 1)
            dve.wait_ge(mixer_out, 16 * N_MIX_OUT)
            dve.wait_ge(zeroed, 8)
            for i in range(2):
                job = f"kk{i}"
                bank = drains(job).rearrange("p (h n) -> p h n", h=4)
                dve.tensor_copy(kbd[0:64, 4 * i:4 * i + 4, 0:PK], bank[0:64])
                ins = dve.tensor_copy(kbd[64:P, 4 * i:4 * i + 4, PK:2 * PK], bank[64:P])
                release(ins, job)
            need(dve, "kk1")
            dve.engine_nop().then_inc(kbd_ready, 1)
            for i, t in enumerate(ORDER):
                dve.wait_ge(ssq_done, 3 + i + 1)
                mean(t, OUTS[t], ssq_done, mean_done)
            for i, t in enumerate(ORDER):
                r = OUTS[t]
                dve.wait_ge(root_done, 3 + i + 1)
                link(dve.reciprocal(stat[0:r, t, 3:4], stat[0:r, t, 2:3]))
                dve.scalar_tensor_tensor(out=h2hold[t][0:r, :], in0=x[0:r, t, :], scalar=stat[0:r, t, 3:4],
                                         in1=gffn[0:r, :], op0=ALU.mult, op1=ALU.mult).then_inc(rows_normed, 1)
            for half in range(2):
                job = f"h2T{C}.{half}"
                bank = drains(job).rearrange("p (k r) -> p k r", k=4)
                release(dve.tensor_copy(hT[:, 4 * half:4 * half + 4, 256:NO], bank[:, :, 0:SAMP]), job)

            def mark(ins):
                links[0] += 1
                ins.then_inc(v_step, 1)
                return links[0]

            def since(n):
                if n:
                    dve.wait_ge(v_step, n)

            def top16_round(n, values, spare, out, index):
                if n == 0:
                    return dve.max(out[:, 0:8], values)
                if n == 1:
                    return dve.max_index(index[:, 0:8], out[:, 0:8], values)
                if n == 2:
                    return dve.match_replace(spare, out[:, 0:8], values, FLOOR)
                if n == 3:
                    return dve.max(out[:, 8:16], spare)
                return dve.max_index(index[:, 8:16], out[:, 8:16], spare)

            def best_keys(t, h, rounds):
                for n in rounds:
                    for c in range(2):
                        since(half_done[c])
                        half_done[c] = mark(top16_round(n, sc[:, t, h, c * PK:c * PK + PK], less[:, c, :],
                                                        sv[:, c, :], si[:, h % 2, c, :]))

            def best_sums(h, n):
                since(sum_done[0])
                if n == 0:
                    a = sv[:, 0, :].unsqueeze(2).broadcast_to([P, TOPK, TOPK])
                    b = sv[:, 1, :].unsqueeze(1).broadcast_to([P, TOPK, TOPK])
                    ins = dve.tensor_tensor(cand[:, :].rearrange("r (i j) -> r i j", i=TOPK), a, b, ALU.add)
                else:
                    ins = top16_round(n - 1, cand[:, :], cand2[:, :], fv[:, h, :], fpos[:, h % 2, :])
                sum_done[0] = mark(ins)

            def numbers(h, n):
                since(number_done[0])
                w = h % 2
                grid = pick[:, :, :, :].rearrange("r c k i -> r (c k) i")
                if n == 0:
                    mark(dve.tensor_single_scalar(fij[:, 0, :], fpos[:, w, :], 4, ALU.logical_shift_right))
                    mark(dve.tensor_single_scalar(fij[:, 1, :], fpos[:, w, :], TOPK - 1, ALU.bitwise_and))
                    ins = dve.tensor_copy(sif[:, :, :], si[:, w])
                elif n == 1:
                    ins = dve.tensor_copy(fijf[:, :, :], fij[:, :, :])
                elif n == 2:
                    want = fijf[:, :, :].rearrange("r c k -> r (c k)").unsqueeze(2).broadcast_to([P, 2 * TOPK, TOPK])
                    have = C_("iota").unsqueeze(1).broadcast_to([P, 2 * TOPK, TOPK])
                    ins = dve.tensor_tensor(grid, want, have, ALU.is_equal)
                elif n == 3:
                    number = sif[:, :, :].unsqueeze(2).broadcast_to([P, 2, TOPK, TOPK])
                    ins = dve.tensor_tensor(pick[:, :, :, :], pick[:, :, :, :], number, ALU.mult)
                elif n == 4:
                    ins = dve.tensor_reduce(eij[:, :, :].rearrange("r c k -> r (c k)"), grid, AX_X, ALU.add)
                else:
                    ins = dve.scalar_tensor_tensor(out=route[:, 0, h, :], in0=eij[:, 0, :], scalar=float(PK),
                                                   in1=eij[:, 1, :], op0=ALU.mult, op1=ALU.add)
                number_done[0] = mark(ins)

            half_done, sum_done, number_done = [0, 0], [0], [0]

            def route_step(t, h, step):
                since(links[0])
                if step < 2:
                    best_keys(t, h, (range(3), range(3, 5))[step])
                else:
                    for n in (range(3), range(3, 6))[step - 2]:
                        best_sums(h, n)
                        if h:
                            numbers(h - 1, n)

            def last_numbers(h):
                since(links[0])
                for n in range(6):
                    numbers(h, n)
                since(links[0])

            def weights_begin(heads):
                last_numbers(heads - 1)
                w = route[:, 1, 0:heads]
                dve.tensor_tensor(w, fv[:, 0:heads], fv[:, 0:heads, 0:1].broadcast_to([P, heads, TOPK]), ALU.subtract
                                  ).then_inc(fv_ready, 1)

            def weights_end(i, heads):
                w, total = route[:, 1, 0:heads], wsum[:, :, 0:heads]
                dve.wait_ge(w_exp, i + 1)
                link(dve.tensor_reduce(total[:, 0], w, AX_X, ALU.add))
                link(dve.reciprocal(total[:, 1], total[:, 0]))
                dve.tensor_tensor(w, w, total[:, 1].unsqueeze(2).broadcast_to([P, heads, TOPK]), ALU.mult
                                  ).then_inc(routed, 1)

            def take_list(i, t):
                dve.wait_ge(lists_turned, i)
                bank = ps[:, LIST_BANK[i], :].rearrange("p (a r) -> p a r", a=4)
                dve.tensor_copy(idxT[:, COL[t]:COL[t] + P], bank[:, 0, :]).then_inc(listed, 1)
                dve.tensor_copy(wT[:, COL[t]:COL[t] + P], bank[:, 1, :]).then_inc(weights_listed, 1)

            need(dve, "pss")
            for h in range(2):
                for step in range(4):
                    route_step(C, h, step)
            weights_begin(2)
            weights_end(0, 2)
            dve.wait_ge(routed, 1)
            link(dve.transpose(turned_s[:, :], route[:, 0, 0:2].rearrange("r h k -> r (h k)")))
            dve.tensor_copy(idxT[:, 256:NO], turned_s[:, :]).then_inc(listed, 1)
            dve.transpose(wT[:, 256:NO], route[:, 1, 0:2].rearrange("r h k -> r (h k)")).then_inc(weights_listed, 1)

            def dot(t, g, s):
                now, landed = held(dve, (GROUP0[t] + g) * NS + (s + 1)), held(dve, 16 * (GROUP0[t] + g + 1))
                dve.wait_ge(spread, now)
                dve.wait_ge(uv_landed[s], landed)
                row_on_all = ps[:, 2 * (s % 2):2 * (s % 2) + 2, :]
                u = uv[:, s, 0:D].rearrange("p (a b) -> p a b", a=2)
                dve.tensor_tensor_reduce(u, row_on_all, u, 1.0, 0.0, ALU.mult, ALU.add, dots[:, s:s + 1]
                                         ).then_inc(dotted, 1)

            def add_sums(i):
                t, r, bank = ORDER[i], OUTS[ORDER[i]], SUM_BANK[i]
                dve.wait_ge(combined, (GROUP0[t] + r // NS) * NS)
                rows = x[0:r, t, :].rearrange("p (a b) -> p a b", a=2)
                dve.tensor_tensor(rows, rows, ps[0:r, bank:bank + 2, :], ALU.add).then_inc(acc_read, 1)

            def final_mean(i):
                dve.wait_ge(fin_ssq, i + 1)
                mean(ORDER[i], OUTS[ORDER[i]], fin_ssq, fin_mean)

            def final_rows(i):
                t, r = ORDER[i], OUTS[ORDER[i]]
                dve.wait_ge(fin_root, i + 1)
                link(dve.reciprocal(stat[0:r, t, 3:4], stat[0:r, t, 2:3]))
                dve.wait_ge(router_landed, 16 * 2)
                if i == 2:
                    dve.wait_ge(y_out[0], 16)
                dve.scalar_tensor_tensor(out=h2[0:r, i % 2, :], in0=x[0:r, t, :], scalar=stat[0:r, t, 3:4],
                                         in1=gfin[0:r, :], op0=ALU.mult, op1=ALU.mult).then_inc(y_ready, 1)

            for i, t in enumerate(ORDER):
                groups = OUTS[t] // NS
                if i < 2:
                    after = ORDER[i + 1]
                    need(dve, f"ps{after}.3")
                    steps = [(h, step) for h in range(PH) for step in range(4)]
                    if i == 0:
                        for h, step in steps[:4]:
                            route_step(after, h, step)
                        del steps[:4]
                groups_before = groups - LIST_AHEAD[i] if i < 2 else 1
                given = 0
                for g in range(groups_before):
                    for s in range(NS):
                        dot(t, g, s)
                        if i and g == 0 and s:
                            (add_sums, final_mean, final_rows)[s - 1](i - 1)
                        if i < 2:
                            due = -(-(g * NS + s + 1) * len(steps) // (groups_before * NS))
                            for h, step in steps[given:due]:
                                route_step(after, h, step)
                            given = due
                if i < 2:
                    weights_begin(PH)
                    dot(t, groups_before, 0)
                    weights_end(i + 1, PH)
                    dot(t, groups_before, 1)
                    take_list(i + 1, after)
                    for s in range(2, NS):
                        dot(t, groups_before, s)
                    groups_before += 1
                with dve.Fori(groups_before, groups) as g:
                    for s in range(NS):
                        dot(t, g, s)
            add_sums(2)
            final_mean(2)
            final_rows(2)


_INS = ["x_prompt", "x_sample", "cache_k_window", "cache_v_window", "state_gla", "meta_tokens", "g_norm_mix", "w_in",
        "w_gate_up", "b_gate", "attn_sinks", "g_gla_norm", "w_branch_a", "w_branch_b", "w_out", "g_norm_ffn",
        "w_peer_q", "peer_sub_keys", "peer_uv", "g_norm_final"]
_OUTS = [(1, SEQ, D), (DEC_B, DEC_T, D), (1, 1, WINDOW, AKV, AD), (1, 1, WINDOW, AKV, AD), (1, 1, BH, BK, BV),
         (1, DEC_B, WINDOW, AKV, AD), (1, DEC_B, WINDOW, AKV, AD), (1, DEC_B, BH, BK, BV)]


def kernel(**inputs):
    import concourse.bacc as bacc
    from concourse.bass_utils import run_bass_kernel_spmd

    nc = bacc.Bacc("TRN2", target_bir_lowering=False, num_devices=1)
    arrays, args = {}, []
    inputs["peer_uv"] = np.concatenate([inputs["peer_u"][0], inputs["peer_v"][0]], 1)
    for name in _INS:
        a = np.ascontiguousarray(inputs[name])
        arrays[f"in_{name}"] = a
        args.append(nc.dram_tensor(f"in_{name}", a.shape, mybir.dt.from_np(a.dtype), kind="ExternalInput").ap())
    arrays["shape_constants"] = shape_constants()
    args.append(nc.dram_tensor("shape_constants", (P, CST_COLS), F32, kind="ExternalInput").ap())
    for i, shape in enumerate(_OUTS):
        args.append(nc.dram_tensor(f"out_{i}", shape, F32, kind="ExternalOutput").ap())
    hybrid_step(nc, *args)
    r = run_bass_kernel_spmd(nc, [arrays], core_ids=[0])
    return tuple(r.results[0][f"out_{i}"] for i in range(len(_OUTS)))
```

```python
from contextlib import ExitStack

import numpy as np

import concourse.bass as bass
from concourse import mybir

F32 = mybir.dt.float32
F32R = mybir.dt.float32r
I32 = mybir.dt.int32
U32 = mybir.dt.uint32
ALU = mybir.AluOpType
ACT = mybir.ActivationFunctionType
AX_X = mybir.AxisListType.X

P = 128
D = 1024
KT = D // P
SEQ, META, DEC_B, DEC_T = 256, 16, 8, 4
SAMP = DEC_B * DEC_T
PAST, META_PAD, WINDOW = 2048, 112, 128
AH, AKV, AD = 8, 2, 64
AG = AH // AKV
ROPE = AD // 4
THETA = 500000.0
BH, BK, BV = 4, 64, 128
CHUNK = 64
RANK = 16
PH, PK, TOPK = 8, 128, 16
NEXP = PK * PK
EPS = 1e-6
NEG = -1e30
FLOOR = -3.0e38

A, B, C = 0, 1, 2
COL = (0, 128, 256)
ROWS = (128, 128, SAMP + META)
OUTS = (128, 128, SAMP)
NT = 304
NO = 288
TILES = (A, B, C)
ORDER = (C, A, B)

Q0, K0, QB0, KB0, VB0, GB0, LR0, GA0, GR0 = 0, 512, 768, 1024, 1280, 1792, 2304, 2320, 3344

CST = dict(ident=128, cos=3 * ROPE, sin=3 * ROPE // 2, mask_a=176, mask_b=256, mask_s=320, gla=128, gla_s=SAMP,
           reset=NT, hsel=AH, batch=DEC_B * SAMP, batch_rows=DEC_B, iota=TOPK, spot=255)
CST_AT, _n = {}, 0
for _name, _w in CST.items():
    CST_AT[_name] = (_n, _w)
    _n += _w
CST_COLS = _n


def shape_constants():
    c = {k: np.zeros((P, w), np.float32) for k, w in CST.items()}
    c["ident"][:] = np.eye(P)
    inv = np.float32(THETA) ** (-np.arange(0, ROPE, 2, dtype=np.float32) / np.float32(ROPE))
    r = np.arange(P)
    pos = np.stack([META + r, META + 128 + r, np.where(r < SAMP, PAST + r % DEC_T, r - SAMP)], 1)
    ang = pos.astype(np.float32)[:, :, None] * inv.astype(np.float32)
    cos, sin = np.cos(ang).astype(np.float32), np.sin(ang).astype(np.float32)
    c["cos"][:] = np.concatenate([cos, cos], 2).reshape(P, -1)
    c["sin"][:] = sin.reshape(P, -1)
    q = r[:, None]
    key = np.arange(176)[None]
    own = key <= q
    meta = (key >= 160) & (q <= META_PAD + key - 160)
    c["mask_a"][:] = np.where(np.where(key < 128, own, meta), 0.0, NEG)
    key = np.arange(256)[None]
    c["mask_b"][:] = np.where(np.where(key < 128, key >= q, key - 128 <= q), 0.0, NEG)
    step = q % DEC_T
    for grp in range(2):
        key = np.arange(160)[None]
        new = (key - 128) // DEC_T == grp * 4 + q // 32
        new = new & ((key - 128) % DEC_T <= step)
        c["mask_s"][:, grp * 160:grp * 160 + 160] = np.where(np.where(key < 128, key >= step, new), 0.0, NEG)
    i = np.arange(P)[None]
    c["gla"][:] = (q <= i) & (q // CHUNK == i // CHUNK)
    i = np.arange(SAMP)[None]
    c["gla_s"][:] = (q <= i) & (q // DEC_T == i // DEC_T)
    c["reset"][:] = 1.0
    c["reset"][:, [0, 64, 128, 192, *range(256, 288, DEC_T), 288]] = 0.0
    b, i = np.arange(DEC_B)[:, None], np.arange(SAMP)[None]
    c["batch"][:] = (i // DEC_T == b).reshape(1, -1)
    c["batch_rows"][:] = q // DEC_T == np.arange(DEC_B)[None]
    c["iota"][:] = np.arange(TOPK)
    c["hsel"][:] = q // DEC_T % AH == np.arange(AH)[None]
    c["spot"][:, 127] = 1.0
    return np.concatenate([c[k] for k in CST], 1)


def psum_jobs():
    jobs = [("gvecT", "v")]
    jobs += [(f"hT{t}.{half}", "v") for t in (A, B) for half in range(2)] + [("kv0", "a")]
    jobs += [("hT2.0", "v"), ("hT2.1", "v"), ("kv1", "a"), ("kv2", "a"), ("lrT", "v")]
    jobs += [(f"qc{j}", "a") for j in range(AG)]
    jobs += [(f"q{t}", "a") for t in TILES]
    jobs += [(f"vbT{h}", "a") for h in range(BH)] + [("ld0", "v"), ("ld1", "v")]
    jobs += [(f"kT{t}", "v") for t in TILES] + [(f"qT{t}", "a") for t in TILES]
    jobs += [(f"gb{h}", "v") for h in range(BH)] + [(f"vb{t}", "a") for t in TILES]
    jobs += [("kb0", "v"), ("kb1", "v"), ("qb0", "v"), ("qb1", "v")]
    jobs += [(f"scA.{j}", "v") for j in range(AG)]
    jobs += [("kcT0", "a"), ("kcT1", "a"), ("ga0", "a"), ("ss0", "v"), ("ss1", "v")]
    jobs += [(f"pTA.{i}", "a") for i in range(4)] + [("ga1", "a"), ("pvA", "v"), ("yaT0", "a")]
    jobs += [(f"scB.{j}", "v") for j in range(AG)]
    jobs += [("spT0", "v"), ("spT1", "v"), ("ga2", "a"), ("spv0", "v"), ("spv1", "v"), ("soT0", "v"), ("soT1", "v")]
    jobs += [(f"pTB.{i}", "a") for i in range(4)] + [("ga3", "a"), ("pvB", "v"), ("yaT1", "a")]
    jobs += [(f"keT{t}", "a") for t in TILES] + [(f"AT{t}", "v") for t in TILES]
    jobs += [(f"up{n}", "v") for n in range(5)]
    jobs += [(f"o{t}", "v") for t in TILES] + [("ga4", "a")]
    for t in TILES:
        jobs += [(f"ybT{t}", "v"), (f"ga{5 + t}", "a")]
    for m in range(KT):
        jobs += [(f"za{m}", "v"), (f"gr{m}", "a"), (f"zb{m}", "v")]
        jobs += [(f"us{m}.{x}", "v") for x in range(2) if m < BH]
    jobs += [(f"wo{n}.{t}", "v") for t in ORDER for n in range(2)]
    jobs += [(f"h2T{C}.{half}", "v") for half in range(2)] + [("kk0", "v"), ("kk1", "v")]
    jobs += [("pqs0", "a"), ("pqs1", "a"), ("pqsT", "a"), ("pss", "a")]
    jobs += [(f"h2T{t}.{half}", "a") for t in (A, B) for half in range(2)]
    for i in range(5):
        jobs += [(f"pq{h}", "a") for h in range(2 * i, 2 * i + 2) if i < 4]
        jobs += [(f"ps{A}.{i - 1}", "a")] * (i > 0)
    return jobs


JOBS = psum_jobs()
AT = {name: i for i, (name, _) in enumerate(JOBS)}
DRAINS = {"v": [n for n, e in JOBS if e == "v"], "a": [n for n, e in JOBS if e == "a"]}
ORDINAL = {n: i + 1 for e in "va" for i, n in enumerate(DRAINS[e])}
DRAINER = dict(JOBS)

RING = 3
UNITS = [("kv", "lrT"), ("q", "qc3"), ("vb", "vbT3"), ("gb", "gb3"), ("qkb", "qb1")]
UNITS += [("ga0", "ga3"), ("ga1", "ga7")] + [(f"mix{_i}", f"zb{2 * _i + 1}") for _i in range(4)]
UNITS += [("wo0", "wo0.1"), ("wo1", "wo1.1"), ("wq0", "pq3"), ("wq1", "pq7")]
UNIT_AT = {n: i for i, (n, _) in enumerate(UNITS)}

NS = 8
PLACE = (0, 1, 6, 7, 2, 3, 4, 5)
LIST_AHEAD = (1, 2, 0)
SUM_BANK = (4, 6, 4)
LATE_BANK = 7
LIST_BANK = (None, 6, 4)
GROUP0 = {C: 0, A: OUTS[C] // NS, B: (OUTS[C] + OUTS[A]) // NS}


def hybrid_step(nc, x_prompt, x_sample, cache_k, cache_v, state_gla, meta_tokens, g_mix, w_in, w_gate_up, b_gate,
                sinks, g_gla, w_a, w_b, w_out, g_ffn, w_pq, sub_keys, peer_uv, g_final, cst_in,
                y_prompt, y_sample, nk_prompt, nv_prompt, ns_prompt, nk_sample, nv_sample, ns_sample):
    with ExitStack() as ctx:
        def sb(name, shape, dt=F32):
            return ctx.enter_context(nc.sbuf_tensor(name, shape, dt))

        def overlay(room, *variants):
            found, most = {}, 0
            for variant in variants:
                with ExitStack() as turn:
                    for name, shape, *dt in variant:
                        found[name] = turn.enter_context(nc.sbuf_tensor(name, shape, *(dt or [F32])))
                most = max(most, sum(int(np.prod(v[1][1:])) for v in variant))
            sb(room, [P, most])
            return found

        def sem(name):
            return ctx.enter_context(nc.semaphore(name))

        ps = ctx.enter_context(nc.psum_tensor("ps", [P, 8, 512], F32))

        cst = sb("cst", [P, CST_COLS])
        x = sb("x", [P, 3, D])
        hT = sb("hT", [P, KT, NT])
        gvec = sb("gvec", [19, P])
        gT = sb("gT", [P, 19])
        gffn = sb("gffn", [P, D])
        stat = sb("stat", [P, 4, 4])
        o1 = overlay("room_ring", [("ring", [P, RING, 4096]), ("mT", [P, KT, NT]), ("yaT", [P, AG, NT]),
                                   ("ybT", [P, BH, NT])], [("uv", [P, NS, 2 * D])])
        ring, mT, yaT, ybT, uv = (o1[k] for k in ("ring", "mT", "yaT", "ybT", "uv"))
        mixer = [("qkv", [P, 3, 768]), ("qT", [P, AG, NT]), ("kz", [P, AKV, NT]), ("kTs", [P, SAMP]),
                 ("kcT", [P, DEC_B, P]), ("vc", [P, DEC_B, P]), ("sinkb", [P, AH]), ("sinkr", [P, 1]),
                 ("sinkt", [P, AH]), ("soft", [P, 6, AH]), ("softs", [P, 6, 2]), ("qs", [P, 2, P]),
                 ("qzs", [P, DEC_B, P]), ("pss", [P, 2, 160]), ("pz", [P, 2, 4 * P]), ("pnT", [SAMP, 2, P]),
                 ("ya", [P, 512]), ("vb", [P, 3, 512]), ("gate", [P, BH, NO]),
                 ("wgu", [RANK, 256]), ("lrT", [RANK, NT]), ("eb", [P, 2, NT]), ("bcum", [P, 2, NT]),
                 ("kt", [P, 2, NT]), ("ket", [P, 2, NT]), ("qh", [P, BH, NT]), ("atm", [P, 2, BH, P]),
                 ("ats", [SAMP, BH, SAMP]), ("ke", [P, 3, 2, P]), ("s0", [P, 2, DEC_B, BV]), ("oss", [P, 3, 4, BH])]
        m = {}
        with ExitStack() as mixers:
            for name, shape in mixer:
                m[name] = mixers.enter_context(nc.sbuf_tensor(name, shape, F32))
            with ExitStack() as turn:
                m["kc"] = turn.enter_context(nc.sbuf_tensor("kc", [P, DEC_B, P], F32))
            m["st"] = mixers.enter_context(nc.sbuf_tensor("st", [P, 5, 2, BV], F32))
            for variant in ([("hrow", [P, 3, D])],
                            [("ropet", [P, 10, 2 * ROPE]), ("so", [P, 2, P]), ("sm", [P, AH, 256]),
                             ("pT", [P, AH, 2, P])],
                            [("qsz", [P, BH, DEC_B, SAMP]), ("vblk", [SAMP, DEC_B, BV]), ("yb", [P, 3, 512]),
                             ("sga", [P, 2, NT])]):
                with ExitStack() as turn:
                    for name, shape in variant:
                        m[name] = turn.enter_context(nc.sbuf_tensor(name, shape, F32))
        (qkv, qT, kz, kTs, kcT, vc, sinkb, sinkr, sinkt, soft, softs, qs, qzs, pss, pz, pnT, ya, vb, gate, wgu,
         lrT, eb, bcum, kt, ket, qh, atm, ats, ke, s0, oss) = (m[k] for k, _ in mixer)
        kc, st, hrow, ropet, so, sm, pT, qsz, vblk, yb, sga = (m[k] for k in (
            "kc", "st", "hrow", "ropet", "so", "sm", "pT", "qsz", "vblk", "yb", "sga"))
        vbT = sm[:, 0:5, :].rearrange("p h k -> p (h k)")[:, 0:BH * NT].rearrange("p (h n) -> p h n", h=BH)
        h2hi = sb("h2hi", [P, 3, D], F32R)
        h2lo = sb("h2lo", [P, 3, D], F32R)
        h2 = sb("h2", [P, 2, D])
        h2c = sb("h2c", [P, D])
        keys = sb("keys", [P, PH, P])
        kbd = sb("kbd", [P, PH, 2 * PK])
        qp = sb("qp", [P, PH, NO])
        sc = sb("sc", [P, 3, PH, 2 * PK])
        gfin = sb("gfin", [P, D])
        pqrow = sc[0:SAMP, B, 0:4, :].rearrange("r h n -> r (h n)")
        less = sb("less", [P, 2, 2, PK])
        sv = sb("sv", [P, 2, 2, TOPK])
        si = sb("si", [P, 2, 2, TOPK], U32)
        sif = sb("sif", [P, 2, TOPK])
        cand = sb("cand", [P, 2, TOPK * TOPK])
        cand2 = sb("cand2", [P, 2, TOPK * TOPK])
        fv = sb("fv", [P, PH, TOPK])
        fpos = sb("fpos", [P, 2, TOPK], U32)
        fij = sb("fij", [P, 2, TOPK], U32)
        fijf = sb("fijf", [P, 2, TOPK])
        pick = sb("pick", [P, 2, TOPK, TOPK])
        eij = sb("eij", [P, 2, TOPK])
        turned_s = sb("turned_s", [P, SAMP])
        route = sb("route", [P, 2, PH, TOPK])
        wsum = sb("wsum", [P, 2, PH])
        onehot = [sb(f"onehot{s}", [P, P], F32R) for s in range(NS)]
        wz = [sb(f"wz{s}", [P, P]) for s in range(NS)]
        islot = [sb(f"islot{s}", [P, 1], I32) for s in range(NS)]
        dots, acts = sb("dots", [P, NS]), sb("acts", [P, NS])
        idxT = sb("idxT", [P, NO], I32)
        wT = sb("wT", [P, NO])

        h2hold = [h2[:, 0, :], h2[:, 1, :], h2c[:, :]]

        def C_(name):
            at, w = CST_AT[name]
            return cst[:, at:at + w]

        ident = C_("ident")

        x_in = [sem(f"x_in{t}") for t in TILES]
        ident_landed, cst_landed = sem("ident_landed"), sem("cst_landed")
        gains_landed = sem("gains_landed")
        small_landed = sem("small_landed")
        cache_landed = sem("cache_landed")
        unit_landed = [sem(f"unit_landed{s}") for s in range(RING)]
        router_landed = sem("router_landed")
        mixer_out = sem("mixer_out")
        cache_copied = sem("cache_copied")
        y_out = [sem(f"y_out{i}") for i in range(3)]
        uv_landed = [sem(f"uv_landed{s}") for s in range(NS)]
        filled = sem("bank_filled")
        drained = {"v": sem("bank_drained_v"), "a": sem("bank_drained_a")}
        v_step = sem("v_step")
        a_step = sem("a_step")
        zeroed = sem("zeroed")
        ssq_done, mean_done, root_done, rows_normed = (sem(k) for k in ("ssq_done", "mean_done", "root_done",
                                                                        "rows_normed"))
        roped = sem("roped")
        ld_abs, ld_log, b_ready, b_exp, last_ready, ket_exp = (sem(k) for k in ("ld_abs", "ld_log", "b_ready",
                                                                                "b_exp", "last_ready", "ket_exp"))
        gate_sig, first_gate_ready = sem("gate_sig"), sem("first_gate_ready")
        max_ready, probs_ready = sem("max_ready"), sem("probs_ready")
        qs_ready, smax_ready, sprobs_ready = sem("qs_ready"), sem("smax_ready"), sem("sprobs_ready")
        states_ready = sem("states_ready")
        o_squared, o_mean, o_root = sem("o_squared"), sem("o_mean"), sem("o_root")
        qsz_ready, vblk_ready, sstate_ready = sem("qsz_ready"), sem("vblk_ready"), sem("sstate_ready")
        merged = sem("merged")
        x2_ready = sem("x2_ready")
        h2_high, h2_split = sem("h2_high"), sem("h2_split")
        kbd_ready = sem("kbd_ready")
        fv_ready, w_exp, routed = sem("fv_ready"), sem("w_exp"), sem("routed")
        late_scored, late_kept = sem("late_scored"), sem("late_kept")
        lists_turned, listed, weights_listed = sem("lists_turned"), sem("listed"), sem("weights_listed")
        idx_copied, onehot_ready = sem("idx_copied"), sem("onehot_ready")
        spread, dotted, factored, wz_ready, combined = (sem(k) for k in ("spread", "dotted", "factored", "wz_ready",
                                                                       "combined"))
        acc_read = sem("acc_read")
        pool_turn = sem("pool_turn")
        fin_ssq, fin_mean, fin_root, y_ready = (sem(k) for k in ("fin_ssq", "fin_mean", "fin_root", "y_ready"))

        N_SMALL_IN, N_CACHE_IN, N_MIX_OUT = 3, 4, 8

        def take(eng, job):
            eng.wait_ge(filled, AT[job] + 1)
            return ps[:, AT[job] % 8, :]

        def release(ins, job):
            ins.then_inc(drained[DRAINER[job]], 1)

        def need(eng, *names):
            for name in names:
                eng.wait_ge(drained[DRAINER[name]], ORDINAL[name])

        w_in_v = w_in[0].rearrange("(k p) n -> p k n", p=P)

        def slot(unit, k):
            s = UNIT_AT[unit] % RING
            return ring[:, s, :].rearrange("p (k n) -> p k n", k=k)

        def unit_dmas(unit):
            full = slot(unit, KT)
            if unit == "kv":
                return [(full[:, :, 0:256], w_in_v[:, :, K0:K0 + 256]),
                        (full[:, :, 256:256 + RANK], w_in_v[:, :, LR0:LR0 + RANK])]
            if unit in ("q", "vb", "gb", "qkb", "ga0", "ga1"):
                at = dict(q=Q0, vb=VB0, gb=GB0, qkb=QB0, ga0=GA0, ga1=GA0 + 512)[unit]
                return [(full, w_in_v[:, :, at:at + 512])]
            n = int(unit[-1])
            if unit.startswith("mix"):
                wav = w_a[0].rearrange("(g j d) n -> g d j n", g=AKV, j=AG)
                cols = slice(256 * n, 256 * n + 256)
                return [(full[:, :, 0:256], w_in_v[:, :, GR0 + 256 * n:GR0 + 256 * n + 256]),
                        (full[0:AD, 0:4, 256:512], wav[0, :, :, cols]), (full[AD:P, 0:4, 256:512], wav[1, :, :, cols]),
                        (full[:, 4:8, 256:512], w_b[0].rearrange("(h e) n -> e h n", h=BH)[:, :, cols])]
            w = w_out if unit.startswith("wo") else w_pq
            return [(full, w[0].rearrange("(k p) n -> p k n", p=P)[:, :, 512 * n:512 * n + 512])]

        landed_at, total = {}, [0] * RING
        for name, _ in UNITS:
            total[UNIT_AT[name] % RING] += 16 * len(unit_dmas(name))
            landed_at[name] = total[UNIT_AT[name] % RING]

        def unit_ready(eng, unit):
            eng.wait_ge(unit_landed[UNIT_AT[unit] % RING], landed_at[unit])

        def held(eng, value):
            return value if isinstance(value, int) else eng.snap(value)

        block = ctx.enter_context(nc.Block())

        @block.sync
        def _(sp):
            for dst, src in ((gvec[0:8, :], g_mix[0].rearrange("(k p) -> k p", p=P)),
                             (gvec[8:16, :], g_ffn[0].rearrange("(k p) -> k p", p=P)),
                             (gvec[16:18, :], b_gate[0].rearrange("(k p) -> k p", p=P)), (gvec[18:19, :], g_gla)):
                sp.dma_start(dst, src).then_inc(gains_landed, 16)
            sp.dma_start(x[:, A, :], x_prompt[0, 0:128, :]).then_inc(x_in[A], 16)
            sp.dma_start(x[:, B, :], x_prompt[0, 128:256, :]).then_inc(x_in[B], 16)
            sp.dma_start(x[0:SAMP, C, :], x_sample.rearrange("b t d -> (b t) d")).then_inc(x_in[C], 16)
            sp.dma_start(x[SAMP:SAMP + META, C, :], meta_tokens).then_inc(x_in[C], 16)
            for n, (unit, _) in enumerate(UNITS):
                if unit == "wq1":
                    sp.wait_ge(mixer_out, 16 * N_MIX_OUT)
                    sp.wait_ge(merged, KT)
                    sp.dma_start(keys[:, :, :].rearrange("n h (c d) -> n h c d", c=2),
                                 sub_keys[0].rearrange("h c n d -> n h c d")).then_inc(router_landed, 16)
                    sp.dma_start(gfin[:, :], g_final.rearrange("(o d) -> o d", o=1).broadcast_to([P, D])
                                 ).then_inc(router_landed, 16)
                if n >= RING:
                    sp.wait_ge(filled, AT[UNITS[n - RING][1]] + 1)
                for dst, src in unit_dmas(unit):
                    sp.dma_start(dst, src).then_inc(unit_landed[n % RING], 16)
                if unit == "ga0":
                    sp.wait_ge(roped, 3)
                    need(sp, "kv0", "kv1", "kv2")
                    for c0, prompt, sample in ((512, nk_prompt, nk_sample), (640, nv_prompt, nv_sample)):
                        sp.dma_start(prompt[0, 0].rearrange("s g d -> s (g d)"),
                                     qkv[:, B, c0:c0 + P]).then_inc(mixer_out, 16)
                        sp.dma_start(sample[0, :, WINDOW - DEC_T:WINDOW].rearrange("b t g d -> b t (g d)"),
                                     qkv[0:SAMP, C, c0:c0 + P]).then_inc(mixer_out, 16)
                if unit == "wo1":
                    sp.wait_ge(states_ready, 4 * 5)
                    for p in range(2):
                        sp.dma_start(ns_prompt[0, 0, 2 * p:2 * p + 2].rearrange("h d e -> (h d) e"),
                                     st[:, 4, p, :]).then_inc(mixer_out, 16)
                    need(sp, "us3.1")
                    for p in range(2):
                        sp.dma_start(ns_sample[0, :, 2 * p:2 * p + 2].rearrange("b h d e -> (h d) b e"),
                                     s0[:, p]).then_inc(mixer_out, 16)
            for i, t in enumerate(ORDER):
                sp.wait_ge(y_ready, i + 1)
                dst = y_sample.rearrange("b t d -> (b t) d") if t == C else y_prompt[0, 128 * t:128 * t + 128, :]
                sp.dma_start(dst, h2[0:OUTS[t], i % 2, :]).then_inc(y_out[i], 16)
            for i in range(3):
                sp.wait_ge(y_out[i], 16)
            sp.wait_ge(cache_copied, 16 * 2)

        @block.gpsimd
        def _(pool):
            pool.dma_start(cst[:, 0:P], cst_in[:, 0:P]).then_inc(ident_landed, 16)
            unit_ready(pool, "q")
            pool.dma_start(cst[:, P:CST_COLS], cst_in[:, P:CST_COLS]).then_inc(cst_landed, 16)
            for dst, src in ((wgu[:, :], w_gate_up[0]),
                             (sinkb[:, :], sinks[0:1, :].broadcast_to([P, AH])),
                             (gffn[:, :], g_ffn[0:1, :].broadcast_to([P, D]))):
                pool.dma_start(dst, src).then_inc(small_landed, 16)
            for dst, src in ((kc[:, :, :], cache_k[0].rearrange("b s g d -> s b (g d)")),
                             (vc[:, :, :], cache_v[0].rearrange("b s g d -> s b (g d)")),
                             (s0[:, 0], state_gla[0, :, 0:2].rearrange("b h d e -> (h d) b e")),
                             (s0[:, 1], state_gla[0, :, 2:4].rearrange("b h d e -> (h d) b e"))):
                pool.dma_start(dst, src).then_inc(cache_landed, 16)
            for cache, out in ((cache_k, nk_sample), (cache_v, nv_sample)):
                pool.dma_start(out[0, :, 0:WINDOW - DEC_T].rearrange("b s g d -> b (s g d)"),
                               cache[0, :, DEC_T:WINDOW].rearrange("b s g d -> b (s g d)")
                               ).then_inc(cache_copied, 16)
            for buf in (kz, qh, qs, qzs, pz, atm, ats):
                pool.memset(buf[:], 0.0).then_inc(zeroed, 1)
            pool.wait_ge(mixer_out, 16 * N_MIX_OUT)
            pool.wait_ge(merged, KT)
            pool.memset(kbd[:, :, :], 0.0).then_inc(zeroed, 1)

            def token(first_use, tk, col, row, s):
                now, back = held(pool, tk + 1), held(pool, tk - (NS - 1))
                if not first_use:
                    pool.wait_ge(uv_landed[s], 16 * ((tk - s) // NS))
                    pool.wait_ge(spread, back)
                pool.tensor_copy(islot[s][:, :], idxT[:, bass.ds(col, 1)]).then_inc(idx_copied, 1)
                pool.tensor_copy(onehot[s][:, :], ident[:, bass.ds(row, 1)].broadcast_to([P, P])
                                 ).then_inc(onehot_ready, 1)
                pool.wait_ge(idx_copied, now)
                if not first_use:
                    pool.wait_ge(combined, back)
                pool.sem_inc(pool_turn, 1)
                pool.indirect_dma_start(uv[:, PLACE[s], :], None, peer_uv,
                                        bass.IndirectOffsetOnAxis(ap=islot[s][:, 0:1], axis=0)
                                        ).then_inc(uv_landed[s], 16)

            for i, t in enumerate(ORDER):
                r = OUTS[t]
                pool.wait_ge(rows_normed, 3 + i + 1)
                pool.tensor_copy(h2hi[0:r, t, :], h2hold[t][0:r, :]).then_inc(h2_high, 1)
                pool.wait_ge(h2_high, i + 1)
                pool.tensor_tensor(h2lo[0:r, t, :], h2hold[t][0:r, :], h2hi[0:r, t, :].bitcast(F32), ALU.subtract
                                   ).then_inc(h2_split, 1)
            for i, t in enumerate(ORDER):
                pool.wait_ge(listed, i + 1)
                g0 = 0
                if i == 0:
                    for s in range(NS):
                        if s in (4, 6):
                            need(pool, "pq3" if s == 4 else "pq7")
                        token(True, s, COL[t] + s, s, s)
                    g0 = 1
                with pool.Fori(g0, OUTS[t] // NS) as g:
                    for s in range(NS):
                        token(False, (GROUP0[t] + g) * NS + s, g * NS + (COL[t] + s), g * NS + s, s)

        @block.tensor
        def _(pe):
            def open_(job):
                assert AT[job] == pe_at[0], (job, JOBS[pe_at[0]])
                pe_at[0] += 1
                if AT[job] >= 8:
                    need(pe, JOBS[AT[job] - 8][0])
                return ps[:, AT[job] % 8, :]

            pe_at = [0]

            def close(ins):
                ins.then_inc(filled, 1)

            pe.wait_ge(ident_landed, 16)
            pe.wait_ge(gains_landed, 16 * 4)
            bank = open_("gvecT")
            close(pe.transpose(bank[:, 0:19], gvec[:, :], ident[0:19, 0:19]))

            def rows_of(unit, job, t, c0, n):
                bank, r, w = open_(job), ROWS[t], slot(unit, KT)
                for k in range(KT):
                    ins = pe.matmul(bank[0:r, 0:n], hT[:, k, COL[t]:COL[t] + r], w[:, k, c0:c0 + n],
                                    start=(k == 0), stop=(k == KT - 1))
                close(ins)

            def cols_of(unit, job, c0, n, width):
                bank, w = open_(job), slot(unit, KT)
                for k in range(KT):
                    ins = pe.matmul(bank[0:n, 0:width], w[:, k, c0:c0 + n], hT[:, k, 0:width],
                                    start=(k == 0), stop=(k == KT - 1))
                close(ins)


            def turn_normed(t):
                pe.wait_ge(rows_normed, t + 1)
                r = ROWS[t]
                for half in range(2):
                    bank = open_(f"hT{t}.{half}").rearrange("p (k r) -> p k r", k=4)
                    for k in range(4):
                        c0 = (4 * half + k) * P
                        ins = pe.transpose(bank[:, k, 0:r], hrow[0:r, t, c0:c0 + P], ident[0:r, 0:r])
                    close(ins)

            turn_normed(A)
            turn_normed(B)
            for t in TILES:
                unit_ready(pe, "kv")
                need(pe, f"hT{t}.1")
                rows_of("kv", f"kv{t}", t, 0, 256)
                if t == A:
                    turn_normed(C)
            cols_of("kv", "lrT", 256, RANK, NT)
            unit_ready(pe, "q")
            for j in range(AG):
                cols_of("q", f"qc{j}", j * P, P, NT)

            def rows_back(job, t, source):
                bank, r = open_(job), ROWS[t]
                for j in range(4):
                    ins = pe.transpose(bank[0:r, j * P:j * P + P], source[:, j, COL[t]:COL[t] + r], ident)
                close(ins)

            need(pe, "qc3")
            for t in TILES:
                rows_back(f"q{t}", t, qT)
            unit_ready(pe, "vb")
            for h in range(BH):
                cols_of("vb", f"vbT{h}", h * BV, BV, NT)
            pe.wait_ge(small_landed, 16 * N_SMALL_IN)
            for p in range(2):
                bank = open_(f"ld{p}")
                need(pe, "lrT")
                close(pe.matmul(bank[:, 0:NT], wgu[:, p * P:p * P + P], lrT[:, :], start=True, stop=True))
            for t in TILES:
                bank, r = open_(f"kT{t}"), ROWS[t]
                pe.wait_ge(roped, t + 1)
                close(pe.transpose(bank[:, 0:r], qkv[0:r, t, 512:640], ident[0:r, 0:r]))
            for t in TILES:
                bank, r = open_(f"qT{t}").rearrange("p (j r) -> p j r", j=AG), ROWS[t]
                for j in range(AG):
                    ins = pe.transpose(bank[:, j, 0:r], qkv[0:r, t, j * P:j * P + P], ident[0:r, 0:r])
                close(ins)
            unit_ready(pe, "gb")
            for h in range(BH):
                cols_of("gb", f"gb{h}", h * BV, BV, NO)
            need(pe, "vbT3")
            for t in TILES:
                rows_back(f"vb{t}", t, vbT)
            unit_ready(pe, "qkb")
            for p in range(2):
                cols_of("qkb", f"kb{p}", 256 + p * P, P, NT)
            for p in range(2):
                cols_of("qkb", f"qb{p}", p * P, P, NT)

            def first_gate(mt):
                unit_ready(pe, f"ga{mt // 4}")
                cols_of(f"ga{mt // 4}", f"ga{mt}", (mt % 4) * P, P, NO)

            def scores(t):
                width = 176 if t == A else 256
                need(pe, f"qT{t}", "kT2")
                for j in range(AG):
                    bank = open_(f"sc{'AB'[t]}.{j}").rearrange("p (g k) -> p g k", g=2)
                    for g in range(AKV):
                        lhs = qT[:, j, COL[t]:COL[t] + P]
                        if t == A:
                            pe.matmul(bank[:, g, 0:128], lhs, kz[:, g, 0:128], start=True, stop=True)
                            ins = pe.matmul(bank[:, g, 128:width], lhs, kz[:, g, 256:304], start=True, stop=True)
                        else:
                            ins = pe.matmul(bank[:, g, :], lhs, kz[:, g, 0:256], start=True, stop=True)
                    close(ins)

            def attend(t):
                pe.wait_ge(probs_ready, t + 1)
                for i in range(4):
                    bank = open_(f"pT{'AB'[t]}.{i}").rearrange("p (h c q) -> p h c q", h=2, c=2)
                    for hh in range(2):
                        row = sm[:, 2 * i + hh, :]
                        pe.transpose(bank[:, hh, 0, :], row[:, 0:128], ident)
                        n = 48 if t == A else 128
                        ins = pe.transpose(bank[0:n, hh, 1, :], row[:, 128:128 + n], ident)
                    close(ins)
                first_gate(1 if t == A else 3)
                bank = open_(f"pv{'AB'[t]}")
                need(pe, f"pT{'AB'[t]}.3", "kv2")
                for h in range(AH):
                    c0 = 640 + (h // AG) * AD
                    first, second = (A, C) if t == A else (A, B)
                    n = ROWS[second]
                    pe.matmul(bank[:, h * AD:h * AD + AD], pT[:, h, 0, :], qkv[:, first, c0:c0 + AD],
                              start=True, stop=False)
                    ins = pe.matmul(bank[:, h * AD:h * AD + AD], pT[0:n, h, 1, :], qkv[0:n, second, c0:c0 + AD],
                                    start=False, stop=True)
                close(ins)
                bank = open_(f"yaT{t}").rearrange("p (j r) -> p j r", j=AG)
                need(pe, f"pv{'AB'[t]}")
                for j in range(AG):
                    ins = pe.transpose(bank[:, j, :], ya[:, j * P:j * P + P], ident)
                close(ins)

            scores(A)
            pe.wait_ge(cache_landed, 16 * N_CACHE_IN)
            for i in range(2):
                bank = open_(f"kcT{i}").rearrange("p (b s) -> p b s", b=4)
                for b in range(4):
                    ins = pe.transpose(bank[:, b, :], kc[:, 4 * i + b, :], ident)
                close(ins)
            first_gate(0)
            need(pe, "kcT1")
            pe.wait_ge(qs_ready, 1)
            for grp in range(2):
                bank = open_(f"ss{grp}")
                for b in range(4):
                    pe.matmul(bank[:, 0:WINDOW], qzs[:, 4 * grp + b, :], kcT[:, 4 * grp + b, :],
                              start=(b == 0), stop=(b == 3))
                close(pe.matmul(bank[:, WINDOW:160], qs[:, grp, :], kTs[:, :], start=True, stop=True))
            attend(A)
            scores(B)
            pe.wait_ge(sprobs_ready, 1)
            for grp in range(2):
                bank = open_(f"spT{grp}")
                pe.transpose(bank[:, 0:P], pss[:, grp, 0:WINDOW], ident)
                close(pe.transpose(bank[0:SAMP, P:2 * P], pss[:, grp, WINDOW:160], ident))
            first_gate(2)
            for grp in range(2):
                bank = open_(f"spv{grp}")
                need(pe, f"spT{grp}")
                for b in range(4):
                    pe.matmul(bank[:, 0:P], pz[:, grp, b * P:b * P + P], vc[:, 4 * grp + b, :],
                              start=(b == 0), stop=False)
                close(pe.matmul(bank[:, 0:P], pnT[:, grp, :], qkv[0:SAMP, C, 640:768], start=False, stop=True))
            for grp in range(2):
                bank = open_(f"soT{grp}")
                need(pe, f"spv{grp}")
                close(pe.transpose(bank[:, 0:P], so[:, grp, :], ident))
            attend(B)

            for t in TILES:
                bank, r = open_(f"keT{t}").rearrange("p (c d) -> p c d", c=4), ROWS[t]
                need(pe, "kb1")
                for p in range(2):
                    ins = pe.transpose(bank[0:r, p, :], ket[:, p, COL[t]:COL[t] + r], ident)
                close(ins)
            for t in TILES:
                r = OUTS[t]
                bank = open_(f"AT{t}")
                need(pe, "qb1")
                for h in range(BH):
                    ins = pe.matmul(bank[0:r, h * r:h * r + r], kt[:, h // 2, COL[t]:COL[t] + r],
                                    qh[:, h, COL[t]:COL[t] + r], start=True, stop=True)
                close(ins)
            chunks = [(C, SAMP, META), (A, 0, CHUNK), (A, CHUNK, CHUNK), (B, 0, CHUNK), (B, CHUNK, CHUNK)]
            need(pe, "keT2", "vb2")
            for n, (t, r0, r) in enumerate(chunks):
                bank = open_(f"up{n}")
                for p in range(2):
                    ins = pe.matmul(bank[:, p * 256:p * 256 + 256], ke[r0:r0 + r, t, p, :],
                                    vb[r0:r0 + r, t, p * 256:p * 256 + 256], start=True, stop=True)
                close(ins)
            for t in (A, B):
                bank = open_(f"o{t}")
                need(pe, f"AT{t}")
                pe.wait_ge(states_ready, 4 * (2 * t + 2))
                for h in range(BH):
                    cols = slice(h * BV, h * BV + BV)
                    pe.matmul(bank[:, cols], atm[:, t, h, :], vb[:, t, cols], start=True, stop=False)
                    for c in range(2):
                        r0 = c * CHUNK
                        ins = pe.matmul(bank[r0:r0 + CHUNK, cols], qh[:, h, COL[t] + r0:COL[t] + r0 + CHUNK],
                                        st[:, 2 * t + c, h // 2, :], start=False, stop=True)
                close(ins)
            bank = open_("o2")
            need(pe, "AT2")
            pe.wait_ge(qsz_ready, 1)
            for h in range(BH):
                cols = slice(h * BV, h * BV + BV)
                pe.matmul(bank[0:SAMP, cols], ats[:, h, :], vb[0:SAMP, C, cols], start=True, stop=False)
                for b in range(DEC_B):
                    ins = pe.matmul(bank[0:SAMP, cols], qsz[:, h, b, :], s0[:, h // 2, b, :],
                                    start=False, stop=(b == DEC_B - 1))
            close(ins)
            first_gate(4)
            for t in TILES:
                bank, r = open_(f"ybT{t}").rearrange("p (j r) -> p j r", j=BH), OUTS[t]
                need(pe, f"o{t}")
                for h in range(BH):
                    ins = pe.transpose(bank[:, h, 0:r], yb[0:r, t, h * BV:h * BV + BV], ident[0:r, 0:r])
                close(ins)
                first_gate(5 + t)
            need(pe, "yaT1", "soT1", "ybT2")
            for mt in range(KT):
                n, c0 = mt // 2, (mt % 2) * P
                unit_ready(pe, f"mix{n}")
                w = slot(f"mix{n}", KT)
                bank = open_(f"za{mt}")
                for j in range(AG):
                    ins = pe.matmul(bank[:, 0:NO], w[:, j, 256 + c0:256 + c0 + P], yaT[:, j, 0:NO],
                                    start=(j == 0), stop=(j == 3))
                close(ins)
                cols_of(f"mix{n}", f"gr{mt}", c0, P, NO)
                bank = open_(f"zb{mt}")
                for j in range(BH):
                    ins = pe.matmul(bank[:, 0:NO], w[:, 4 + j, 256 + c0:256 + c0 + P], ybT[:, j, 0:NO],
                                    start=(j == 0), stop=(j == 3))
                close(ins)
                if mt < BH:
                    pe.wait_ge(vblk_ready, mt + 1)
                    for i in range(2):
                        bank = open_(f"us{mt}.{i}")
                        close(pe.matmul(bank, ke[0:SAMP, C, mt // 2, :], vblk[:, 4 * i:4 * i + 4, :],
                                        start=True, stop=True))
            pe.wait_ge(merged, KT)
            for t in ORDER:
                for n in range(2):
                    unit_ready(pe, f"wo{n}")
                    bank, r, w = open_(f"wo{n}.{t}"), OUTS[t], slot(f"wo{n}", KT)
                    for k in range(KT):
                        ins = pe.matmul(bank[0:r, :], mT[:, k, COL[t]:COL[t] + r], w[:, k, :],
                                        start=(k == 0), stop=(k == KT - 1))
                    close(ins)

            def turn_rows(i, t):
                pe.wait_ge(rows_normed, 3 + i + 1)
                r = OUTS[t]
                for half in range(2):
                    bank = open_(f"h2T{t}.{half}").rearrange("p (k r) -> p k r", k=4)
                    for k in range(4):
                        c0 = (4 * half + k) * P
                        ins = pe.transpose(bank[:, k, 0:r], h2hold[t][0:r, c0:c0 + P], ident[0:r, 0:r])
                    close(ins)

            turn_rows(0, C)
            pe.wait_ge(router_landed, 16 * 2)
            for i in range(2):
                bank = open_(f"kk{i}").rearrange("p (h n) -> p h n", h=4)
                for h in range(4):
                    ins = pe.transpose(bank[:, h, :], keys[:, 4 * i + h, :], ident)
                close(ins)
            need(pe, f"h2T{C}.1")
            for n in range(2):
                unit_ready(pe, f"wq{n}")
                bank, w = open_(f"pqs{n}"), slot(f"wq{n}", KT)
                for k in range(KT):
                    ins = pe.matmul(bank[0:SAMP, :], hT[:, k, 256:NO], w[:, k, :], start=(k == 0), stop=(k == KT - 1))
                close(ins)
            bank = open_("pqsT").rearrange("p (h r) -> p h r", r=SAMP)[:, 0:PH]
            for h in range(PH):
                if h % 4 == 0:
                    need(pe, f"pqs{h // 4}")
                ins = pe.transpose(bank[:, h, :], pqrow[:, h * P:h * P + P], ident[0:SAMP, 0:SAMP])
            close(ins)
            need(pe, "pqsT")
            pe.wait_ge(kbd_ready, 1)
            bank = open_("pss").rearrange("p (h n) -> p h n", h=2)
            for h in range(PH):
                ins = pe.matmul(bank[32 * (h // 2):32 * (h // 2) + 32, h % 2, :], qp[:, h, 256:NO], kbd[:, h, :],
                                start=True, stop=True)
            close(ins)
            for i, t in ((1, A), (2, B)):
                turn_rows(i, t)
            need(pe, f"h2T{B}.1")
            def pair_scores(bank, t, i):
                for hh in range(2):
                    h = 2 * i + hh
                    ins = pe.matmul(bank[:, hh * 256:hh * 256 + 256], qp[:, h, COL[t]:COL[t] + P], kbd[:, h, :],
                                    start=True, stop=True)
                return ins

            for i in range(5):
                if i < 4:
                    for h in (2 * i, 2 * i + 1):
                        cols_of(f"wq{h // 4}", f"pq{h}", (h % 4) * P, P, 256)
                if i:
                    need(pe, f"pq{2 * i - 1}")
                    close(pair_scores(open_(f"ps{A}.{i - 1}"), A, i - 1))

            def turn_lists(i):
                pe.wait_ge(routed, i + 1)
                if i == 2:
                    pe.wait_ge(acc_read, 1)
                bank = ps[:, LIST_BANK[i], :].rearrange("p (a r) -> p a r", a=4)
                for a in range(2):
                    ins = pe.transpose(bank[:, a, :], route[:, a].rearrange("r h k -> r (h k)"), ident)
                ins.then_inc(lists_turned, 1)

            need(pe, DRAINS["v"][-1], DRAINS["a"][-1])
            pe.wait_ge(h2_split, 3)

            def spread_row(t, tk, s, free):
                r = OUTS[t]
                pe.wait_ge(onehot_ready, tk + 1)
                if free:
                    pe.wait_ge(dotted, tk - 1)
                for n in range(2):
                    cols = slice(512 * n, 512 * n + 512)
                    out = ps[:, 2 * (s % 2) + n, :]
                    pe.matmul(out, onehot[s][0:r, :], h2hi[0:r, t, cols], start=True, stop=False)
                    ins = pe.matmul(out, onehot[s][0:r, :], h2lo[0:r, t, cols], start=False, stop=True)
                ins.then_inc(spread, 1)

            def combine(i, tk, g, s, first, last):
                pe.wait_ge(wz_ready, tk + 1)
                pe.wait_ge(uv_landed[s], 16 * (g + 1))
                for n in range(2):
                    v = uv[:, PLACE[s], D + 512 * n:D + 512 * n + 512]
                    ins = pe.matmul(ps[:, SUM_BANK[i] + n, :], wz[s][:, :], v,
                                    start=first, stop=last, skip_group_check=True)
                ins.then_inc(combined, 1)

            for i, t in enumerate(ORDER):
                groups = OUTS[t] // NS

                def group(g, first=False, last=False, turn=False, late=None):
                    tk = (GROUP0[t] + g) * NS
                    for s in range(NS):
                        if not (last and s >= NS - 2):
                            spread_row(t, tk + s + 2, (s + 2) % NS, True)
                        elif i < 2:
                            spread_row(ORDER[i + 1], tk + s + 2, (s + 2) % NS, True)
                        combine(i, tk + s, GROUP0[t] + g, s, first and s == 0, last and s == NS - 1)
                        if turn and s == 0:
                            turn_lists(i + 1)
                        if late is not None and s == 1:
                            if late:
                                pe.wait_ge(late_kept, late)
                            pair_scores(ps[:, LATE_BANK, :], B, late).then_inc(late_scored, 1)

                if i == 0:
                    for s in range(2):
                        spread_row(t, s, s, False)
                else:
                    pe.wait_ge(weights_listed, i + 1)
                if i == 0:
                    for g in range(groups):
                        group(g, first=g == 0, last=g == groups - 1, turn=g == groups - LIST_AHEAD[i], late=g)
                else:
                    group(0, first=True)
                    with pe.Fori(1, groups - max(LIST_AHEAD[i], 1)) as g:
                        group(g)
                    if LIST_AHEAD[i]:
                        group(groups - LIST_AHEAD[i], turn=True)
                    group(groups - 1, last=True)

        @block.scalar
        def _(act):
            def drains(job):
                assert DRAINS["a"][a_at[0]] == job, (job, DRAINS["a"][a_at[0]])
                a_at[0] += 1
                return take(act, job)

            a_at, junk = [0], mT[:, 0:4, 0:256]

            def copy(out, in_, job):
                release(act.activation(out, in_, ACT.Copy), job)

            def squares(t):
                act.wait_ge(x_in[t], 32 if t == C else 16)
                r = ROWS[t]
                if t:
                    act.wait_ge(ssq_done, t)
                act.activation(junk[0:r], x[0:r, t, :].rearrange("p (a b) -> p a b", a=4), ACT.Square,
                               accum_out=stat[0:r, t, 0:1]).then_inc(ssq_done, 1)

            def root(t):
                act.wait_ge(mean_done, t + 1)
                act.activation(stat[0:ROWS[t], t, 2:3], stat[0:ROWS[t], t, 1:2], ACT.Sqrt).then_inc(root_done, 1)

            squares(A)
            root(A)
            squares(B)
            root(B)
            squares(C)
            root(C)
            for t in TILES:
                r = ROWS[t]
                copy(qkv[0:r, t, 512:768], drains(f"kv{t}")[0:r, 0:256], f"kv{t}")
            for j in range(AG):
                copy(qT[:, j, :], drains(f"qc{j}")[:, 0:NT], f"qc{j}")
            for t in TILES:
                r = ROWS[t]
                bank = drains(f"q{t}")[0:r, :].rearrange("r (g j d) -> r g j d", g=AKV, j=AG)
                copy(qkv[0:r, t, 0:512].rearrange("r (j g d) -> r g j d", g=AKV, j=AG), bank, f"q{t}")
            for h in range(BH):
                copy(vbT[:, h, :], drains(f"vbT{h}")[:, 0:NT], f"vbT{h}")
            act.wait_ge(ld_abs, 1)
            act.activation(bcum[:, :, :], kt[:, :, :], ACT.Exp, scale=-1.0).then_inc(a_step, 1)
            act.wait_ge(a_step, 1)
            act.activation(bcum[:, :, :], bcum[:, :, :], ACT.Ln, bias=1.0).then_inc(ld_log, 1)
            act.wait_ge(b_ready, 1)
            act.activation(eb[:, :, :], bcum[:, :, :], ACT.Exp).then_inc(b_exp, 1)
            act.activation(kt[:, :, :], bcum[:, :, :], ACT.Exp, scale=-1.0).then_inc(b_exp, 1)
            act.wait_ge(last_ready, 3)
            act.activation(ket[:, :, :], ket[:, :, :], ACT.Exp).then_inc(ket_exp, 1)
            for t in TILES:
                r = ROWS[t]
                bank = drains(f"qT{t}").rearrange("p (j r) -> p j r", j=AG)
                copy(qT[:, :, COL[t]:COL[t] + r], bank[:, :, 0:r], f"qT{t}")
            for h in range(BH):
                bank = take(act, f"gb{h}")
                act.activation(gate[:, h, :], bank[:, 0:NO], ACT.Sigmoid).then_inc(gate_sig, 1)
            for t in TILES:
                r = ROWS[t]
                copy(vb[0:r, t, :], drains(f"vb{t}")[0:r, :], f"vb{t}")

            def probs(i, width):
                act.wait_ge(max_ready, i + 1)
                for h in range(AH):
                    act.activation(sm[:, h, 0:width], sm[:, h, 0:width], ACT.Exp, bias=soft[:, 1, h:h + 1],
                                   accum_out=soft[:, 3, h:h + 1])
                act.activation(soft[:, 4, :], soft[:, 2, :], ACT.Exp).then_inc(probs_ready, 1)

            def keep_gate(mt):
                copy(mT[:, mt, 0:NO], drains(f"ga{mt}")[:, 0:NO], f"ga{mt}")

            def turn(t):
                for i in range(4):
                    job = f"pT{'AB'[t]}.{i}"
                    bank = drains(job).rearrange("p (h c q) -> p h c q", h=2, c=2)
                    if t == A:
                        act.activation(pT[:, 2 * i:2 * i + 2, 0, :], bank[:, :, 0, :], ACT.Copy)
                        copy(pT[0:48, 2 * i:2 * i + 2, 1, :], bank[0:48, :, 1, :], job)
                    else:
                        copy(pT[:, 2 * i:2 * i + 2], bank, job)
                keep_gate(1 if t == A else 3)
                job = f"yaT{t}"
                bank = drains(job).rearrange("p (j r) -> p j r", j=AG)
                copy(yaT[:, :, COL[t]:COL[t] + P], bank, job)

            for i in range(2):
                job = f"kcT{i}"
                bank = drains(job).rearrange("p (b s) -> p b s", b=4)
                copy(kcT[:, 4 * i:4 * i + 4, :], bank, job)
            keep_gate(0)
            probs(0, 176)
            act.wait_ge(smax_ready, 1)
            for grp in range(2):
                act.activation(pss[:, grp, :], pss[:, grp, :], ACT.Exp, bias=softs[:, 1, grp:grp + 1],
                               accum_out=softs[:, 3, grp:grp + 1])
            act.activation(softs[:, 4, :], softs[:, 2, :], ACT.Exp).then_inc(sprobs_ready, 1)
            turn(A)
            probs(1, 256)
            keep_gate(2)
            turn(B)
            for t in TILES:
                job, r = f"keT{t}", ROWS[t]
                bank = drains(job).rearrange("p (c d) -> p c d", c=4)
                copy(ke[0:r, t], bank[0:r, 0:2, :], job)
            for t in TILES:
                r, bank = OUTS[t], take(act, f"o{t}")
                if t:
                    act.wait_ge(o_squared, t)
                for h in range(BH):
                    ins = act.activation(ket[0:r, h // 2, h % 2 * BV:h % 2 * BV + BV],
                                         bank[0:r, h * BV:h * BV + BV], ACT.Square, accum_out=oss[0:r, t, 0, h:h + 1])
                ins.then_inc(o_squared, 1)
                act.wait_ge(o_mean, t + 1)
                act.activation(oss[0:r, t, 2, :], oss[0:r, t, 1, :], ACT.Sqrt).then_inc(o_root, 1)
            keep_gate(4)
            for t in TILES:
                keep_gate(5 + t)
            need(act, "ga7")
            act.activation(mT[:, :, 0:NO], mT[:, :, 0:NO], ACT.Sigmoid).then_inc(first_gate_ready, 1)
            for mt in range(KT):
                job = f"gr{mt}"
                bank = drains(job)
                if mt >= 2:
                    act.wait_ge(merged, mt - 1)
                release(act.activation(sga[:, mt % 2, 0:NO], bank[:, 0:NO], ACT.Sigmoid), job)
            for i, t in enumerate(ORDER):
                act.wait_ge(x2_ready, i + 1)
                if i:
                    act.wait_ge(ssq_done, 3 + i)
                r = OUTS[t]
                act.activation(hT[0:r, 0:4, 0:256], x[0:r, t, :].rearrange("p (a b) -> p a b", a=4), ACT.Square,
                               accum_out=stat[0:r, t, 0:1]).then_inc(ssq_done, 1)
                act.wait_ge(mean_done, 3 + i + 1)
                act.activation(stat[0:r, t, 2:3], stat[0:r, t, 1:2], ACT.Sqrt).then_inc(root_done, 1)
            for n in range(2):
                copy(pqrow[:, 512 * n:512 * n + 512], drains(f"pqs{n}")[0:SAMP, :], f"pqs{n}")
            copy(qp[:, :, 256:NO], drains("pqsT").rearrange("p (h r) -> p h r", r=SAMP)[:, 0:PH], "pqsT")
            copy(sc[:, C, 0:2].rearrange("r h n -> r (h n)"), drains("pss"), "pss")
            for t in (A, B):
                for half in range(2):
                    job = f"h2T{t}.{half}"
                    bank = drains(job).rearrange("p (k r) -> p k r", k=4)
                    copy(hT[:, 4 * half:4 * half + 4, COL[t]:COL[t] + P], bank, job)
            def list_exp(i, heads):
                act.wait_ge(fv_ready, i + 1)
                act.activation(route[:, 1, 0:heads], route[:, 1, 0:heads], ACT.Exp).then_inc(w_exp, 1)

            for i in range(5):
                if i < 4:
                    for h in (2 * i, 2 * i + 1):
                        copy(qp[:, h, 0:256], drains(f"pq{h}")[:, 0:256], f"pq{h}")
                if i:
                    job = f"ps{A}.{i - 1}"
                    copy(sc[:, A, 2 * i - 2:2 * i].rearrange("r h n -> r (h n)"), drains(job), job)
                if i == 0:
                    list_exp(0, 2)

            spot = C_("spot")

            def weigh_experts(t, g, s, reuse=True):
                tk, row = (GROUP0[t] + g) * NS + s, g * NS + s
                now, back, both = held(act, tk + 1), held(act, tk - (NS - 1)), held(act, 2 * tk + 2)
                place = held(act, 127 - row)
                if reuse:
                    act.wait_ge(combined, back)
                act.activation(wz[s][:, :], spot[:, bass.ds(place, P)], ACT.Copy,
                               scale=wT[:, bass.ds(row + COL[t], 1)]).then_inc(factored, 1)
                act.wait_ge(dotted, now)
                act.activation(acts[:, s:s + 1], dots[:, s:s + 1], ACT.Gelu).then_inc(factored, 1)
                act.wait_ge(factored, both)
                act.activation(wz[s][:, :], wz[s][:, :], ACT.Copy, scale=acts[:, s:s + 1]).then_inc(wz_ready, 1)

            def final_squares(i):
                r, t = OUTS[ORDER[i]], ORDER[i]
                act.wait_ge(acc_read, i + 1)
                act.activation(hT[0:r, 0:4, 0:256], x[0:r, t, :].rearrange("p (a b) -> p a b", a=4), ACT.Square,
                               accum_out=stat[0:r, t, 0:1]).then_inc(fin_ssq, 1)

            def final_root(i):
                r, t = OUTS[ORDER[i]], ORDER[i]
                act.wait_ge(fin_mean, i + 1)
                act.activation(stat[0:r, t, 2:3], stat[0:r, t, 1:2], ACT.Sqrt).then_inc(fin_root, 1)

            for i, t in enumerate(ORDER):
                groups = OUTS[t] // NS
                act.wait_ge(weights_listed, i + 1)
                ahead = groups - LIST_AHEAD[i]
                if i == 0:
                    for g in range(groups):
                        if g == ahead:
                            list_exp(1, PH)
                        for s in range(NS):
                            weigh_experts(t, g, s, reuse=g > 0)
                            if s == NS // 2:
                                act.wait_ge(late_scored, g + 1)
                                act.activation(sc[:, B, 2 * g:2 * g + 2].rearrange("r h n -> r (h n)"),
                                               ps[:, LATE_BANK, :], ACT.Copy).then_inc(late_kept, 1)
                else:
                    for s in range(NS):
                        weigh_experts(t, 0, s)
                        if s == 1:
                            final_squares(i - 1)
                        if s == 2:
                            final_root(i - 1)
                    with act.Fori(1, ahead) as g:
                        for s in range(NS):
                            weigh_experts(t, g, s)
                    if i == 1:
                        list_exp(2, PH)
                        with act.Fori(ahead, groups) as g:
                            for s in range(NS):
                                weigh_experts(t, g, s)
            final_squares(2)
            final_root(2)

        @block.vector
        def _(dve):
            links, v_at = [0], [0]

            def link(ins):
                links[0] += 1
                ins.then_inc(v_step, 1)
                dve.wait_ge(v_step, links[0])

            def drains(job):
                assert DRAINS["v"][v_at[0]] == job, (job, DRAINS["v"][v_at[0]])
                v_at[0] += 1
                return take(dve, job)

            def mean(t, r, ssq, done):
                ins = dve.tensor_scalar(stat[0:r, t, 1:2], stat[0:r, t, 0:1], 1.0 / D, EPS, ALU.mult, ALU.add)
                ins.then_inc(done, 1)

            bank = drains("gvecT")
            release(dve.tensor_copy(gT[:, :], bank[:, 0:19]), "gvecT")
            need(dve, "gvecT")
            for t in TILES:
                r = ROWS[t]
                dve.wait_ge(ssq_done, t + 1)
                mean(t, r, ssq_done, mean_done)
                dve.wait_ge(root_done, t + 1)
                link(dve.reciprocal(stat[0:r, t, 3:4], stat[0:r, t, 2:3]))
                dve.tensor_scalar(hrow[0:r, t, :], x[0:r, t, :], stat[0:r, t, 3:4], None, ALU.mult
                                  ).then_inc(rows_normed, 1)
                for half in range(2):
                    job = f"hT{t}.{half}"
                    bank = drains(job).rearrange("p (k r) -> p k r", k=4)
                    gain = gT[:, 4 * half:4 * half + 4].unsqueeze(2).broadcast_to([P, 4, r])
                    release(dve.tensor_tensor(hT[:, 4 * half:4 * half + 4, COL[t]:COL[t] + r], bank[:, :, 0:r], gain,
                                              ALU.mult), job)
            dve.wait_ge(cst_landed, 16)
            dve.wait_ge(small_landed, 16 * N_SMALL_IN)

            def rope(t):
                r = ROWS[t]
                need(dve, f"q{t}", f"kv{t}")
                if t:
                    dve.wait_ge(roped, t)
                heads = qkv[0:r, t, 0:640].rearrange("r (h d) -> r h d", d=AD)
                half = ROPE // 2
                cos = C_("cos")[0:r, t * ROPE:t * ROPE + ROPE].unsqueeze(1).broadcast_to([r, 10, ROPE])
                sin = C_("sin")[0:r, t * half:t * half + half].unsqueeze(1).broadcast_to([r, 10, half])
                dve.tensor_tensor(ropet[0:r, :, 0:ROPE], heads[:, :, 0:ROPE], cos, ALU.mult)
                dve.tensor_tensor(ropet[0:r, :, ROPE:ROPE + half], heads[:, :, half:ROPE], sin, ALU.mult)
                link(dve.tensor_tensor(ropet[0:r, :, ROPE + half:2 * ROPE], heads[:, :, 0:half], sin, ALU.mult))
                dve.tensor_tensor(heads[:, :, 0:half], ropet[0:r, :, 0:half], ropet[0:r, :, ROPE:ROPE + half],
                                  ALU.subtract)
                dve.tensor_tensor(heads[:, :, half:ROPE], ropet[0:r, :, half:ROPE],
                                  ropet[0:r, :, ROPE + half:2 * ROPE], ALU.add).then_inc(roped, 1)

            bank = drains("lrT")
            release(dve.tensor_copy(lrT[:, :], bank[0:RANK, 0:NT]), "lrT")
            for t in TILES:
                rope(t)
            for p in range(2):
                bank = drains(f"ld{p}")
                release(dve.tensor_scalar(eb[:, p, :], bank[:, 0:NT], gT[:, 16 + p:17 + p], None, ALU.add), f"ld{p}")
            need(dve, "ld1")
            dve.scalar_tensor_tensor(out=kt[:, :, :], in0=eb[:, :, :], scalar=-1.0, in1=eb[:, :, :], op0=ALU.mult,
                                     op1=ALU.max).then_inc(ld_abs, 1)
            link(dve.tensor_scalar(ket[:, :, :], eb[:, :, :], 0.0, 1.0 / 16, ALU.min, ALU.mult))
            dve.wait_ge(ld_log, 1)
            link(dve.scalar_tensor_tensor(out=ket[:, :, :], in0=bcum[:, :, :], scalar=-1.0 / 16, in1=ket[:, :, :],
                                          op0=ALU.mult, op1=ALU.add))
            for p in range(2):
                ins = dve.tensor_tensor_scan(bcum[:, p, :], C_("reset"), ket[:, p, :], 0.0, ALU.mult, ALU.add)
            ins.then_inc(b_ready, 1)
            dve.wait_ge(b_ready, 1)
            for c0, n, w in ((0, 4, CHUNK), (256, DEC_B, DEC_T), (288, 1, META)):
                b = bcum[:, :, c0:c0 + n * w].rearrange("p a (n w) -> p a n w", w=w)
                out = ket[:, :, c0:c0 + n * w].rearrange("p a (n w) -> p a n w", w=w)
                dve.tensor_tensor(out, b[:, :, :, w - 1:w].broadcast_to([P, 2, n, w]), b, ALU.subtract
                                  ).then_inc(last_ready, 1)

            dve.wait_ge(zeroed, 7)
            for t in TILES:
                job, r = f"kT{t}", ROWS[t]
                bank = drains(job)
                if t == C:
                    dve.tensor_copy(kTs[:, :], bank[:, 0:SAMP])
                dve.tensor_copy(kz[0:AD, 0, COL[t]:COL[t] + r], bank[0:AD, 0:r])
                release(dve.tensor_copy(kz[AD:P, 1, COL[t]:COL[t] + r], bank[AD:P, 0:r]), job)
            for h in range(BH):
                job = f"gb{h}"
                bank = drains(job)
                dve.wait_ge(gate_sig, h + 1)
                release(dve.scalar_tensor_tensor(out=gate[:, h, :], in0=bank[:, 0:NO], scalar=gT[:, 18:19],
                                                 in1=gate[:, h, :], op0=ALU.mult, op1=ALU.mult), job)
            dve.wait_ge(b_exp, 2)
            dve.wait_ge(ket_exp, 1)
            for p in range(2):
                job = f"kb{p}"
                bank = drains(job)
                dve.tensor_tensor(kt[:, p, :], bank[:, 0:NT], kt[:, p, :], ALU.mult)
                release(dve.tensor_tensor(ket[:, p, :], bank[:, 0:NT], ket[:, p, :], ALU.mult), job)
            for p in range(2):
                job = f"qb{p}"
                bank = drains(job)
                for hh in range(2):
                    lanes = slice(hh * BK, hh * BK + BK)
                    ins = dve.scalar_tensor_tensor(out=qh[lanes, 2 * p + hh, :], in0=bank[lanes, 0:NT],
                                                   scalar=BK ** -0.5, in1=eb[lanes, p, :], op0=ALU.mult, op1=ALU.mult)
                release(ins, job)

            def row_max(t):
                width, mask = (176, C_("mask_a")) if t == A else (256, C_("mask_b"))
                for j in range(AG):
                    job = f"sc{'AB'[t]}.{j}"
                    bank = drains(job).rearrange("p (g k) -> p g k", g=2)
                    out = sm[:, :, :].rearrange("p (g j) k -> p j g k", g=2)[:, j, :, 0:width]
                    release(dve.scalar_tensor_tensor(out=out, in0=bank[:, :, 0:width], scalar=AD ** -0.5,
                                                     in1=mask.unsqueeze(1).broadcast_to([P, 2, width]),
                                                     op0=ALU.mult, op1=ALU.add), job)
                need(dve, job)
                link(dve.tensor_reduce(soft[:, 0, :], sm[:, :, 0:width], AX_X, ALU.max))
                link(dve.tensor_tensor(soft[:, 0, :], soft[:, 0, :], sinkb[:, :], ALU.max))
                dve.tensor_scalar(soft[:, 1, :], soft[:, 0, :], -1.0, None, ALU.mult)
                dve.tensor_tensor(soft[:, 2, :], sinkb[:, :], soft[:, 0, :], ALU.subtract).then_inc(max_ready, 1)

            def weigh(t):
                dve.wait_ge(probs_ready, t + 1)
                link(dve.tensor_tensor(soft[:, 5, :], soft[:, 3, :], soft[:, 4, :], ALU.add))
                link(dve.reciprocal(soft[:, 5, :], soft[:, 5, :]))
                job = f"pv{'AB'[t]}"
                bank = drains(job).rearrange("p (g j d) -> p g j d", g=AKV, j=AG)
                share = soft[:, 5, :].rearrange("p (g j) -> p g j", g=AKV).unsqueeze(3).broadcast_to([P, AKV, AG, AD])
                release(dve.tensor_tensor(ya[:, :].rearrange("p (j g d) -> p g j d", g=AKV, j=AG), bank, share,
                                          ALU.mult), job)

            row_max(A)
            need(dve, "qT2")
            for g in range(AKV):
                lanes = slice(g * AD, g * AD + AD)
                for grp in range(2):
                    out = qs[lanes, grp, :].rearrange("p (b h t) -> p h b t", b=4, h=AH)[:, 4 * g:4 * g + 4]
                    src = qT[lanes, :, 256 + 16 * grp:272 + 16 * grp].rearrange("p j (b t) -> p j b t", t=DEC_T)
                    ins = dve.tensor_copy(out, src)
            link(ins)
            for b in range(DEC_B):
                c0 = (b % 4) * 32
                ins = dve.tensor_copy(qzs[:, b, c0:c0 + 32], qs[:, b // 4, c0:c0 + 32])
            ins.then_inc(qs_ready, 1)
            dve.tensor_tensor(sinkt[:, :], sinkb[:, :], C_("hsel"), ALU.mult).then_inc(v_step, 1)
            links[0] += 1
            dve.wait_ge(v_step, links[0])
            link(dve.tensor_reduce(sinkr[:, :], sinkt[:, :], AX_X, ALU.add))
            for grp in range(2):
                job = f"ss{grp}"
                bank = drains(job)
                release(dve.scalar_tensor_tensor(out=pss[:, grp, :], in0=bank[:, 0:160], scalar=AD ** -0.5,
                                                 in1=C_("mask_s")[:, grp * 160:grp * 160 + 160], op0=ALU.mult,
                                                 op1=ALU.add), job)
            need(dve, "ss1")
            link(dve.tensor_reduce(softs[:, 0, :], pss[:, :, :], AX_X, ALU.max))
            link(dve.tensor_scalar(softs[:, 0, :], softs[:, 0, :], sinkr[:, 0:1], None, ALU.max))
            dve.tensor_scalar(softs[:, 1, :], softs[:, 0, :], -1.0, None, ALU.mult)
            dve.tensor_scalar(softs[:, 2, :], softs[:, 0, :], -1.0, sinkr[:, 0:1], ALU.mult, ALU.add
                              ).then_inc(smax_ready, 1)
            weigh(A)
            row_max(B)
            dve.wait_ge(sprobs_ready, 1)
            link(dve.tensor_tensor(softs[:, 5, :], softs[:, 3, :], softs[:, 4, :], ALU.add))
            link(dve.reciprocal(softs[:, 5, :], softs[:, 5, :]))
            for grp in range(2):
                job = f"spT{grp}"
                bank = drains(job)
                for b in range(4):
                    c0 = b * 32
                    dve.tensor_copy(pz[:, grp, b * P + c0:b * P + c0 + 32], bank[:, c0:c0 + 32])
                release(dve.tensor_copy(pnT[:, grp, :], bank[0:SAMP, P:2 * P]), job)
            for grp in range(2):
                job = f"spv{grp}"
                bank = drains(job)
                release(dve.tensor_scalar(so[:, grp, :], bank[:, 0:P], softs[:, 5, grp:grp + 1], None, ALU.mult), job)
            for grp in range(2):
                job = f"soT{grp}"
                bank = drains(job)
                for g in range(AKV):
                    lanes = slice(g * AD, g * AD + AD)
                    c0 = 256 + grp * 16
                    out = yaT[lanes, :, c0:c0 + 16].rearrange("p j (b t) -> p j b t", t=DEC_T)
                    src = bank[lanes, 0:P].rearrange("p (b h t) -> p h b t", b=4, h=AH)[:, 4 * g:4 * g + 4]
                    ins = dve.tensor_copy(out, src)
                release(ins, job)
            weigh(B)

            for t in TILES:
                job, r = f"AT{t}", OUTS[t]
                bank = drains(job)[0:r, 0:BH * r].rearrange("p (h i) -> p h i", h=BH)
                out = ats[:, :, :] if t == C else atm[:, t]
                mask = (C_("gla_s") if t == C else C_("gla"))[0:r].bitcast(U32)
                release(dve.copy_predicated(out, mask.unsqueeze(1).broadcast_to([r, BH, r]), bank), job)
            last = [288 + META - 1, CHUNK - 1, 2 * CHUNK - 1, 3 * CHUNK - 1, 4 * CHUNK - 1]
            for n in range(5):
                job = f"up{n}"
                bank = drains(job)
                if n:
                    dve.wait_ge(states_ready, 4 * n)
                for p in range(2):
                    for hh in range(2):
                        lanes = slice(hh * BK, hh * BK + BK)
                        src = bank[lanes, p * 256 + hh * BV:p * 256 + hh * BV + BV]
                        if n == 0:
                            ins = dve.tensor_copy(st[lanes, 0, p, :], src)
                        else:
                            ins = dve.scalar_tensor_tensor(out=st[lanes, n, p, :], in0=st[lanes, n - 1, p, :],
                                                           scalar=eb[lanes, p, last[n]:last[n] + 1], in1=src,
                                                           op0=ALU.mult, op1=ALU.add)
                        if not (p and hh):
                            ins.then_inc(states_ready, 1)
                dve.wait_ge(states_ready, 4 * n + 3)
                release(ins, job)
                need(dve, job)
                dve.engine_nop().then_inc(states_ready, 1)
            for h in range(BH):
                src = qh[:, h, 256:288].unsqueeze(1).broadcast_to([P, DEC_B, SAMP])
                ins = dve.tensor_tensor(qsz[:, h], src, C_("batch").rearrange("p (b i) -> p b i", b=DEC_B), ALU.mult)
            ins.then_inc(qsz_ready, 1)
            for t in TILES:
                job, r = f"o{t}", OUTS[t]
                bank = drains(job)
                dve.wait_ge(o_squared, t + 1)
                dve.tensor_scalar(oss[0:r, t, 1, :], oss[0:r, t, 0, :], 1.0 / BV, EPS, ALU.mult, ALU.add
                                  ).then_inc(o_mean, 1)
                dve.wait_ge(o_root, t + 1)
                link(dve.reciprocal(oss[0:r, t, 3, :], oss[0:r, t, 2, :]))
                rows = yb[0:r, t, :].rearrange("r (h e) -> r h e", h=BH)
                release(dve.tensor_tensor(rows, bank[0:r, :].rearrange("r (h e) -> r h e", h=BH),
                                          oss[0:r, t, 3, :].unsqueeze(2).broadcast_to([r, BH, BV]), ALU.mult), job)
            for t in TILES:
                job, cols = f"ybT{t}", slice(COL[t], COL[t] + OUTS[t])
                bank = drains(job).rearrange("p (j r) -> p j r", j=BH)
                release(dve.tensor_tensor(ybT[:, :, cols], bank[:, :, 0:OUTS[t]], gate[:, :, cols], ALU.mult), job)
            for p in range(2):
                decay = eb[:, p, 256:288].rearrange("p (b t) -> p b t", t=DEC_T)[:, :, DEC_T - 1:DEC_T]
                ins = dve.tensor_tensor(s0[:, p], s0[:, p], decay.broadcast_to([P, DEC_B, BV]), ALU.mult)
            link(ins)
            for mt in range(KT):
                if mt < BH:
                    src = vb[0:SAMP, C, mt * BV:mt * BV + BV].unsqueeze(1).broadcast_to([SAMP, DEC_B, BV])
                    dve.tensor_tensor(vblk[:, :, :], src,
                                      C_("batch_rows")[0:SAMP].unsqueeze(2).broadcast_to([SAMP, DEC_B, BV]), ALU.mult
                                      ).then_inc(vblk_ready, 1)
                if mt == 0:
                    dve.wait_ge(first_gate_ready, 1)
                job = f"za{mt}"
                bank = drains(job)
                release(dve.tensor_tensor(mT[:, mt, 0:NO], bank[:, 0:NO], mT[:, mt, 0:NO], ALU.mult), job)
                need(dve, f"gr{mt}")
                job, gated = f"zb{mt}", sga[:, mt % 2, 0:NO]
                bank = drains(job)
                release(dve.tensor_tensor(gated, bank[:, 0:NO], gated, ALU.mult), job)
                need(dve, job)
                dve.tensor_tensor(mT[:, mt, 0:NO], mT[:, mt, 0:NO], gated, ALU.add).then_inc(merged, 1)
                if mt < BH:
                    lanes = slice((mt % 2) * BK, (mt % 2) * BK + BK)
                    for i in range(2):
                        job = f"us{mt}.{i}"
                        bank = drains(job).rearrange("p (b e) -> p b e", b=4)
                        part = s0[lanes, mt // 2, 4 * i:4 * i + 4, :]
                        release(dve.tensor_tensor(part, part, bank[lanes], ALU.add), job)

            def norm_rows(i, t):
                r = OUTS[t]
                dve.wait_ge(ssq_done, 3 + i + 1)
                mean(t, r, ssq_done, mean_done)
                dve.wait_ge(root_done, 3 + i + 1)
                link(dve.reciprocal(stat[0:r, t, 3:4], stat[0:r, t, 2:3]))
                if i == 0:
                    dve.wait_ge(mixer_out, 16 * N_MIX_OUT)
                dve.scalar_tensor_tensor(out=h2hold[t][0:r, :], in0=x[0:r, t, :], scalar=stat[0:r, t, 3:4],
                                         in1=gffn[0:r, :], op0=ALU.mult, op1=ALU.mult).then_inc(rows_normed, 1)

            for i, t in enumerate(ORDER):
                r = OUTS[t]
                for n in range(2):
                    job = f"wo{n}.{t}"
                    bank = drains(job)
                    part = x[0:r, t, 512 * n:512 * n + 512]
                    release(dve.tensor_tensor(part, part, bank[0:r, :], ALU.add), job)
                need(dve, job)
                dve.engine_nop().then_inc(x2_ready, 1)
                if i < 2:
                    norm_rows(i, t)
            for half in range(2):
                job = f"h2T{C}.{half}"
                bank = drains(job).rearrange("p (k r) -> p k r", k=4)
                release(dve.tensor_copy(hT[:, 4 * half:4 * half + 4, 256:NO], bank[:, :, 0:SAMP]), job)
            dve.wait_ge(zeroed, 8)
            for i in range(2):
                job = f"kk{i}"
                bank = drains(job).rearrange("p (h n) -> p h n", h=4)
                dve.tensor_copy(kbd[0:64, 4 * i:4 * i + 4, 0:PK], bank[0:64])
                ins = dve.tensor_copy(kbd[64:P, 4 * i:4 * i + 4, PK:2 * PK], bank[64:P])
                release(ins, job)
            need(dve, "kk1")
            dve.engine_nop().then_inc(kbd_ready, 1)
            norm_rows(2, B)

            def mark(ins):
                links[0] += 1
                ins.then_inc(v_step, 1)
                return links[0]

            def since(n):
                if n:
                    dve.wait_ge(v_step, n)

            def top16_round(n, values, spare, out, index):
                if n == 0:
                    return dve.max(out[:, 0:8], values)
                if n == 1:
                    return dve.max_index(index[:, 0:8], out[:, 0:8], values)
                if n == 2:
                    return dve.match_replace(spare, out[:, 0:8], values, FLOOR)
                if n == 3:
                    return dve.max(out[:, 8:16], spare)
                return dve.max_index(index[:, 8:16], out[:, 8:16], spare)

            def best_keys(t, heads, rounds):
                for n in rounds:
                    for h in heads:
                        for c in range(2):
                            since(half_done[h % 2][c])
                            half_done[h % 2][c] = mark(top16_round(
                                n, sc[:, t, h, c * PK:c * PK + PK], less[:, h % 2, c, :], sv[:, h % 2, c, :],
                                si[:, h % 2, c, :]))

            def best_sums(h, n):
                w = h % 2
                since(sum_done[w])
                if n == 0:
                    a = sv[:, w, 0, :].unsqueeze(2).broadcast_to([P, TOPK, TOPK])
                    b = sv[:, w, 1, :].unsqueeze(1).broadcast_to([P, TOPK, TOPK])
                    ins = dve.tensor_tensor(cand[:, w, :].rearrange("r (i j) -> r i j", i=TOPK), a, b, ALU.add)
                else:
                    ins = top16_round(n - 1, cand[:, w, :], cand2[:, w, :], fv[:, h, :], fpos[:, w, :])
                sum_done[w] = mark(ins)

            def numbers(h, n):
                since(number_done[0])
                w = h % 2
                grid = pick[:, :, :, :].rearrange("r c k i -> r (c k) i")
                if n == 0:
                    mark(dve.tensor_single_scalar(fij[:, 0, :], fpos[:, w, :], 4, ALU.logical_shift_right))
                    mark(dve.tensor_single_scalar(fij[:, 1, :], fpos[:, w, :], TOPK - 1, ALU.bitwise_and))
                    ins = dve.tensor_copy(sif[:, :, :], si[:, w])
                elif n == 1:
                    ins = dve.tensor_copy(fijf[:, :, :], fij[:, :, :])
                elif n == 2:
                    want = fijf[:, :, :].rearrange("r c k -> r (c k)").unsqueeze(2).broadcast_to([P, 2 * TOPK, TOPK])
                    have = C_("iota").unsqueeze(1).broadcast_to([P, 2 * TOPK, TOPK])
                    ins = dve.tensor_tensor(grid, want, have, ALU.is_equal)
                elif n == 3:
                    number = sif[:, :, :].unsqueeze(2).broadcast_to([P, 2, TOPK, TOPK])
                    ins = dve.tensor_tensor(pick[:, :, :, :], pick[:, :, :, :], number, ALU.mult)
                elif n == 4:
                    ins = dve.tensor_reduce(eij[:, :, :].rearrange("r c k -> r (c k)"), grid, AX_X, ALU.add)
                else:
                    ins = dve.scalar_tensor_tensor(out=route[:, 0, h, :], in0=eij[:, 0, :], scalar=float(PK),
                                                   in1=eij[:, 1, :], op0=ALU.mult, op1=ALU.add)
                number_done[0] = mark(ins)

            half_done, sum_done, number_done = [[0, 0], [0, 0]], [0, 0], [0]

            def route_step(t, h, step):
                since(links[0])
                if step < 2:
                    best_keys(t, [h], (range(3), range(3, 5))[step])
                else:
                    for n in (range(3), range(3, 6))[step - 2]:
                        if h < PH:
                            best_sums(h, n)
                        if h:
                            numbers(h - 1, n)

            def weights_begin(heads):
                w = route[:, 1, 0:heads]
                dve.tensor_tensor(w, fv[:, 0:heads], fv[:, 0:heads, 0:1].broadcast_to([P, heads, TOPK]), ALU.subtract
                                  ).then_inc(fv_ready, 1)

            def weights_end(i, heads):
                w, total = route[:, 1, 0:heads], wsum[:, :, 0:heads]
                dve.wait_ge(w_exp, i + 1)
                link(dve.tensor_reduce(total[:, 0], w, AX_X, ALU.add))
                link(dve.reciprocal(total[:, 1], total[:, 0]))
                dve.tensor_tensor(w, w, total[:, 1].unsqueeze(2).broadcast_to([P, heads, TOPK]), ALU.mult
                                  ).then_inc(routed, 1)

            def take_list(i, t):
                dve.wait_ge(lists_turned, i)
                bank = ps[:, LIST_BANK[i], :].rearrange("p (a r) -> p a r", a=4)
                dve.tensor_copy(idxT[:, COL[t]:COL[t] + P], bank[:, 0, :]).then_inc(listed, 1)
                dve.tensor_copy(wT[:, COL[t]:COL[t] + P], bank[:, 1, :]).then_inc(weights_listed, 1)

            need(dve, "pss")
            best_keys(C, (0, 1), range(5))
            since(links[0])
            for n in range(6):
                for h in range(2):
                    best_sums(h, n)
            since(links[0])
            weights_begin(2)
            for h in range(2):
                for n in range(6):
                    numbers(h, n)
            since(links[0])
            weights_end(0, 2)
            dve.wait_ge(routed, 1)
            link(dve.transpose(turned_s[:, :], route[:, 0, 0:2].rearrange("r h k -> r (h k)")))
            dve.tensor_copy(idxT[:, 256:NO], turned_s[:, :]).then_inc(listed, 1)
            dve.transpose(wT[:, 256:NO], route[:, 1, 0:2].rearrange("r h k -> r (h k)")).then_inc(weights_listed, 1)

            def dot(t, g, s):
                now, landed = held(dve, (GROUP0[t] + g) * NS + (s + 1)), held(dve, 16 * (GROUP0[t] + g + 1))
                dve.wait_ge(spread, now)
                dve.wait_ge(uv_landed[s], landed)
                row_on_all = ps[:, 2 * (s % 2):2 * (s % 2) + 2, :]
                u = uv[:, PLACE[s], 0:D].rearrange("p (a b) -> p a b", a=2)
                dve.tensor_tensor_reduce(u, row_on_all, u, 1.0, 0.0, ALU.mult, ALU.add, dots[:, s:s + 1]
                                         ).then_inc(dotted, 1)

            def add_sums(i):
                t, r, bank = ORDER[i], OUTS[ORDER[i]], SUM_BANK[i]
                dve.wait_ge(combined, (GROUP0[t] + r // NS) * NS)
                rows = x[0:r, t, :].rearrange("p (a b) -> p a b", a=2)
                dve.tensor_tensor(rows, rows, ps[0:r, bank:bank + 2, :], ALU.add).then_inc(acc_read, 1)

            def final_mean(i):
                dve.wait_ge(fin_ssq, i + 1)
                mean(ORDER[i], OUTS[ORDER[i]], fin_ssq, fin_mean)

            def final_rows(i):
                t, r = ORDER[i], OUTS[ORDER[i]]
                dve.wait_ge(fin_root, i + 1)
                link(dve.reciprocal(stat[0:r, t, 3:4], stat[0:r, t, 2:3]))
                dve.wait_ge(router_landed, 16 * 2)
                if i == 2:
                    dve.wait_ge(y_out[0], 16)
                dve.scalar_tensor_tensor(out=h2[0:r, i % 2, :], in0=x[0:r, t, :], scalar=stat[0:r, t, 3:4],
                                         in1=gfin[0:r, :], op0=ALU.mult, op1=ALU.mult).then_inc(y_ready, 1)

            for i, t in enumerate(ORDER):
                groups = OUTS[t] // NS
                if i < 2:
                    after = ORDER[i + 1]
                    steps = [(h, step) for h in range(PH) for step in range(4)] + [(PH, 2), (PH, 3)]
                    if i == 0:
                        need(dve, f"ps{A}.0")
                        for h, step in steps[:8]:
                            route_step(after, h, step)
                        del steps[:8]
                    if after == A:
                        need(dve, f"ps{A}.3")
                    else:
                        dve.wait_ge(late_kept, PH // 2)
                groups_before = groups - LIST_AHEAD[i] if i < 2 else 1
                given = 0
                for g in range(groups_before):
                    for s in range(NS):
                        dot(t, g, s)
                        if i and g == 0 and 1 <= s <= 3:
                            (add_sums, final_mean, final_rows)[s - 1](i - 1)
                        if i < 2:
                            due = -(-(g * NS + s + 1) * len(steps) // (groups_before * NS))
                            for h, step in steps[given:due]:
                                route_step(after, h, step)
                            given = due
                if i < 2:
                    since(links[0])
                    weights_begin(PH)
                    dot(t, groups_before, 0)
                    weights_end(i + 1, PH)
                    dot(t, groups_before, 1)
                    take_list(i + 1, after)
                    for s in range(2, NS):
                        dot(t, groups_before, s)
                    groups_before += 1
                if groups_before < groups:
                    with dve.Fori(groups_before, groups) as g:
                        for s in range(NS):
                            dot(t, g, s)
            add_sums(2)
            final_mean(2)
            final_rows(2)


_INS = ["x_prompt", "x_sample", "cache_k_window", "cache_v_window", "state_gla", "meta_tokens", "g_norm_mix", "w_in",
        "w_gate_up", "b_gate", "attn_sinks", "g_gla_norm", "w_branch_a", "w_branch_b", "w_out", "g_norm_ffn",
        "w_peer_q", "peer_sub_keys", "peer_uv", "g_norm_final"]
_OUTS = [(1, SEQ, D), (DEC_B, DEC_T, D), (1, 1, WINDOW, AKV, AD), (1, 1, WINDOW, AKV, AD), (1, 1, BH, BK, BV),
         (1, DEC_B, WINDOW, AKV, AD), (1, DEC_B, WINDOW, AKV, AD), (1, DEC_B, BH, BK, BV)]


def kernel(**inputs):
    import concourse.bacc as bacc
    from concourse.bass_utils import run_bass_kernel_spmd

    nc = bacc.Bacc("TRN2", target_bir_lowering=False, num_devices=1)
    arrays, args = {}, []
    inputs["peer_uv"] = np.concatenate([inputs["peer_u"][0], inputs["peer_v"][0]], 1)
    for name in _INS:
        a = np.ascontiguousarray(inputs[name])
        arrays[f"in_{name}"] = a
        args.append(nc.dram_tensor(f"in_{name}", a.shape, mybir.dt.from_np(a.dtype), kind="ExternalInput").ap())
    arrays["shape_constants"] = shape_constants()
    args.append(nc.dram_tensor("shape_constants", (P, CST_COLS), F32, kind="ExternalInput").ap())
    for i, shape in enumerate(_OUTS):
        args.append(nc.dram_tensor(f"out_{i}", shape, F32, kind="ExternalOutput").ap())
    hybrid_step(nc, *args)
    r = run_bass_kernel_spmd(nc, [arrays], core_ids=[0])
    return tuple(r.results[0][f"out_{i}"] for i in range(len(_OUTS)))
```
